# Optimizing a Trainium2 kernel written in Bass

```python
import jax, jax.numpy as jnp
from jax import lax
import numpy as np

D_MODEL = 1024
BATCH = 1
SEQ = 2048
DEPTH = 1

ATTN_HEADS = 8
HEAD_DIM = 64
ATTN_WIDTH = ATTN_HEADS * HEAD_DIM
DILATED_PATTERNS = ((128, 1), (512, 4), (2048, 16))
POOL_WINDOWS = (2, 4, 8, 16)
POOL_GROUPS = len(POOL_WINDOWS)
POOL_WIDTH = D_MODEL // 2
POOL_GROUP_DIM = POOL_WIDTH // POOL_GROUPS
MIX_WIDTH = ATTN_WIDTH + POOL_WIDTH
IN_WIDTH = 3 * ATTN_WIDTH + POOL_WIDTH
MEM_LEN = 256
MEM_HEADS = 4
MEM_HEAD_DIM = 128
MEM_WIDTH = MEM_HEADS * MEM_HEAD_DIM
N_EXPERTS = 64
N_EXPERT_GROUPS = 8
TOPK_GROUPS = 4
TOP_K = 8
EXPERT_HIDDEN = 256
SHARED_HIDDEN = 256
ROUTED_SCALE = 2.5
MOE_BLOCK = 128
LN_EPS = 1e-5
NEG_INF = -1e30

kernel_name = 'hybrid_dilated_pool_moe_block'

def layer_norm(x, g, b):
    xf = x.astype(jnp.float32)
    mu = xf.mean(-1, keepdims=True)
    var = jnp.square(xf - mu).mean(-1, keepdims=True)
    y = (xf - mu) * lax.rsqrt(var + LN_EPS) * g.astype(jnp.float32) + b.astype(jnp.float32)
    return y.astype(x.dtype)

def alibi_slopes(n_heads):
    return 2.0 ** (-8.0 * jnp.arange(1, n_heads + 1, dtype=jnp.float32) / n_heads)

def _to_strided_blocks(a, dil, blk):
    B, T, H, hd = a.shape
    L = T // dil
    Lp = -(-L // blk) * blk
    a = a.reshape(B, L, dil, H, hd).transpose(0, 3, 2, 1, 4)
    a = jnp.pad(a, ((0, 0), (0, 0), (0, 0), (0, Lp - L), (0, 0)))
    return a.reshape(B, H, dil, Lp // blk, blk, hd)

def dilated_branch(q, k, v, slopes, window, dil):
    B, T, H, hd = q.shape
    steps = window // dil
    blk = steps
    L = T // dil
    qb, kb, vb = (_to_strided_blocks(a, dil, blk) for a in (q, k, v))
    nb = qb.shape[3]

    def with_prev(a):
        prev = jnp.pad(a[:, :, :, :-1], ((0, 0), (0, 0), (0, 0), (1, 0), (0, 0), (0, 0)))
        return jnp.concatenate([prev, a], axis=4)

    kk, vv = with_prev(kb), with_prev(vb)
    dist = jnp.arange(blk)[:, None] + blk - jnp.arange(2 * blk)[None, :]
    first = (jnp.arange(nb) == 0)[:, None, None] & (jnp.arange(2 * blk) < blk)[None, None, :]
    valid = (dist >= 0)[None] & (dist <= steps)[None] & ~first
    s = jnp.einsum('bhrnqd,bhrnkd->bhrnqk', qb, kk, preferred_element_type=jnp.float32) * (hd ** -0.5)
    s = s - slopes[None, :, None, None, None, None] * (dist * dil).astype(jnp.float32)
    s = jnp.where(valid, s, NEG_INF)
    lse = jax.nn.logsumexp(s, axis=-1)
    p = jnp.exp(s - lse[..., None])
    o = jnp.einsum('bhrnqk,bhrnkd->bhrnqd', p.astype(v.dtype), vv, preferred_element_type=jnp.float32)
    o = o.reshape(B, H, dil, nb * blk, hd)[:, :, :, :L].transpose(0, 3, 2, 1, 4).reshape(B, T, H, hd)
    lse = lse.reshape(B, H, dil, nb * blk)[:, :, :, :L].transpose(0, 3, 2, 1).reshape(B, T, H)
    return o, lse

def dilated_attention(q, k, v):
    slopes = alibi_slopes(q.shape[2])
    outs, lses = [], []
    for window, dil in DILATED_PATTERNS:
        o, lse = dilated_branch(q, k, v, slopes, window, dil)
        outs.append(o)
        lses.append(lse)
    wts = jax.nn.softmax(jnp.stack(lses), axis=0)
    return jnp.einsum('gbth,gbthd->bthd', wts, jnp.stack(outs))

def multiscale_pool(p, pool_w, pool_scale):
    B, T, _ = p.shape
    grp = p.astype(jnp.float32).reshape(B, T, POOL_GROUPS, POOL_GROUP_DIM)
    cs0 = jnp.pad(jnp.cumsum(grp, axis=1), ((0, 0), (1, 0), (0, 0), (0, 0)))
    pos = jnp.arange(T, dtype=jnp.float32)
    outs = []
    for g, w in enumerate(POOL_WINDOWS):
        upper = cs0[:, 1:, g]
        lower = jnp.pad(cs0[:, :T + 1 - w, g], ((0, 0), (w - 1, 0), (0, 0)))
        count = jnp.minimum(pos + 1.0, float(w))[None, :, None]
        outs.append((upper - lower) / count - grp[:, :, g])
    pooled = jnp.stack(outs, axis=2)
    mixed = jnp.einsum('btgc,gcd->btgd', pooled, pool_w.astype(jnp.float32))
    return (mixed.reshape(B, T, POOL_WIDTH) * pool_scale.astype(jnp.float32)).astype(p.dtype)

def hybrid_mixer(h, w_in, pool_w, pool_scale, w_out):
    B, T, _ = h.shape
    proj = h @ w_in
    q, k, v, p = jnp.split(proj, [ATTN_WIDTH, 2 * ATTN_WIDTH, 3 * ATTN_WIDTH], axis=-1)
    heads = lambda a: a.reshape(B, T, ATTN_HEADS, HEAD_DIM)
    attn = dilated_attention(heads(q), heads(k), heads(v)).reshape(B, T, ATTN_WIDTH).astype(h.dtype)
    pool = multiscale_pool(p, pool_w, pool_scale)
    return jnp.concatenate([attn, pool], axis=-1) @ w_out

def memory_cross_attention(h, mem, w_cq, w_ck, w_cv, w_co):
    B, T, _ = h.shape
    M = mem.shape[1]
    q = (h @ w_cq).reshape(B, T, MEM_HEADS, MEM_HEAD_DIM)
    k = (mem @ w_ck).reshape(B, M, MEM_HEADS, MEM_HEAD_DIM)
    v = (mem @ w_cv).reshape(B, M, MEM_HEADS, MEM_HEAD_DIM)
    s = jnp.einsum('bthd,bmhd->bhtm', q, k, preferred_element_type=jnp.float32) * (MEM_HEAD_DIM ** -0.5)
    p = jax.nn.softmax(s, axis=-1)
    o = jnp.einsum('bhtm,bmhd->bthd', p.astype(v.dtype), v).reshape(B, T, MEM_WIDTH)
    return o @ w_co

def moe_ffn(h, w_router, router_bias, exp_gate, exp_up, exp_down, sh_gate, sh_up, sh_down):
    B, T, D = h.shape
    N = B * T
    hf = h.reshape(N, D)
    scores = jax.nn.sigmoid(jnp.matmul(hf, w_router, preferred_element_type=jnp.float32))
    biased = scores + router_bias.astype(jnp.float32)
    per_group = N_EXPERTS // N_EXPERT_GROUPS
    group_score = lax.top_k(biased.reshape(N, N_EXPERT_GROUPS, per_group), 2)[0].sum(-1)
    _, top_groups = lax.top_k(group_score, TOPK_GROUPS)
    group_mask = jax.nn.one_hot(top_groups, N_EXPERT_GROUPS, dtype=jnp.float32).sum(1) > 0
    expert_mask = jnp.repeat(group_mask, per_group, axis=1)
    _, idx = lax.top_k(jnp.where(expert_mask, biased, NEG_INF), TOP_K)
    gates = jnp.take_along_axis(scores, idx, axis=1)
    gates = gates / gates.sum(-1, keepdims=True) * ROUTED_SCALE

    A = N * TOP_K
    flat_e = idx.reshape(A)
    order = jnp.argsort(flat_e)
    sorted_e = flat_e[order]
    tok = (order // TOP_K).astype(jnp.int32)
    counts = jnp.bincount(flat_e, length=N_EXPERTS)
    padded = (counts + MOE_BLOCK - 1) // MOE_BLOCK * MOE_BLOCK
    pad_ends = jnp.cumsum(padded)
    rank = jnp.arange(A) - (jnp.cumsum(counts) - counts)[sorted_e]
    dest = (pad_ends - padded)[sorted_e] + rank
    n_blocks = -(-A // MOE_BLOCK) + N_EXPERTS
    P = n_blocks * MOE_BLOCK
    buf_tok = jnp.zeros((P,), jnp.int32).at[dest].set(tok)
    buf_w = jnp.zeros((P,), jnp.float32).at[dest].set(gates.reshape(A)[order])
    block_expert = jnp.minimum(
        jnp.searchsorted(pad_ends, jnp.arange(n_blocks) * MOE_BLOCK, side='right'), N_EXPERTS - 1)

    def expert_block(args):
        tok_blk, e = args
        xb = hf[tok_blk]
        return (jax.nn.silu(xb @ exp_gate[e]) * (xb @ exp_up[e])) @ exp_down[e]

    y = lax.map(expert_block, (buf_tok.reshape(n_blocks, MOE_BLOCK), block_expert))
    routed = jnp.zeros((N, D), jnp.float32).at[buf_tok].add(
        y.reshape(P, D).astype(jnp.float32) * buf_w[:, None])
    shared = (jax.nn.silu(hf @ sh_gate) * (hf @ sh_up)) @ sh_down
    return (routed + shared.astype(jnp.float32)).astype(h.dtype).reshape(B, T, D)

def setup_inputs(seed: int = 0) -> dict:
    key = jax.random.key(seed)
    ks = jax.random.split(key, 26)
    f32 = jnp.float32
    beta = (8.0 * DEPTH) ** -0.25

    def nrm(k, shape, fan_in, scale=1.0):
        return jax.random.normal(k, shape, f32) * (scale * fan_in ** -0.5)

    def gain(k):
        return 1.0 + 0.02 * jax.random.normal(k, (DEPTH, D_MODEL), f32)

    def small(k, shape):
        return 0.02 * jax.random.normal(k, shape, f32)

    col_scale = jnp.concatenate([jnp.ones((2 * ATTN_WIDTH,), f32), jnp.full((ATTN_WIDTH,), beta, f32),
                                 jnp.ones((POOL_WIDTH,), f32)])
    return {
        'x': jax.random.normal(ks[0], (BATCH, SEQ, D_MODEL), f32),
        'mem': jax.random.normal(ks[1], (BATCH, MEM_LEN, D_MODEL), f32),
        'w_in': nrm(ks[2], (DEPTH, D_MODEL, IN_WIDTH), D_MODEL) * col_scale,
        'pool_w': nrm(ks[3], (DEPTH, POOL_GROUPS, POOL_GROUP_DIM, POOL_GROUP_DIM), POOL_GROUP_DIM),
        'pool_scale': 1.0 + 0.02 * jax.random.normal(ks[4], (DEPTH, POOL_WIDTH), f32),
        'w_out': nrm(ks[5], (DEPTH, MIX_WIDTH, D_MODEL), MIX_WIDTH, beta),
        'ln1_g': gain(ks[6]),
        'ln1_b': small(ks[7], (DEPTH, D_MODEL)),
        'w_cq': nrm(ks[8], (DEPTH, D_MODEL, MEM_WIDTH), D_MODEL),
        'w_ck': nrm(ks[9], (DEPTH, D_MODEL, MEM_WIDTH), D_MODEL),
        'w_cv': nrm(ks[10], (DEPTH, D_MODEL, MEM_WIDTH), D_MODEL, beta),
        'w_co': nrm(ks[11], (DEPTH, MEM_WIDTH, D_MODEL), MEM_WIDTH, beta),
        'ln2_g': gain(ks[12]),
        'ln2_b': small(ks[13], (DEPTH, D_MODEL)),
        'w_router': nrm(ks[14], (DEPTH, D_MODEL, N_EXPERTS), D_MODEL),
        'router_bias': 0.01 * jax.random.normal(ks[15], (DEPTH, N_EXPERTS), f32),
        'exp_gate': nrm(ks[16], (DEPTH, N_EXPERTS, D_MODEL, EXPERT_HIDDEN), D_MODEL),
        'exp_up': nrm(ks[17], (DEPTH, N_EXPERTS, D_MODEL, EXPERT_HIDDEN), D_MODEL),
        'exp_down': nrm(ks[18], (DEPTH, N_EXPERTS, EXPERT_HIDDEN, D_MODEL), EXPERT_HIDDEN, beta),
        'sh_gate': nrm(ks[19], (DEPTH, D_MODEL, SHARED_HIDDEN), D_MODEL),
        'sh_up': nrm(ks[20], (DEPTH, D_MODEL, SHARED_HIDDEN), D_MODEL),
        'sh_down': nrm(ks[21], (DEPTH, SHARED_HIDDEN, D_MODEL), SHARED_HIDDEN, beta),
        'ln3_g': gain(ks[22]),
        'ln3_b': small(ks[23], (DEPTH, D_MODEL)),
    }

def reference(x, mem, w_in, pool_w, pool_scale, w_out, ln1_g, ln1_b, w_cq, w_ck, w_cv, w_co,
              ln2_g, ln2_b, w_router, router_bias, exp_gate, exp_up, exp_down, sh_gate, sh_up,
              sh_down, ln3_g, ln3_b):
    alpha = (2.0 * DEPTH) ** 0.25
    for l in range(DEPTH):
        x = layer_norm(alpha * x + hybrid_mixer(x, w_in[l], pool_w[l], pool_scale[l], w_out[l]),
                       ln1_g[l], ln1_b[l])
        x = layer_norm(alpha * x + memory_cross_attention(x, mem, w_cq[l], w_ck[l], w_cv[l], w_co[l]),
                       ln2_g[l], ln2_b[l])
        x = layer_norm(alpha * x + moe_ffn(x, w_router[l], router_bias[l], exp_gate[l], exp_up[l],
                                           exp_down[l], sh_gate[l], sh_up[l], sh_down[l]),
                       ln3_g[l], ln3_b[l])
    return x


_drawn_inputs = setup_inputs


def setup_inputs(seed=0):
    import zlib

    import numpy as np

    out = dict(_drawn_inputs(seed))
    spreads = {}
    factors = {}
    for name, (base, spread) in spreads.items():
        noise = np.random.default_rng([zlib.crc32(name.encode()), seed]).standard_normal(out[name].shape)
        drawn = base * np.exp(spread * noise) if base else spread * noise
        out[name] = __import__('jax').numpy.asarray(drawn.astype(out[name].dtype))
    for name, factor in factors.items():
        out[name] = (out[name] * factor).astype(out[name].dtype)
    return out
```

```python
from contextlib import ExitStack

import concourse.bass as bass
import numpy as np
from concourse import mybir

F32 = mybir.dt.float32
F32R = mybir.dt.float32r
I32 = mybir.dt.int32
U32 = mybir.dt.uint32
ALU = mybir.AluOpType
ACT = mybir.ActivationFunctionType
AX = mybir.AxisListType

P = 128
D = 1024
T = 2048
NT = T // P
KC = D // P
HEADS, HD = 8, 64
AW = HEADS * HD
PAIRS = HEADS // 2
PATTERNS = ((128, 1), (512, 4), (2048, 16))
POOL_WINDOWS = (2, 4, 8, 16)
PADW = 16
PW = 512
MIX = AW + PW
MEM = 256
MH, MHD = 4, 128
MW = MH * MHD
E = 64
EG = 8
TOPG = 4
TOPK = 8
HID = 256
ROUTED_SCALE = 2.5
LN_EPS = 1e-5
BIG = 1e30
ALPHA = 2.0 ** 0.25
GRP = 512
NG = T // GRP
NBLK = T * TOPK // P + E
ds = bass.ds


class Stage:

    def __init__(self, nc, name):
        self.nc, self.name, self.ctx, self.sems = nc, name, ExitStack(), []

    def __enter__(self):
        return self

    def __exit__(self, *exc):
        if self.sems:
            self.nc.clear_and_free_semaphores(self.sems)
            self.nc.all_engine_barrier()
        self.ctx.close()

    def sb(self, name, shape, dt=F32):
        return self.ctx.enter_context(self.nc.sbuf_tensor(f"{self.name}_{name}", shape, dt))

    def ps(self, name, shape, dt=F32):
        return self.ctx.enter_context(self.nc.psum_tensor(f"{self.name}_{name}", shape, dt))

    def sem(self, name):
        self.sems.append(self.nc.alloc_semaphore(name=f"{self.name}_{name}"))
        return self.sems[-1]


class Steps:

    def __init__(self, eng, sem, base=0):
        self.eng, self.sem, self.base, self.n = eng, sem, base, 0

    def then(self, ins):
        ins.then_inc(self.sem, 1)
        self.n += 1
        self.eng.wait_ge(self.sem, self.base + self.n)


def product(pe, out, a_hi, a_lo, b_hi, b_lo, first, last):
    pe.matmul(out, a_hi, b_hi, start=first, stop=False)
    pe.matmul(out, a_hi, b_lo, start=False, stop=False)
    return pe.matmul(out, a_lo, b_hi, start=False, stop=last)


LEAD = 2


def lead(eng, *sems, by=1):
    for sem in sems:
        eng.sem_inc(sem, LEAD * by)


def done(t, by=1):
    return (t + 1 + LEAD) * by


def loaded(i):
    return 16 * i + 32


def f32(ap):
    return ap.bitcast(F32)


def make_identity(nc, ident):
    with Stage(nc, "const") as st:
        cleared = st.sem("cleared")
        with nc.Block() as block:
            @block.gpsimd
            def _(pool):
                pool.memset(ident[:, :], 0.0).then_inc(cleared, 1)
                pool.wait_ge(cleared, 1)
                pool.affine_select(out=ident[:, :], in_=ident[:, :], compare_op=ALU.not_equal, fill=1.0,
                                   base=0, pattern=[[-1, P]], channel_multiplier=1)


def stage_transpose_and_v(nc, ident, xt_hi, xt_lo, x, w_in, v_dram):
    with Stage(nc, "xv") as st:
        x_in = st.sb("x_in", [P, 2, D])
        w_raw = st.sb("w_raw", [P, KC, AW])
        w_hi = st.sb("w_hi", [P, KC, AW], F32R)
        w_lo = st.sb("w_lo", [P, KC, AW], F32R)
        t_hi = st.sb("t_hi", [P, 2, KC, P], F32R)
        t_lo = st.sb("t_lo", [P, 2, KC, P], F32R)
        v_out = st.sb("v_out", [P, 2, AW])
        tp = st.ps("tp", [P, 2, KC, P])
        pv = st.ps("pv", [P, 2, AW])
        w_loaded, w_hi_ready, w_lo_ready = st.sem("w_loaded"), st.sem("w_hi_ready"), st.sem("w_lo_ready")
        x_loaded = [st.sem("x_loaded0"), st.sem("x_loaded1")]
        v_stored = [st.sem("v_stored0"), st.sem("v_stored1")]
        tp_ready, hi_ready, lo_ready = st.sem("tp_ready"), st.sem("hi_ready"), st.sem("lo_ready")
        hi_kept, lo_kept = st.sem("hi_kept"), st.sem("lo_kept")
        pv_ready, v_ready = st.sem("pv_ready"), st.sem("v_ready")

        with nc.Block() as block:
            @block.sync
            def _(sp):
                for u in range(2):
                    lead(sp, x_loaded[u], by=8)
                with sp.Fori(0, NT // 2) as i:
                    for u in range(2):
                        t = 2 * i + u
                        sp.wait_ge(tp_ready, done(t - 2))
                        sp.dma_start(x_in[:, u, :], x[ds(t * P, P), :]).then_inc(x_loaded[u], 16)

            @block.gpsimd
            def _(pool):
                lead(pool, hi_kept)
                with pool.Fori(0, NT // 2) as i:
                    for u in range(2):
                        t = 2 * i + u
                        pool.wait_ge(hi_ready, done(t))
                        pool.tensor_copy(xt_hi[:, :, ds(t * P, P)], t_hi[:, u, :, :]).then_inc(hi_kept, 1)

            @block.scalar
            def _(act):
                act.dma_start(w_raw[:, :, :], w_in[:, 2 * AW:3 * AW].rearrange("(k p) n -> p k n", p=P))\
                    .then_inc(w_loaded, 16)
                lead(act, lo_kept, v_ready)
                lead(act, *v_stored, by=8)
                act.wait_ge(w_loaded, 16)
                act.activation(w_hi[:, :, :], w_raw[:, :, :], ACT.Copy).then_inc(w_hi_ready, 1)
                with act.Fori(0, NT // 2) as i:
                    for u in range(2):
                        t = 2 * i + u
                        act.wait_ge(lo_ready, done(t))
                        act.activation(xt_lo[:, :, ds(t * P, P)], t_lo[:, u, :, :], ACT.Copy).then_inc(lo_kept, 1)
                        act.wait_ge(pv_ready, done(t))
                        act.wait_ge(v_stored[u], loaded(i - 1))
                        act.activation(v_out[:, u, :], pv[:, u, :], ACT.Copy).then_inc(v_ready, 1)
                        act.wait_ge(v_ready, done(t))
                        act.dma_start(v_dram[ds(t * P, P), :], v_out[:, u, :]).then_inc(v_stored[u], 16)
                for u in range(2):
                    act.wait_ge(v_stored[u], loaded(NT // 2 - 1))

            @block.vector
            def _(dve):
                lead(dve, hi_ready, lo_ready)
                dve.wait_ge(w_hi_ready, 1)
                dve.tensor_tensor(w_lo[:, :, :], w_raw[:, :, :], f32(w_hi[:, :, :]), ALU.subtract)\
                    .then_inc(w_lo_ready, 1)
                with dve.Fori(0, NT // 2) as i:
                    for u in range(2):
                        t = 2 * i + u
                        dve.wait_ge(tp_ready, done(t))
                        dve.wait_ge(hi_kept, done(t - 2))
                        dve.wait_ge(lo_kept, done(t - 2))
                        dve.wait_ge(pv_ready, done(t - 2))
                        dve.tensor_copy(t_hi[:, u, :, :], tp[:, u, :, :]).then_inc(hi_ready, 1)
                        dve.wait_ge(hi_ready, done(t))
                        dve.tensor_tensor(t_lo[:, u, :, :], tp[:, u, :, :], f32(t_hi[:, u, :, :]), ALU.subtract)\
                            .then_inc(lo_ready, 1)

            @block.tensor
            def _(pe):
                lead(pe, tp_ready, pv_ready)

                def transposes(i, u):
                    pe.wait_ge(x_loaded[u], loaded(i))
                    pe.wait_ge(lo_ready, done(2 * i + u - 2))
                    for k in range(KC):
                        last = pe.transpose(tp[:, u, k, :], x_in[:, u, k * P:(k + 1) * P], ident[:, :])
                    last.then_inc(tp_ready, 1)

                def products(t, u):
                    pe.wait_ge(lo_ready, done(t))
                    pe.wait_ge(v_ready, done(t - 2))
                    for k in range(KC):
                        last = product(pe, pv[:, u, :], t_hi[:, u, k, :], t_lo[:, u, k, :],
                                       w_hi[:, k, :], w_lo[:, k, :], k == 0, k == KC - 1)
                    last.then_inc(pv_ready, 1)

                transposes(0, 0)
                pe.wait_ge(w_lo_ready, 1)
                with pe.Fori(0, NT // 2 - 1) as i:
                    transposes(i, 1)
                    products(2 * i, 0)
                    transposes(i + 1, 0)
                    products(2 * i + 1, 1)
                transposes(NT // 2 - 1, 1)
                products(NT - 2, 0)
                products(NT - 1, 1)


def stage_project_qk(nc, xt_hi, xt_lo, w_in, qt_dram, kt_dram):
    steps = AW // P
    with Stage(nc, "qk") as st:
        w_raw = st.sb("w_raw", [P, 2, KC, P])
        w_hi = st.sb("w_hi", [P, 2, KC, P], F32R)
        w_lo = st.sb("w_lo", [P, 2, KC, P], F32R)
        out = st.sb("out", [P, 2, NG, GRP])
        acc = st.ps("acc", [P, 2, NG, GRP])
        w_loaded = [st.sem("w_loaded0"), st.sem("w_loaded1")]
        stored = [st.sem("stored0"), st.sem("stored1")]
        hi_ready, lo_ready = st.sem("hi_ready"), st.sem("lo_ready")
        acc_ready, out_ready = st.sem("acc_ready"), st.sem("out_ready")
        with nc.Block() as block:
            @block.sync
            def _(sp):
                lead(sp, *w_loaded, by=8)
                with sp.Fori(0, steps) as i:
                    for u in range(2):
                        sp.wait_ge(lo_ready, done(2 * i + u - 2))
                        sp.dma_start(w_raw[:, u, :, :],
                                     w_in[:, ds(u * AW + i * P, P)].rearrange("(k p) n -> p k n", p=P))\
                            .then_inc(w_loaded[u], 16)

            @block.vector
            def _(dve):
                lead(dve, hi_ready, lo_ready)
                with dve.Fori(0, steps) as i:
                    for u in range(2):
                        t = 2 * i + u
                        dve.wait_ge(w_loaded[u], loaded(i))
                        dve.wait_ge(acc_ready, done(t - 2))
                        dve.tensor_copy(w_hi[:, u, :, :], w_raw[:, u, :, :]).then_inc(hi_ready, 1)
                        dve.wait_ge(hi_ready, done(t))
                        dve.tensor_tensor(w_lo[:, u, :, :], w_raw[:, u, :, :], f32(w_hi[:, u, :, :]), ALU.subtract)\
                            .then_inc(lo_ready, 1)

            @block.tensor
            def _(pe):
                lead(pe, acc_ready)
                with pe.Fori(0, steps) as i:
                    for u in range(2):
                        t = 2 * i + u
                        pe.wait_ge(lo_ready, done(t))
                        pe.wait_ge(out_ready, done(t - 2))
                        for k in range(KC):
                            for g in range(NG):
                                cols = slice(g * GRP, (g + 1) * GRP)
                                last = product(pe, acc[:, u, g, :], w_hi[:, u, k, :], w_lo[:, u, k, :],
                                               xt_hi[:, k, cols], xt_lo[:, k, cols], k == 0, k == KC - 1)
                        last.then_inc(acc_ready, 1)

            @block.scalar
            def _(act):
                lead(act, out_ready)
                lead(act, *stored, by=8)
                with act.Fori(0, steps) as i:
                    for u, (scale, dram) in enumerate(((-(HD ** -0.5), qt_dram), (1.0, kt_dram))):
                        t = 2 * i + u
                        act.wait_ge(acc_ready, done(t))
                        act.wait_ge(stored[u], loaded(i - 1))
                        act.activation(out[:, u, :, :], acc[:, u, :, :], ACT.Copy, scale=scale).then_inc(out_ready, 1)
                        act.wait_ge(out_ready, done(t))
                        act.dma_start(dram[ds(i, 1), :, :].rearrange("a p n -> p (a n)"),
                                      out[:, u, :, :].rearrange("p g n -> p (g n)")).then_inc(stored[u], 16)
                for u in range(2):
                    act.wait_ge(stored[u], loaded(steps - 1))


def stage_pool(nc, xt_hi, xt_lo, w_in, pool_w, pool_scale, mix_hi_dram, mix_lo_dram):
    groups = len(POOL_WINDOWS)
    with Stage(nc, "pool") as st:
        w_raw = st.sb("w_raw", [P, 2, KC, P])
        w_hi = st.sb("w_hi", [P, 2, KC, P], F32R)
        w_lo = st.sb("w_lo", [P, 2, KC, P], F32R)
        pw = st.sb("pw", [P, groups, P])
        sc = st.sb("sc", [P, groups])
        tok = st.sb("tok", [P, PADW + T])
        sum_a = st.sb("sum_a", [P, PADW + T])
        sum_b = st.sb("sum_b", [P, PADW + T])
        first_n = st.sb("first_n", [P, PADW], I32)
        first_inv = st.sb("first_inv", [P, PADW])
        out_hi = st.sb("out_hi", [P, T], F32R)
        out_lo = st.sb("out_lo", [P, T], F32R)
        acc = st.ps("acc", [P, 2, NG, GRP])
        w_loaded, small_loaded = st.sem("w_loaded"), st.sem("small_loaded")
        split, acc_ready, tok_ready = st.sem("split"), st.sem("acc_ready"), st.sem("tok_ready")
        pooled, mixed, hi_ready, lo_ready = st.sem("pooled"), st.sem("mixed"), st.sem("hi_ready"), st.sem("lo_ready")
        padded, step, stored = st.sem("padded"), st.sem("step"), st.sem("stored")
        with nc.Block() as block:
            @block.sync
            def _(sp):
                sp.dma_start(pw[:, :, :], pool_w.rearrange("g c d -> c g d")).then_inc(small_loaded, 16)
                sp.dma_start(sc[:, :], pool_scale).then_inc(small_loaded, 16)
                for g in range(groups):
                    if g >= 2:
                        sp.wait_ge(split, 2 * (g - 1))
                        sp.wait_ge(w_loaded, 16 * g)
                    col = 3 * AW + g * P
                    sp.dma_start(w_raw[:, g % 2, :, :], w_in[:, col:col + P].rearrange("(k p) n -> p k n", p=P))\
                        .then_inc(w_loaded, 16)
                    if g == 0:
                        sp.wait_ge(w_loaded, 16)

            @block.gpsimd
            def _(pool):
                for b in (tok, sum_a, sum_b):
                    pool.memset(b[:, 0:PADW], 0.0).then_inc(padded, 1)
                pool.iota(first_n[:, :], pattern=[[1, PADW]], base=1, channel_multiplier=0).then_inc(padded, 1)

            @block.vector
            def _(dve):
                s = Steps(dve, step)
                dve.wait_ge(padded, 4)
                s.then(dve.tensor_copy(first_inv[:, :], first_n[:, :]))
                s.then(dve.reciprocal(first_inv[:, :], first_inv[:, :]))

                def split_weights(g):
                    dve.wait_ge(w_loaded, 16 * (g + 1))
                    if g >= 2:
                        dve.wait_ge(acc_ready, g - 1)
                    dve.tensor_copy(w_hi[:, g % 2, :, :], w_raw[:, g % 2, :, :]).then_inc(split, 1)
                    dve.wait_ge(split, 2 * g + 1)
                    dve.tensor_tensor(w_lo[:, g % 2, :, :], w_raw[:, g % 2, :, :], f32(w_hi[:, g % 2, :, :]),
                                      ALU.subtract).then_inc(split, 1)

                def rest(g):
                    dve.wait_ge(hi_ready, g + 1)
                    if g >= 1:
                        dve.wait_ge(stored, 32 * g)
                    dve.scalar_tensor_tensor(out=out_lo[:, :], in0=acc[:, g % 2, :, :].rearrange("p a n -> p (a n)"),
                                             scalar=sc[:, g:g + 1], in1=f32(out_hi[:, :]),
                                             op0=ALU.mult, op1=ALU.subtract).then_inc(lo_ready, 1)

                split_weights(0)
                split_weights(1)
                for g, w in enumerate(POOL_WINDOWS):
                    dve.wait_ge(tok_ready, g + 1)
                    if g >= 1:
                        dve.wait_ge(mixed, g)
                    src, ends = tok, [sum_a, sum_b]
                    for j in range(g + 1):
                        back, dst = 2 ** j, ends[j % 2]
                        s.then(dve.tensor_tensor(dst[:, PADW:], src[:, PADW:], src[:, PADW - back:PADW + T - back],
                                                 ALU.add))
                        src = dst
                    dst = ends[(g + 1) % 2]
                    s.then(dve.scalar_tensor_tensor(out=dst[:, PADW:], in0=src[:, PADW:], scalar=1.0 / w,
                                                    in1=tok[:, PADW:], op0=ALU.mult, op1=ALU.subtract))
                    s.then(dve.tensor_tensor(src[:, PADW:PADW + w], src[:, PADW:PADW + w], first_inv[:, 0:w], ALU.mult))
                    dve.tensor_tensor(dst[:, PADW:PADW + w], src[:, PADW:PADW + w], tok[:, PADW:PADW + w],
                                      ALU.subtract).then_inc(pooled, 1)
                    if g + 2 < groups:
                        split_weights(g + 2)
                    rest(g)

            @block.tensor
            def _(pe):
                def project(g):
                    pe.wait_ge(split, 2 * g + 2)
                    if g >= 2:
                        pe.wait_ge(lo_ready, g - 1)
                    for k in range(KC):
                        for n in range(NG):
                            cols = slice(n * GRP, (n + 1) * GRP)
                            last = product(pe, acc[:, g % 2, n, :], w_hi[:, g % 2, k, :], w_lo[:, g % 2, k, :],
                                           xt_hi[:, k, cols], xt_lo[:, k, cols], k == 0, k == KC - 1)
                    last.then_inc(acc_ready, 1)

                def linear(g):
                    pe.wait_ge(pooled, g + 1)
                    src = [sum_a, sum_b][(g + 1) % 2]
                    for n in range(NG):
                        last = pe.matmul(acc[:, g % 2, n, :], pw[:, g, :],
                                         src[:, PADW + n * GRP:PADW + (n + 1) * GRP], start=True, stop=True)
                    last.then_inc(mixed, 1)

                pe.wait_ge(small_loaded, 32)
                project(0)
                for g in range(groups):
                    if g + 1 < groups:
                        project(g + 1)
                    linear(g)

            @block.scalar
            def _(act):
                act.wait_ge(padded, 4)
                act.wait_ge(small_loaded, 32)
                for g in range(groups):
                    act.wait_ge(acc_ready, g + 1)
                    if g >= 1:
                        act.wait_ge(pooled, g)
                    act.activation(tok[:, PADW:], acc[:, g % 2, :, :].rearrange("p a n -> p (a n)"), ACT.Copy)\
                        .then_inc(tok_ready, 1)
                    act.wait_ge(mixed, g + 1)
                    if g >= 1:
                        act.wait_ge(stored, 32 * g)
                    act.activation(out_hi[:, :], acc[:, g % 2, :, :].rearrange("p a n -> p (a n)"), ACT.Copy,
                                   scale=sc[:, g:g + 1]).then_inc(hi_ready, 1)
                    act.wait_ge(lo_ready, g + 1)
                    act.dma_start(mix_hi_dram[g, :, :], f32(out_hi[:, :])).then_inc(stored, 16)
                    act.dma_start(mix_lo_dram[g, :, :], f32(out_lo[:, :])).then_inc(stored, 16)
                act.wait_ge(stored, 32 * groups)


def attention(nc, ident, v_dram, qt_dram, kt_dram, o_dram, stats_dram):
    tiles = [(b, dil, m, 1 if m < dil else 2) for b, (_, dil) in enumerate(PATTERNS) for m in range(NT)]
    assert all(window // dil == P for window, dil in PATTERNS)
    branches = len(PATTERNS)
    with Stage(nc, "attn") as st:
        q_t = st.sb("q_t", [P, 2, PAIRS, T])
        k_t = st.sb("k_t", [P, PAIRS, T])
        v_dil = st.sb("v_dil", [P, 2, NT, AW])
        bias = st.sb("bias", [P, 2, HEADS, 2 * P])
        dist_i = st.sb("dist_i", [P, 2 * P], I32)
        probs = st.sb("probs", [P, 2, HEADS, 2 * P])
        stats = st.sb("stats", [P, 4, 2, HEADS])
        p_t = st.sb("p_t", [P, 2, 2, 2, P])
        o_sb = st.sb("o_sb", [P, 2, AW])
        s_ps = st.ps("s_ps", [P, PAIRS, 2, 256])
        pt_ps = st.ps("pt_ps", [P, 2, 2, 256])
        o_ps = st.ps("o_ps", [P, 2, AW])
        qk_loaded, cleared, half_cleared = st.sem("qk_loaded"), st.sem("cleared"), st.sem("half_cleared")
        v_loaded = [st.sem(f"v_loaded{b}") for b in range(branches)]
        dist_ready, slopes_ready, cut_ready, bias_ready = (
            st.sem(n) for n in ("dist_ready", "slopes_ready", "cut_ready", "bias_ready"))
        s_ready, sm_ready = st.sem("s_ready"), st.sem("sm_ready")
        p_ready, pt_ready, pt_copied, pair_done = (st.sem(n) for n in ("p_ready", "pt_ready", "pt_copied", "pair_done"))
        o_copied = st.sem("o_copied")
        stored = [st.sem("stored0"), st.sem("stored1")]

        def run(scores, finish, tail=None):
            for t in range(len(tiles) + 1):
                for c in range(PAIRS):
                    if t < len(tiles):
                        scores(t, c)
                    if t:
                        finish(t - 1, c)
                if t and tail is not None:
                    tail(t - 1)

        def tokens(dil, m, count=P, back=0):
            first = (m // dil) * P * dil + m % dil - back * P * dil
            return ds(first, count, dil)

        with nc.Block() as block:
            @block.gpsimd
            def _(pool):
                pool.iota(dist_i[:, :], pattern=[[-1, 2 * P]], base=P, channel_multiplier=1).then_inc(dist_ready, 1)
                pool.wait_ge(dist_ready, 1)
                pool.memset(q_t[HD:, 0, :, :], 0.0).then_inc(cleared, 1)
                pool.wait_ge(cleared, 1)
                for b in range(branches):
                    pool.wait_ge(slopes_ready, b + 1)
                    pool.affine_select(out=bias[:, b % 2, :, :], in_=bias[:, b % 2, :, :], compare_op=ALU.is_ge, fill=BIG,
                                       base=P, pattern=[[0, HEADS], [-1, 2 * P]], channel_multiplier=1)\
                        .then_inc(cut_ready, 1)
                    pool.wait_ge(cut_ready, b + 1)
                    pool.affine_select(out=bias[:, b % 2, :, :], in_=bias[:, b % 2, :, :], compare_op=ALU.is_ge, fill=BIG,
                                       base=0, pattern=[[0, HEADS], [1, 2 * P]], channel_multiplier=-1)\
                        .then_inc(bias_ready, 1)

            @block.tensor
            def _(pe):
                def scores(t, c):
                    b, dil, m, blocks = tiles[t]
                    if t >= 1:
                        pe.wait_ge(sm_ready, PAIRS * (t - 1) + c + 1)
                    for half in range(2):
                        last = pe.matmul(s_ps[:, c, half, 0:blocks * P], q_t[:, half, c, tokens(dil, m)],
                                         k_t[:, c, tokens(dil, m, blocks * P, blocks - 1)], start=True, stop=True)
                    last.then_inc(s_ready, 1)

                def values(t, c):
                    b, dil, m, blocks = tiles[t]
                    pe.wait_ge(pt_copied, PAIRS * t + c + 1)
                    if c == 0 and t >= 2:
                        pe.wait_ge(o_copied, t - 1)
                    if c == 0 and m == 0:
                        pe.wait_ge(v_loaded[b], 16 * (NT // dil))
                    for half in range(2):
                        h = 2 * c + half
                        for k in range(blocks):
                            last = pe.matmul(o_ps[:, t % 2, h * HD:(h + 1) * HD], p_t[:, c % 2, half, k, :],
                                             v_dil[:, b % 2, m - dil * (blocks - 1 - k), h * HD:(h + 1) * HD],
                                             start=k == 0, stop=k == blocks - 1)
                    last.then_inc(pair_done, 1)

                def finish(t, c):
                    n = PAIRS * t + c
                    pe.wait_ge(p_ready, n + 1)
                    if n >= 2:
                        pe.wait_ge(pt_copied, n - 1)
                    for half in range(2):
                        for k in range(tiles[t][3]):
                            last = pe.transpose(pt_ps[:, c % 2, half, k * P:(k + 1) * P],
                                                probs[:, t % 2, 2 * c + half, k * P:(k + 1) * P], ident[:, :])
                    last.then_inc(pt_ready, 1)
                    if c:
                        values(t, c - 1)

                pe.wait_ge(qk_loaded, 64)
                pe.wait_ge(cleared, 1)
                pe.wait_ge(half_cleared, 1)
                run(scores, finish, lambda t: values(t, PAIRS - 1))

            @block.vector
            def _(dve):
                def slopes(b):
                    for h in range(HEADS):
                        last = dve.tensor_scalar(bias[:, b % 2, h, :], dist_i[:, :],
                                                 PATTERNS[b][1] * 2.0 ** (-8.0 * (h + 1) / HEADS), None, ALU.mult)
                    last.then_inc(slopes_ready, 1)

                def scores(t, c):
                    b, dil, m, blocks = tiles[t]
                    dve.wait_ge(s_ready, PAIRS * t + c + 1)
                    if c == 0:
                        dve.wait_ge(bias_ready, b + 1)
                    if c == 0 and m == 0 and 2 <= b + 1 < branches:
                        slopes(b + 1)
                    if c == 0 and t >= 2:
                        dve.wait_ge(pt_ready, PAIRS * (t - 1))
                    if c == 0 and t >= 4:
                        dve.wait_ge(stored[t % 2], 32 * (t // 2 - 1))
                    for half in range(2):
                        h = 2 * c + half
                        last = dve.tensor_tensor_reduce(out=probs[:, t % 2, h, 0:blocks * P],
                                                        in0=s_ps[:, c, half, 0:blocks * P],
                                                        in1=bias[:, b % 2, h, (2 - blocks) * P:], scale=1.0, scalar=3e38,
                                                        op0=ALU.add, op1=ALU.min, accum_out=stats[:, t % 4, 0, h:h + 1])
                    last.then_inc(sm_ready, 1)

                def finish(t, c):
                    n = PAIRS * t + c
                    dve.wait_ge(pt_ready, n + 1)
                    if n >= 2:
                        dve.wait_ge(pair_done, n - 1)
                    blocks = tiles[t][3]
                    dve.tensor_copy(p_t[:, c % 2, :, 0:blocks, :],
                                    pt_ps[:, c % 2, :, 0:blocks * P].rearrange("p a (k j) -> p a k j", j=P))\
                        .then_inc(pt_copied, 1)

                dve.memset(q_t[0:HD, 1, :, :], 0.0).then_inc(half_cleared, 1)
                dve.wait_ge(dist_ready, 1)
                slopes(0)
                slopes(1)
                run(scores, finish)

            @block.scalar
            def _(act):
                def exponentials(t, c):
                    blocks = tiles[t][3]
                    act.wait_ge(sm_ready, PAIRS * t + c + 1)
                    for half in range(2):
                        h = 2 * c + half
                        row = probs[:, t % 2, h, 0:blocks * P]
                        last = act.activation(row, row, ACT.Exp, scale=-1.0, bias=stats[:, t % 4, 0, h:h + 1],
                                              accum_out=stats[:, t % 4, 1, h:h + 1])
                    last.then_inc(p_ready, 1)

                def copy_out(t):
                    act.wait_ge(pair_done, PAIRS * (t + 1))
                    if t >= 2:
                        act.wait_ge(stored[t % 2], 32 * (t // 2))
                    act.activation(o_sb[:, t % 2, :], o_ps[:, t % 2, :], ACT.Copy).then_inc(o_copied, 1)

                run(exponentials, lambda t, c: None, copy_out)

            @block.sync
            def _(sp):
                def load_v(b):
                    dil = PATTERNS[b][1]
                    source = v_dram.rearrange("(n i r) f -> i n r f", r=dil, i=P)
                    for n in range(NT // dil):
                        sp.dma_start(v_dil[:, b % 2, n * dil:(n + 1) * dil, :], source[:, n, :, :])\
                            .then_inc(v_loaded[b], 16)

                def store(t):
                    b, dil, m, _ = tiles[t]
                    sp.wait_ge(o_copied, t + 1)
                    sp.dma_start(o_dram[b][tokens(dil, m), :], o_sb[:, t % 2, :]).then_inc(stored[t % 2], 16)
                    sp.dma_start(stats_dram[b][tokens(dil, m), :], stats[:, t % 4, :, :].rearrange("p a h -> p (a h)"))\
                        .then_inc(stored[t % 2], 16)
                    if m == NT - 1 and b + 2 < branches:
                        load_v(b + 2)

                for half in range(2):
                    rows = slice(half * HD, (half + 1) * HD)
                    sp.dma_start(q_t[rows, half, :, :], qt_dram[:, rows, :].rearrange("c p n -> p c n"))\
                        .then_inc(qk_loaded, 16)
                    sp.dma_start(k_t[rows, :, :], kt_dram[:, rows, :].rearrange("c p n -> p c n"))\
                        .then_inc(qk_loaded, 16)
                load_v(0)
                load_v(1)
                run(lambda t, c: None, lambda t, c: None, store)
                for u in range(2):
                    sp.wait_ge(stored[u], 32 * (len(tiles) // 2))


class Norm:

    def __init__(self, st, gain, shift):
        self.y = st.sb("y", [P, 2, D])
        self.out = st.sb("out", [P, 2, D])
        self.stored = [st.sem("stored0"), st.sem("stored1")]
        self.part = st.sb("bn", [P, 2, 2, 6])
        self.mv = st.sb("mv", [P, 2, 2])
        self.sd = st.sb("sd", [P, 2, 3])
        self.gate = st.sb("gate", [P, 1])
        self.gain, self.shift = st.sb("gain", [P, D]), st.sb("shift", [P, D])
        self.gain_in, self.shift_in = gain, shift
        self.loaded = st.sem("norm_loaded")
        self.var_ready, self.root_ready, self.map_ready = st.sem("var_ready"), st.sem("root_ready"), st.sem("map_ready")
        self.normed, self.gained, self.shifted = st.sem("normed"), st.sem("gained"), st.sem("shifted")

    def load(self, sp):
        sp.dma_start(self.gain[:, :], self.gain_in.partition_broadcast(P)).then_inc(self.loaded, 16)
        sp.dma_start(self.shift[:, :], self.shift_in.partition_broadcast(P)).then_inc(self.loaded, 16)

    def vector_stats(self, dve, s, u):
        for half in range(2):
            ins = dve.bn_stats(self.part[:, u, half, :], self.y[:, u, half * 512:(half + 1) * 512])
            if half:
                s.then(ins)
        dve.memset(self.gate[:, :], 0.0)
        s.then(dve.bn_aggr(self.mv[:, u, :], self.part[:, u, :, :].rearrange("p a b -> p (a b)")))
        dve.tensor_scalar(self.sd[:, u, 0:1], self.mv[:, u, 1:2], LN_EPS, None, ALU.add).then_inc(self.var_ready, 1)

    def scalar_root(self, act, t, u):
        act.wait_ge(self.var_ready, done(t))
        act.activation(self.sd[:, u, 0:1], self.sd[:, u, 0:1], ACT.Sqrt).then_inc(self.root_ready, 1)

    def vector_map(self, dve, s, t, u):
        dve.wait_ge(self.root_ready, done(t))
        s.then(dve.reciprocal(self.sd[:, u, 1:2], self.sd[:, u, 0:1]))
        dve.scalar_tensor_tensor(out=self.sd[:, u, 2:3], in0=self.mv[:, u, 0:1], scalar=-1.0,
                                 in1=self.sd[:, u, 1:2], op0=ALU.mult, op1=ALU.mult).then_inc(self.map_ready, 1)

    def scalar_norm(self, act, t, u):
        act.wait_ge(self.map_ready, done(t))
        act.activation(self.y[:, u, :], self.y[:, u, :], ACT.Identity, bias=self.sd[:, u, 2:3],
                       scale=self.sd[:, u, 1:2]).then_inc(self.normed, 1)

    def vector_gain(self, dve, t, u):
        dve.wait_ge(self.normed, done(t))
        dve.tensor_tensor(self.y[:, u, :], self.y[:, u, :], self.gain[:, :], ALU.mult).then_inc(self.gained, 1)

    def pool_shift(self, pool, t, i, u, *drams):
        pool.wait_ge(self.gained, done(t))
        if type(i) is not int or i:
            pool.wait_ge(self.stored[u], len(drams) * 16 * i)
        pool.tensor_tensor(self.out[:, u, :], self.y[:, u, :], self.shift[:, :], ALU.add).then_inc(self.shifted, 1)
        pool.wait_ge(self.shifted, done(t))
        for dram in drams:
            pool.dma_start(dram[ds(t * P, P), :], self.out[:, u, :]).then_inc(self.stored[u], 16)

    def all_stored(self, pool, drams=1):
        for u in range(2):
            pool.wait_ge(self.stored[u], drams * 16 * (NT // 2))

    def leads(self, dve=None, act=None, pool=None):
        if dve:
            lead(dve, self.var_ready, self.map_ready, self.gained)
        if act:
            lead(act, self.root_ready, self.normed)
        if pool:
            lead(pool, self.shifted)


class Splitter:

    def __init__(self, st, width):
        self.raw = st.sb("w_raw", [P, 2, width])
        self.loaded = [st.sem("w_loaded0"), st.sem("w_loaded1")]
        self.ready = st.sem("w_ready")
        self.jobs = []

    def add(self, dram, hi, lo):
        k = dram.shape[0] // P
        for j in range(k):
            self.jobs.append((dram[j * P:(j + 1) * P, :], hi[:, j, :], lo[:, j, :], dram.shape[1]))
        return 2 * len(self.jobs)

    def load(self, sp):
        for n, (src, _, _, w) in enumerate(self.jobs):
            if n >= 2:
                sp.wait_ge(self.ready, 2 * (n - 1))
            sp.dma_start(self.raw[:, n % 2, 0:w], src).then_inc(self.loaded[n % 2], 16)

    def cut(self, eng):
        for n, (_, hi, lo, w) in enumerate(self.jobs):
            eng.wait_ge(self.loaded[n % 2], 16 * (n // 2 + 1))
            eng.tensor_copy(hi, self.raw[:, n % 2, 0:w]).then_inc(self.ready, 1)
            eng.wait_ge(self.ready, 2 * n + 1)
            eng.tensor_tensor(lo, self.raw[:, n % 2, 0:w], f32(hi), ALU.subtract).then_inc(self.ready, 1)


def stage_mix(nc, ident, y_dram, x, o_dram, stats_dram, mix_hi_dram, mix_lo_dram, w_out, ln_g, ln_b):
    nb = len(PATTERNS)
    with Stage(nc, "mix") as st:
        sp_w = Splitter(st, D)
        w_hi = st.sb("w_hi", [P, MIX // P, D], F32R)
        w_lo = st.sb("w_lo", [P, MIX // P, D], F32R)
        weights_cut = sp_w.add(w_out, w_hi, w_lo)
        norm = Norm(st, ln_g, ln_b)
        o_in = st.sb("o_in", [P, 2, nb, AW])
        s_in = st.sb("s_in", [P, 2, nb, 2, HEADS])
        m_hi = st.sb("m_hi", [P, 2, PW // P, P], F32R)
        m_lo = st.sb("m_lo", [P, 2, PW // P, P], F32R)
        x_in = st.sb("x_in", [P, 2, D])
        low = st.sb("low", [P, 2, HEADS])
        wt = st.sb("wt", [P, 2, nb, HEADS])
        wl = st.sb("wl", [P, 2, nb, HEADS])
        den = st.sb("den", [P, 2, HEADS])
        a_hi = st.sb("a_hi", [P, 2, AW // P, P], F32R)
        a_lo = st.sb("a_lo", [P, 2, AW // P, P], F32R)
        tp = st.ps("tp", [P, 2, AW // P, P])
        acc = st.ps("acc", [P, 2, D])
        in_loaded = [st.sem("in_loaded0"), st.sem("in_loaded1")]
        m_loaded = [st.sem("m_loaded0"), st.sem("m_loaded1")]
        x_loaded = [st.sem("x_loaded0"), st.sem("x_loaded1")]
        link, diff_ready, weight_ready = st.sem("link"), st.sem("diff_ready"), st.sem("weight_ready")
        attn_ready, tp_ready, hi_ready = st.sem("attn_ready"), st.sem("tp_ready"), st.sem("hi_ready")
        a_ready, acc_ready, y_ready = st.sem("a_ready"), st.sem("acc_ready"), st.sem("y_ready")
        MERGE, LN = 8, 3

        with nc.Block() as block:
            @block.sync
            def _(sp):
                lead(sp, *x_loaded, by=8)
                lead(sp, *in_loaded, by=8 * 2 * nb)
                lead(sp, *m_loaded, by=8 * 2)
                norm.load(sp)

                def loads(t, i, u):
                    sp.wait_ge(tp_ready, done(t - 2))
                    rows = ds(t * P, P)
                    for b in range(nb):
                        sp.dma_start(o_in[:, u, b, :], o_dram[b][rows, :]).then_inc(in_loaded[u], 16)
                    for b in range(nb):
                        sp.dma_start(s_in[:, u, b, :, :].rearrange("p a h -> p (a h)"), stats_dram[b][rows, :])\
                            .then_inc(in_loaded[u], 16)
                    sp.wait_ge(y_ready, done(t - 2))
                    sp.dma_start(x_in[:, u, :], x[rows, :]).then_inc(x_loaded[u], 16)
                    for part, dram in ((m_hi, mix_hi_dram), (m_lo, mix_lo_dram)):
                        sp.dma_start(f32(part[:, u, :, :]), dram[:, :, rows].rearrange("g c n -> c g n"))\
                            .then_inc(m_loaded[u], 16)

                loads(0, 0, 0)
                loads(1, 0, 1)
                sp_w.load(sp)
                with sp.Fori(1, NT // 2) as i:
                    for u in range(2):
                        loads(2 * i + u, i, u)

            @block.vector
            def _(dve):
                lead(dve, diff_ready, attn_ready, a_ready, y_ready)
                norm.leads(dve=dve)
                dve.wait_ge(norm.loaded, 32)

                def merge(t, i, u, s):
                    dve.wait_ge(in_loaded[u], 2 * nb * loaded(i))
                    s.then(dve.tensor_tensor(low[:, u, :], s_in[:, u, 0, 0, :], s_in[:, u, 1, 0, :], ALU.min))
                    s.then(dve.tensor_tensor(low[:, u, :], low[:, u, :], s_in[:, u, 2, 0, :], ALU.min))
                    dve.tensor_tensor(wt[:, u, :, :], low[:, u, :].unsqueeze(1).to_broadcast([P, nb, HEADS]),
                                      s_in[:, u, :, 0, :], ALU.subtract).then_inc(diff_ready, 1)
                    dve.wait_ge(weight_ready, done(t))
                    s.then(dve.tensor_tensor(wl[:, u, :, :], wt[:, u, :, :], s_in[:, u, :, 1, :], ALU.mult))
                    s.then(dve.tensor_reduce(den[:, u, :], wl[:, u, :, :].rearrange("p b h -> p h b"), AX.X, ALU.add))
                    s.then(dve.reciprocal(den[:, u, :], den[:, u, :]))
                    s.then(dve.tensor_tensor(wt[:, u, :, :], wt[:, u, :, :],
                                             den[:, u, :].unsqueeze(1).to_broadcast([P, nb, HEADS]), ALU.mult))
                    outs = o_in[:, u, :, :].rearrange("p b (h d) -> p (b h) d", d=HD)
                    s.then(dve.tensor_tensor(outs, outs, wt[:, u, :, :].rearrange("p b h -> p (b h)").unsqueeze(2)
                                             .to_broadcast([P, nb * HEADS, HD]), ALU.mult))
                    s.then(dve.tensor_tensor(o_in[:, u, 0, :], o_in[:, u, 0, :], o_in[:, u, 1, :], ALU.add))
                    dve.tensor_tensor(o_in[:, u, 0, :], o_in[:, u, 0, :], o_in[:, u, 2, :], ALU.add)\
                        .then_inc(attn_ready, 1)

                def rest(t, u):
                    dve.wait_ge(hi_ready, done(t))
                    dve.tensor_tensor(a_lo[:, u, :, :], tp[:, u, :, :], f32(a_hi[:, u, :, :]), ALU.subtract)\
                        .then_inc(a_ready, 1)

                def residual(t, i, u, s):
                    dve.wait_ge(acc_ready, done(t))
                    dve.wait_ge(x_loaded[u], loaded(i))
                    dve.wait_ge(norm.shifted, done(t - 2))
                    dve.scalar_tensor_tensor(out=norm.y[:, u, :], in0=x_in[:, u, :], scalar=ALPHA,
                                             in1=acc[:, u, :], op0=ALU.mult, op1=ALU.add).then_inc(y_ready, 1)
                    dve.wait_ge(y_ready, done(t))
                    norm.vector_stats(dve, s, u)

                def finish(t, u, s):
                    norm.vector_map(dve, s, t, u)
                    norm.vector_gain(dve, t, u)

                def merge_of(t, i, u, normed):
                    s = Steps(dve, link, MERGE * t + LN * normed)
                    merge(t, i, u, s)
                    rest(t, u)
                    assert s.n == MERGE

                merge_of(0, 0, 0, 0)
                sp_w.cut(dve)
                merge_of(1, 0, 1, 0)
                with dve.Fori(0, NT // 2 - 1) as i:
                    for u in range(2):
                        merge_of(2 * i + u + 2, i + 1, u, 2 * i + u)
                        s = Steps(dve, link, (MERGE + LN) * (2 * i + u) + 3 * MERGE)
                        residual(2 * i + u, i, u, s)
                        finish(2 * i + u, u, s)
                for u in range(2):
                    s = Steps(dve, link, MERGE * NT + LN * (NT - 2 + u))
                    residual(NT - 2 + u, NT // 2 - 1, u, s)
                    finish(NT - 2 + u, u, s)

            @block.scalar
            def _(act):
                lead(act, weight_ready, hi_ready)
                norm.leads(act=act)

                def merge(t, u):
                    act.wait_ge(diff_ready, done(t))
                    act.activation(wt[:, u, :, :], wt[:, u, :, :], ACT.Exp).then_inc(weight_ready, 1)
                    act.wait_ge(tp_ready, done(t))
                    act.wait_ge(acc_ready, done(t - 2))
                    act.activation(a_hi[:, u, :, :], tp[:, u, :, :], ACT.Copy).then_inc(hi_ready, 1)

                def finish(t, u):
                    norm.scalar_root(act, t, u)
                    norm.scalar_norm(act, t, u)

                merge(0, 0)
                merge(1, 1)
                with act.Fori(0, NT // 2 - 1) as i:
                    for u in range(2):
                        merge(2 * i + u + 2, u)
                        finish(2 * i + u, u)
                finish(NT - 2, 0)
                finish(NT - 1, 1)

            @block.tensor
            def _(pe):
                lead(pe, tp_ready, acc_ready)

                def transposes(t, u):
                    pe.wait_ge(attn_ready, done(t))
                    pe.wait_ge(a_ready, done(t - 2))
                    for c in range(AW // P):
                        last = pe.transpose(tp[:, u, c, :], o_in[:, u, 0, c * P:(c + 1) * P], ident[:, :])
                    last.then_inc(tp_ready, 1)

                def products(t, i, u):
                    pe.wait_ge(a_ready, done(t))
                    pe.wait_ge(m_loaded[u], 2 * loaded(i))
                    pe.wait_ge(y_ready, done(t - 2))
                    parts = [(a_hi[:, u, c, :], a_lo[:, u, c, :]) for c in range(AW // P)]
                    parts += [(m_hi[:, u, c, :], m_lo[:, u, c, :]) for c in range(PW // P)]
                    for k, (hi, lo) in enumerate(parts):
                        for n in range(2):
                            cols = slice(n * 512, (n + 1) * 512)
                            last = product(pe, acc[:, u, cols], hi, lo, w_hi[:, k, cols], w_lo[:, k, cols],
                                           k == 0, k == len(parts) - 1)
                    last.then_inc(acc_ready, 1)

                transposes(0, 0)
                pe.wait_ge(sp_w.ready, weights_cut)
                with pe.Fori(0, NT // 2 - 1) as i:
                    for u in range(2):
                        transposes(2 * i + u + 1, 1 - u)
                        products(2 * i + u, i, u)
                transposes(NT - 1, 1)
                products(NT - 2, NT // 2 - 1, 0)
                products(NT - 1, NT // 2 - 1, 1)

            @block.gpsimd
            def _(pool):
                norm.leads(pool=pool)
                for u in range(2):
                    norm.pool_shift(pool, u, 0, u, y_dram)
                with pool.Fori(1, NT // 2) as i:
                    for u in range(2):
                        norm.pool_shift(pool, 2 * i + u, i, u, y_dram)
                norm.all_stored(pool)


def stage_memory(nc, ident, mem, w_ck, w_cv, k_mem, v_mem):
    blocks = MEM // P
    with Stage(nc, "mem") as st:
        m_in = st.sb("m_in", [P, blocks, D])
        m_t = st.sb("m_t", [P, KC, MEM])
        wk = st.sb("wk", [P, KC, MW])
        wv = st.sb("wv", [P, KC, MW])
        tp = st.ps("tp", [P, KC, MEM])
        kp = st.ps("kp", [P, MH, MEM])
        vp = st.ps("vp", [P, blocks, MW])
        m_loaded, w_loaded = st.sem("m_loaded"), st.sem("w_loaded")
        tp_ready, t_ready, k_ready, v_ready = (st.sem(n) for n in ("tp_ready", "t_ready", "k_ready", "v_ready"))
        with nc.Block() as block:
            @block.sync
            def _(sp):
                sp.dma_start(m_in[:, :, :], mem.rearrange("(b p) n -> p b n", p=P)).then_inc(m_loaded, 16)
                sp.dma_start(wk[:, :, :], w_ck.rearrange("(k p) n -> p k n", p=P)).then_inc(w_loaded, 16)
                sp.wait_ge(w_loaded, 16)
                sp.dma_start(wv[:, :, :], w_cv.rearrange("(k p) n -> p k n", p=P)).then_inc(w_loaded, 16)

            @block.tensor
            def _(pe):
                pe.wait_ge(m_loaded, 16)
                for b in range(blocks):
                    for k in range(KC):
                        last = pe.transpose(tp[:, k, b * P:(b + 1) * P], m_in[:, b, k * P:(k + 1) * P], ident[:, :])
                last.then_inc(tp_ready, 1)
                pe.wait_ge(t_ready, 1)
                pe.wait_ge(w_loaded, 16)
                for h in range(MH):
                    for k in range(KC):
                        last = pe.matmul(kp[:, h, :], wk[:, k, h * P:(h + 1) * P], m_t[:, k, :],
                                         start=k == 0, stop=k == KC - 1)
                last.then_inc(k_ready, 1)
                pe.wait_ge(w_loaded, 32)
                for b in range(blocks):
                    for k in range(KC):
                        last = pe.matmul(vp[:, b, :], m_t[:, k, b * P:(b + 1) * P], wv[:, k, :],
                                         start=k == 0, stop=k == KC - 1)
                last.then_inc(v_ready, 1)

            @block.vector
            def _(dve):
                dve.wait_ge(tp_ready, 1)
                dve.tensor_copy(m_t[:, :, :], tp[:, :, :]).then_inc(t_ready, 1)
                dve.wait_ge(k_ready, 1)
                dve.tensor_copy(k_mem[:, :, :], kp[:, :, :])

            @block.scalar
            def _(act):
                act.wait_ge(v_ready, 1)
                act.activation(v_mem[:, :, :], vp[:, :, :], ACT.Copy)


def stage_cross(nc, ident, x_dram, k_mem, v_mem, w_cq, w_co, ln_g, ln_b, *y_drams):
    scale = MHD ** -0.5
    mb = MEM // P
    J = GRP // P
    with Stage(nc, "cross") as st:
        sp_w = Splitter(st, D)
        cq_hi, cq_lo = st.sb("cq_hi", [P, KC, MW], F32R), st.sb("cq_lo", [P, KC, MW], F32R)
        co_hi, co_lo = st.sb("co_hi", [P, MH, D], F32R), st.sb("co_lo", [P, MH, D], F32R)
        cq_cut = sp_w.add(w_cq, cq_hi, cq_lo)
        co_cut = sp_w.add(w_co, co_hi, co_lo)
        norm = Norm(st, ln_g, ln_b)
        xa = st.sb("xa", [P, 2, D])
        xr = st.sb("xr", [P, 2, D])
        xg_hi, xg_lo = st.sb("xg_hi", [P, KC, GRP], F32R), st.sb("xg_lo", [P, KC, GRP], F32R)
        q_t = st.sb("q_t", [P, MH, GRP])
        probs = st.sb("probs", [P, MH, MEM])
        p_t = st.sb("p_t", [P, MH, mb, GRP])
        o_hi, o_lo = st.sb("o_hi", [P, MH, GRP], F32R), st.sb("o_lo", [P, MH, GRP], F32R)
        top, nlow, tot, inv = (st.sb(n, [P, 2, MH]) for n in ("top", "nlow", "tot", "inv"))
        tp = st.ps("tp", [P, KC, P])
        s_ps = st.ps("s_ps", [P, MH, MEM])
        qd = st.ps("qd", [P, 2, GRP])
        acc = st.ps("acc", [P, D])
        a_loaded = [st.sem("a_loaded0"), st.sem("a_loaded1")]
        r_loaded = [st.sem("r_loaded0"), st.sem("r_loaded1")]
        ta_ready, ta_hi, ta_lo = st.sem("ta_ready"), st.sem("ta_hi"), st.sem("ta_lo")
        q_acc, q_copied = st.sem("q_acc"), st.sem("q_copied")
        s_ready, top_ready, low_ready, e_ready, p_ready = (
            st.sem(n) for n in ("s_ready", "top_ready", "low_ready", "e_ready", "p_ready"))
        pt_ready, pt_copied = st.sem("pt_ready"), st.sem("pt_copied")
        d_ready, d_hi, d_lo = st.sem("d_ready"), st.sem("d_hi"), st.sem("d_lo")
        acc_ready, y_ready, link = st.sem("acc_ready"), st.sem("y_ready"), st.sem("link")
        LN, SOFT = 3, 1

        with nc.Block() as block:
            @block.sync
            def _(sp):
                lead(sp, *a_loaded, *r_loaded, by=8)
                norm.load(sp)

                def load_a(t, i, u):
                    sp.wait_ge(ta_ready, done(t - 2))
                    sp.dma_start(xa[:, u, :], x_dram[ds(t * P, P), :]).then_inc(a_loaded[u], 16)

                def load_r(t, i, u):
                    sp.wait_ge(y_ready, done(t - 2))
                    sp.dma_start(xr[:, u, :], x_dram[ds(t * P, P), :]).then_inc(r_loaded[u], 16)

                for t in range(J):
                    load_a(t, t // 2, t % 2)
                sp_w.load(sp)
                for t in range(J, 2 * J):
                    load_a(t, t // 2, t % 2)
                for t in range(2):
                    load_r(t, 0, t)
                with sp.Fori(0, (NT - 2 * J) // 2) as i:
                    for u in range(2):
                        load_a(2 * i + u + 2 * J, i + J, u)
                        load_r(2 * i + u + 2, i + 1, u)
                for t in range(NT - 2 * J + 2, NT):
                    load_r(t, t // 2, t % 2)

            def groups(eng, tile, group):
                def one(g, first=False, last=False, end=False):
                    for j in range(J):
                        tile(g, j, first, last, end)
                    if not end:
                        group(g, last)

                one(0, first=True)
                with eng.Fori(1, NG - 1) as g:
                    one(g)
                one(NG - 1, last=True)
                one(NG, end=True)

            @block.tensor
            def _(pe):
                lead(pe, ta_ready, q_acc, s_ready, pt_ready, d_ready, acc_ready)

                def transpose_x(t, i, u):
                    pe.wait_ge(a_loaded[u], loaded(i))
                    for k in range(KC):
                        last = pe.transpose(tp[:, k, :], xa[:, u, k * P:(k + 1) * P], ident[:, :])
                    last.then_inc(ta_ready, 1)

                def queries(g):
                    pe.wait_ge(ta_lo, done(J * g + J - 1))
                    for h in range(MH):
                        if h < 2:
                            if type(g) is not int or g:
                                pe.wait_ge(d_lo, done(MH * (g - 1) + h + 2))
                        else:
                            pe.wait_ge(q_copied, done(MH * g + h - 2))
                        for k in range(KC):
                            last = product(pe, qd[:, h % 2, :], cq_hi[:, k, h * P:(h + 1) * P],
                                           cq_lo[:, k, h * P:(h + 1) * P], xg_hi[:, k, :], xg_lo[:, k, :],
                                           k == 0, k == KC - 1)
                        last.then_inc(q_acc, 1)

                def tile(g, j, first, last, end):
                    t = J * g + j
                    if not end:
                        pe.wait_ge(q_copied, done(MH * g + MH - 1))
                        pe.wait_ge(e_ready, done(t - 1))
                        for h in range(MH):
                            ins = pe.matmul(s_ps[:, h, :], q_t[:, h, j * P:(j + 1) * P], k_mem[:, h, :],
                                            start=True, stop=True)
                        ins.then_inc(s_ready, 1)
                    if not first:
                        pe.wait_ge(d_lo, done(MH * (g - 1) + MH - 1))
                        pe.wait_ge(y_ready, done(t - J - 1))
                        for h in range(MH):
                            for n in range(2):
                                cols = slice(n * 512, (n + 1) * 512)
                                ins = product(pe, acc[:, cols], o_hi[:, h, j * P:(j + 1) * P],
                                              o_lo[:, h, j * P:(j + 1) * P], co_hi[:, h, cols], co_lo[:, h, cols],
                                              h == 0, h == MH - 1)
                        ins.then_inc(acc_ready, 1)
                    if not last and not end:
                        pe.wait_ge(pt_copied, done(t - 1))
                        transpose_x(t + J, (J // 2) * (g + 1) + j // 2, j % 2)
                    if not end:
                        pe.wait_ge(p_ready, done(t))
                        if last:
                            pe.wait_ge(pt_copied, done(t - 1))
                        else:
                            pe.wait_ge(ta_lo, done(t + J))
                        for h in range(MH):
                            for b in range(mb):
                                ins = pe.transpose(tp[:, 2 * h + b, :], probs[:, h, b * P:(b + 1) * P], ident[:, :])
                        ins.then_inc(pt_ready, 1)

                def group(g, last):
                    pe.wait_ge(pt_copied, done(J * g + J - 1))
                    for h in range(MH):
                        if h < 2:
                            pe.wait_ge(q_copied, done(MH * g + h + 2))
                        else:
                            pe.wait_ge(d_lo, done(MH * g + h - 2))
                        for b in range(mb):
                            ins = pe.matmul(qd[:, h % 2, :], v_mem[:, b, h * P:(h + 1) * P], p_t[:, h, b, :],
                                            start=b == 0, stop=b == mb - 1)
                        ins.then_inc(d_ready, 1)
                    if not last:
                        queries(g + 1)

                for t in range(J):
                    if t:
                        pe.wait_ge(ta_lo, done(t - 1))
                    transpose_x(t, t // 2, t % 2)
                pe.wait_ge(sp_w.ready, cq_cut)
                queries(0)
                pe.wait_ge(sp_w.ready, co_cut)
                groups(pe, tile, group)

            @block.vector
            def _(dve):
                lead(dve, ta_lo, top_ready, low_ready, p_ready, d_lo, y_ready)
                norm.leads(dve=dve)
                dve.wait_ge(norm.loaded, 32)

                def cut_x(t, col):
                    dve.wait_ge(ta_hi, done(t))
                    dve.tensor_tensor(xg_lo[:, :, col:col + P], tp[:, :, :], f32(xg_hi[:, :, col:col + P]),
                                      ALU.subtract).then_inc(ta_lo, 1)

                def tile(g, j, first, last, end):
                    t = J * g + j
                    u = j % 2
                    e = t - J
                    if not end:
                        dve.wait_ge(s_ready, done(t))
                        dve.wait_ge(e_ready, done(t - 2))
                        dve.tensor_reduce(top[:, u, :], s_ps[:, :, :], AX.X, ALU.max).then_inc(top_ready, 1)
                        dve.wait_ge(top_ready, done(t))
                        dve.tensor_scalar(nlow[:, u, :], top[:, u, :], -scale, None, ALU.mult).then_inc(low_ready, 1)
                    if not end:
                        dve.wait_ge(e_ready, done(t))
                        s = Steps(dve, link, SOFT * t + (0 if first else LN * e))
                        s.then(dve.reciprocal(inv[:, u, :], tot[:, u, :]))
                        dve.tensor_tensor(probs[:, :, :], probs[:, :, :],
                                          inv[:, u, :].unsqueeze(2).to_broadcast([P, MH, MEM]), ALU.mult)\
                            .then_inc(p_ready, 1)
                    if not first:
                        dve.wait_ge(acc_ready, done(e))
                        dve.wait_ge(r_loaded[u], loaded((J // 2) * (g - 1) + j // 2))
                        dve.wait_ge(norm.shifted, done(e - 2))
                        dve.scalar_tensor_tensor(out=norm.y[:, u, :], in0=xr[:, u, :], scalar=ALPHA,
                                                 in1=acc[:, :], op0=ALU.mult, op1=ALU.add).then_inc(y_ready, 1)
                        dve.wait_ge(y_ready, done(e))
                        s = Steps(dve, link, SOFT * (NT if end else t + 1) + LN * e)
                        norm.vector_stats(dve, s, u)
                        norm.vector_map(dve, s, e, u)
                        norm.vector_gain(dve, e, u)
                    if not last and not end:
                        cut_x(t + J, j * P)

                def group(g, last):
                    for h in range(MH):
                        dve.wait_ge(d_hi, done(MH * g + h))
                        dve.tensor_tensor(o_lo[:, h, :], qd[:, h % 2, :], f32(o_hi[:, h, :]), ALU.subtract)\
                            .then_inc(d_lo, 1)

                for t in range(J):
                    cut_x(t, t * P)
                sp_w.cut(dve)
                groups(dve, tile, group)

            @block.scalar
            def _(act):
                lead(act, ta_hi, q_copied, e_ready, pt_copied, d_hi)
                norm.leads(act=act)

                def cut_x(t, col):
                    act.wait_ge(ta_ready, done(t))
                    act.activation(xg_hi[:, :, col:col + P], tp[:, :, :], ACT.Copy).then_inc(ta_hi, 1)

                def copy_queries(g):
                    for h in range(MH):
                        act.wait_ge(q_acc, done(MH * g + h))
                        act.activation(q_t[:, h, :], qd[:, h % 2, :], ACT.Copy).then_inc(q_copied, 1)

                def tile(g, j, first, last, end):
                    t = J * g + j
                    u = j % 2
                    if not end:
                        act.wait_ge(low_ready, done(t))
                        act.wait_ge(pt_ready, done(t - 1))
                        act.wait_ge(p_ready, done(t - 2))
                        for h in range(MH):
                            ins = act.activation(probs[:, h, :], s_ps[:, h, :], ACT.Exp, scale=scale,
                                                 bias=nlow[:, u, h:h + 1], accum_out=tot[:, u, h:h + 1])
                        ins.then_inc(e_ready, 1)
                    if not first:
                        norm.scalar_root(act, t - J, u)
                        norm.scalar_norm(act, t - J, u)
                    if not last and not end:
                        cut_x(t + J, j * P)
                    if not end:
                        act.wait_ge(pt_ready, done(t))
                        act.activation(p_t[:, :, :, j * P:(j + 1) * P],
                                       tp[:, :, :].rearrange("p (h b) n -> p h b n", b=mb), ACT.Copy)\
                            .then_inc(pt_copied, 1)

                def group(g, last):
                    for h in range(MH):
                        act.wait_ge(d_ready, done(MH * g + h))
                        act.activation(o_hi[:, h, :], qd[:, h % 2, :], ACT.Copy).then_inc(d_hi, 1)
                    if not last:
                        copy_queries(g + 1)

                for t in range(J):
                    cut_x(t, t * P)
                copy_queries(0)
                groups(act, tile, group)

            @block.gpsimd
            def _(pool):
                norm.leads(pool=pool)
                for u in range(2):
                    norm.pool_shift(pool, u, 0, u, *y_drams)
                with pool.Fori(1, NT // 2) as i:
                    for u in range(2):
                        norm.pool_shift(pool, 2 * i + u, i, u, *y_drams)
                norm.all_stored(pool, len(y_drams))


TAB = NBLK + 4
HALF = TAB // 2
ROWS = T + P


def stage_route(nc, ident, x_dram, w_router, scores):
    J = GRP // P
    with Stage(nc, "route") as st:
        w_raw = st.sb("w_raw", [P, KC, E])
        w_hi, w_lo = st.sb("w_hi", [P, KC, P], F32R), st.sb("w_lo", [P, KC, P], F32R)
        xa = st.sb("xa", [P, 2, D])
        xg_hi, xg_lo = st.sb("xg_hi", [P, 2, KC, GRP], F32R), st.sb("xg_lo", [P, 2, KC, GRP], F32R)
        lg_t = st.sb("lg_t", [E, 2, GRP])
        tp = st.ps("tp", [P, 2, KC, P])
        lg = st.ps("lg", [P, 2, GRP])
        tb = st.ps("tb", [P, 2, 512])
        w_loaded, w_cut, cleared = st.sem("w_loaded"), st.sem("w_cut"), st.sem("cleared")
        a_loaded = [st.sem("a_loaded0"), st.sem("a_loaded1")]
        ta_ready, ta_hi, ta_lo = st.sem("ta_ready"), st.sem("ta_hi"), st.sem("ta_lo")
        lg_ready, lg_copied, tb_ready, s_ready = (st.sem(n) for n in ("lg_ready", "lg_copied", "tb_ready", "s_ready"))
        with nc.Block() as block:
            @block.gpsimd
            def _(pool):
                pool.memset(f32(w_hi[:, :, :]), 0.0).then_inc(cleared, 1)
                pool.memset(f32(w_lo[:, :, :]), 0.0).then_inc(cleared, 1)

            @block.sync
            def _(sp):
                sp.dma_start(w_raw[:, :, :], w_router.rearrange("(k p) n -> p k n", p=P)).then_inc(w_loaded, 16)
                for t in range(NT):
                    if t >= 2:
                        sp.wait_ge(ta_ready, t - 1)
                    sp.dma_start(xa[:, t % 2, :], x_dram[t * P:(t + 1) * P, :]).then_inc(a_loaded[t % 2], 16)

            @block.tensor
            def _(pe):
                def transposes(g):
                    for t in range(J * g, J * g + J):
                        pe.wait_ge(a_loaded[t % 2], 16 * (t // 2 + 1))
                        if t >= 2:
                            pe.wait_ge(ta_lo, t - 1)
                        for k in range(KC):
                            last = pe.transpose(tp[:, t % 2, k, :], xa[:, t % 2, k * P:(k + 1) * P], ident[:, :])
                        last.then_inc(ta_ready, 1)

                def logits(g):
                    pe.wait_ge(ta_lo, J * (g + 1))
                    if g >= 2:
                        pe.wait_ge(lg_copied, g - 1)
                    for k in range(KC):
                        last = product(pe, lg[:, g % 2, :], w_hi[:, k, :], w_lo[:, k, :], xg_hi[:, g % 2, k, :],
                                       xg_lo[:, g % 2, k, :], k == 0, k == KC - 1)
                    last.then_inc(lg_ready, 1)

                def back(g):
                    pe.wait_ge(lg_copied, g + 1)
                    if g >= 2:
                        pe.wait_ge(s_ready, g - 1)
                    for j in range(J):
                        last = pe.transpose(tb[:, g % 2, j * E:(j + 1) * E], lg_t[:, g % 2, j * P:(j + 1) * P],
                                            ident[0:E, 0:E])
                    last.then_inc(tb_ready, 1)

                transposes(0)
                pe.wait_ge(w_cut, 2)
                for g in range(NG):
                    if g + 1 < NG:
                        transposes(g + 1)
                    logits(g)
                    back(g)

            @block.vector
            def _(dve):
                dve.wait_ge(w_loaded, 16)
                dve.wait_ge(cleared, 2)
                dve.tensor_copy(w_hi[:, :, 0:E], w_raw[:, :, :]).then_inc(w_cut, 1)
                dve.wait_ge(w_cut, 1)
                dve.tensor_tensor(w_lo[:, :, 0:E], w_raw[:, :, :], f32(w_hi[:, :, 0:E]), ALU.subtract).then_inc(w_cut, 1)
                for t in range(NT):
                    g, cols = t // J, slice(t % J * P, (t % J + 1) * P)
                    dve.wait_ge(ta_hi, t + 1)
                    dve.tensor_tensor(xg_lo[:, g % 2, :, cols], tp[:, t % 2, :, :], f32(xg_hi[:, g % 2, :, cols]),
                                      ALU.subtract).then_inc(ta_lo, 1)

            @block.scalar
            def _(act):
                def finish(g):
                    act.wait_ge(lg_ready, g + 1)
                    act.activation(lg_t[:, g % 2, :], lg[0:E, g % 2, :], ACT.Copy).then_inc(lg_copied, 1)
                    act.wait_ge(tb_ready, g + 1)
                    act.activation(scores[:, J * g:J * (g + 1), :].rearrange("p t e -> p (t e)"),
                                   tb[:, g % 2, 0:J * E], ACT.Sigmoid).then_inc(s_ready, 1)

                for t in range(NT):
                    g, cols = t // J, slice(t % J * P, (t % J + 1) * P)
                    act.wait_ge(ta_ready, t + 1)
                    if g >= 2 and t % J == 0:
                        act.wait_ge(lg_ready, g - 1)
                    act.activation(xg_hi[:, g % 2, :, cols], tp[:, t % 2, :, :], ACT.Copy).then_inc(ta_hi, 1)
                    if t % J == J - 1 and g:
                        finish(g - 1)
                finish(NG - 1)


class Routing:

    def __init__(self, st):
        self.rows = st.sb("rows", [P, 2, HALF], I32)
        self.gates = st.sb("gates", [P, 2, HALF])
        self.table = st.sb("table", [1, 2, TAB], I32)
        self.total = st.sb("total", [1, 1], I32)


def stage_shared_and_dispatch(nc, ident, x_dram, acc_dram, slots_dram, sh_gate, sh_up, sh_down, bias_in, scores,
                              routing):
    J = GRP // P
    HC = HID // P
    with Stage(nc, "shared") as st:
        sp_w = Splitter(st, D)
        gu_hi, gu_lo = st.sb("gu_hi", [P, KC, 2 * HID], F32R), st.sb("gu_lo", [P, KC, 2 * HID], F32R)
        dn_hi, dn_lo = st.sb("dn_hi", [P, HC, D], F32R), st.sb("dn_lo", [P, HC, D], F32R)
        sp_w.add(sh_gate, gu_hi[:, :, 0:HID], gu_lo[:, :, 0:HID])
        gu_cut = sp_w.add(sh_up, gu_hi[:, :, HID:], gu_lo[:, :, HID:])
        dn_cut = sp_w.add(sh_down, dn_hi, dn_lo)
        xa = st.sb("xa", [P, 2, D])
        xr = st.sb("xr", [P, 2, D])
        out = st.sb("out", [P, 2, D])
        xg_hi, xg_lo = st.sb("xg_hi", [P, KC, GRP], F32R), st.sb("xg_lo", [P, KC, GRP], F32R)
        sg = st.sb("sg", [P, HC, GRP])
        h_hi, h_lo = st.sb("h_hi", [P, HC, GRP], F32R), st.sb("h_lo", [P, HC, GRP], F32R)
        bias = st.sb("bias", [P, E])
        upper = st.sb("upper", [P, P])
        upper_i = st.sb("upper_i", [E, E])
        ones = st.sb("ones", [P, P])
        low8 = st.sb("low8", [P, EG, EG])
        num_i = st.sb("num_i", [P, TAB], I32)
        num = st.sb("num", [P, TAB])
        tok_i = st.sb("tok_i", [P, NT], I32)
        biased = st.sb("biased", [P, NT, E])
        top8 = st.sb("top8", [P, NT * EG, 8])
        gsum = st.sb("gsum", [P, NT, EG])
        beats = st.sb("beats", [P, NT, EG, EG])
        ties = top8[:, :, :].rearrange("p (t g) m -> p t g m", g=EG)
        grank = st.sb("grank", [P, NT, EG])
        val8 = st.sb("val8", [P, NT, TOPK])
        idx8 = st.sb("idx8", [P, NT, TOPK], U32)
        idxf = st.sb("idxf", [P, NT, TOPK])
        chosen = st.sb("chosen", [P, NT, E])
        slot = st.sb("slot", [P, NT, E])
        one_hot = st.sb("one_hot", [P, J, TOPK, E])
        picked = st.sb("picked", [P, J, TOPK, E])
        slot8 = st.sb("slot8", [P, NT, TOPK])
        slot8_i = st.sb("slot8_i", [P, NT, TOPK], I32)
        gate8 = st.sb("gate8", [P, NT, TOPK])
        gtot = st.sb("gtot", [P, NT])
        pairs = st.sb("pairs", [P, NT, TOPK, 2])
        empty = st.sb("empty", [HALF, P, 2])
        nblk_i = st.sb("nblk_i", [E, P], I32)
        nblk = st.sb("nblk", [E, P])
        base = st.sb("base", [P, E])
        incl = st.sb("incl", [E, 1])
        past = st.sb("past", [E, TAB])
        erow = st.sb("erow", [1, 2, TAB])
        slots_in = st.sb("slots_in", [HALF, 2, P, 2])
        tp = st.ps("tp", [P, KC, P])
        gu = st.ps("gu", [P, 2 * HC, GRP])
        acc = st.ps("acc", [P, D])
        (a_loaded0, a_loaded1, r_loaded0, r_loaded1, ta_ready, ta_hi, ta_lo, gu_ready, sg_ready, hh_ready, h_ready,
         acc_ready, out_ready, stored0, stored1, link) = (st.sem(n) for n in (
             "a_loaded0", "a_loaded1", "r_loaded0", "r_loaded1", "ta_ready", "ta_hi", "ta_lo", "gu_ready",
             "sg_ready", "hh_ready", "h_ready", "acc_ready", "out_ready", "stored0", "stored1", "link"))
        a_loaded, r_loaded, stored = [a_loaded0, a_loaded1], [r_loaded0, r_loaded1], [stored0, stored1]
        (consts, bias_loaded, chosen_ready, count_ready, nblk_ready, base_ready, slot_ready, table_ready, erow_ready,
         empty_ready, inited, pairs_ready, scattered, slots_loaded, slots_t, z_ready) = (st.sem(n) for n in (
             "consts", "bias_loaded", "chosen_ready", "count_ready", "nblk_ready", "base_ready", "slot_ready",
             "table_ready", "erow_ready", "empty_ready", "inited", "pairs_ready", "scattered", "slots_loaded",
             "slots_t", "z_ready"))
        h_product, z_stored = st.sem("h_product"), st.sem("z_stored")
        zero = st.sb("zero", [P, D])
        rk = gu[:, 0:2, :].rearrange("p a n -> p (a n)").rearrange("p (t e) -> p t e", e=E)
        slots_v = slots_dram.rearrange("(a q p) c -> q a p c", a=2, p=P)

        with nc.Block() as block:
            @block.gpsimd
            def _(pool):
                pool.iota(num_i[:, :], pattern=[[1, TAB]], base=0, channel_multiplier=0).then_inc(consts, 1)
                pool.iota(tok_i[:, :], pattern=[[P, NT]], base=0, channel_multiplier=1).then_inc(consts, 1)
                pool.memset(zero[:, :], 0.0).then_inc(z_ready, 1)
                pool.memset(ones[:, :], 1.0).then_inc(consts, 1)
                pool.memset(upper[:, :], 1.0).then_inc(consts, 1)
                pool.memset(upper_i[:, :], 1.0).then_inc(consts, 1)
                pool.memset(low8[:, :, :], 1.0).then_inc(consts, 1)
                pool.wait_ge(consts, 6)
                pool.affine_select(out=upper[:, :], in_=upper[:, :], compare_op=ALU.is_gt, fill=0.0, base=0,
                                   pattern=[[1, P]], channel_multiplier=-1).then_inc(consts, 1)
                pool.affine_select(out=upper_i[:, :], in_=upper_i[:, :], compare_op=ALU.is_ge, fill=0.0, base=0,
                                   pattern=[[1, E]], channel_multiplier=-1).then_inc(consts, 1)
                pool.affine_select(out=low8[:, :, :], in_=low8[:, :, :], compare_op=ALU.is_gt, fill=0.0, base=0,
                                   pattern=[[1, EG], [-1, EG]], channel_multiplier=0).then_inc(consts, 1)
                pool.wait_ge(inited, 32)
                n = 0
                for g in range(NG):
                    pool.wait_ge(pairs_ready, g + 1)
                    for t in range(J * g, J * g + J):
                        for k in range(TOPK):
                            pool.indirect_dma_start(slots_dram, bass.IndirectOffsetOnAxis(ap=slot8_i[:, t, k:k + 1], axis=0),
                                                    pairs[:, t, k, :], None).then_inc(scattered, 16)
                            n += 16
                pool.wait_ge(scattered, n)

            @block.sync
            def _(sp):
                lead(sp, *a_loaded, *r_loaded, *stored, by=8)
                sp.dma_start(bias[:, :], bias_in.partition_broadcast(P)).then_inc(bias_loaded, 16)

                def load_a(t, i, u):
                    sp.wait_ge(ta_ready, done(t - 2))
                    sp.dma_start(xa[:, u, :], x_dram[ds(t * P, P), :]).then_inc(a_loaded[u], 16)

                def load_r(t, i, u):
                    sp.wait_ge(out_ready, done(t - 2))
                    sp.dma_start(xr[:, u, :], x_dram[ds(t * P, P), :]).then_inc(r_loaded[u], 16)

                def store(t, u):
                    sp.wait_ge(out_ready, done(t))
                    sp.dma_start(acc_dram[ds(t * P, P), :], out[:, u, :]).then_inc(stored[u], 16)

                def group(g, next_group):
                    for j in range(J if next_group else 0):
                        load_a(J * (g + 1) + j, (J // 2) * (g + 1) + j // 2, j % 2)
                    for j in range(J):
                        load_r(J * g + j, (J // 2) * g + j // 2, j % 2)
                        if j:
                            store(J * g + j - 1, (j - 1) % 2)
                    store(J * g + J - 1, 1)

                load_a(0, 0, 0)
                load_a(1, 0, 1)
                sp.wait_ge(empty_ready, 1)
                for a in range(2):
                    sp.dma_start(slots_v[:, a, :, :], empty[:, :, :]).then_inc(inited, 16)
                sp.wait_ge(z_ready, 1)
                for dram in (x_dram, acc_dram):
                    sp.dma_start(dram[T:ROWS, :], zero[:, :]).then_inc(z_stored, 16)
                sp_w.load(sp)
                load_a(2, 1, 0)
                load_a(3, 1, 1)
                with sp.Fori(0, NG - 1) as g:
                    group(g, True)
                group(NG - 1, False)
                sp.wait_ge(z_stored, 32)
                for u in range(2):
                    sp.wait_ge(stored[u], loaded(NT // 2 - 1))
                sp.wait_ge(scattered, 16 * NT * TOPK)
                sp.dma_start(slots_in[:, :, :, :], slots_v).then_inc(slots_loaded, 16)

            @block.tensor
            def _(pe):
                lead(pe, ta_ready, gu_ready, acc_ready)

                def transposes(g):
                    for j in range(J):
                        t = J * g + j
                        pe.wait_ge(a_loaded[j % 2], loaded(g * (J // 2) + j // 2))
                        pe.wait_ge(ta_lo, done(t - 1))
                        for k in range(KC):
                            last = pe.transpose(tp[:, k, :], xa[:, j % 2, k * P:(k + 1) * P], ident[:, :])
                        last.then_inc(ta_ready, 1)

                def up(g):
                    pe.wait_ge(ta_lo, done(J * g + J - 1))
                    pe.wait_ge(h_ready, done(g - 1))
                    for c in range(2 * HC):
                        for k in range(KC):
                            last = product(pe, gu[:, c, :], gu_hi[:, k, c * P:(c + 1) * P], gu_lo[:, k, c * P:(c + 1) * P],
                                           xg_hi[:, k, :], xg_lo[:, k, :], k == 0, k == KC - 1)
                    last.then_inc(gu_ready, 1)

                def down(g):
                    pe.wait_ge(h_ready, done(g))
                    for j in range(J):
                        pe.wait_ge(out_ready, done(J * g + j - 1))
                        for c in range(HC):
                            for n in range(2):
                                cols, rows = slice(n * 512, (n + 1) * 512), slice(j * P, (j + 1) * P)
                                last = product(pe, acc[:, cols], h_hi[:, c, rows], h_lo[:, c, rows],
                                               dn_hi[:, c, cols], dn_lo[:, c, cols], c == 0, c == HC - 1)
                        last.then_inc(acc_ready, 1)

                transposes(0)
                pe.wait_ge(consts, 9)
                pe.wait_ge(chosen_ready, 1)
                for t in range(NT):
                    last = pe.matmul(rk[:, t, :], upper[:, :], chosen[:, t, :], start=True, stop=t == 0)
                    if t:
                        last = pe.matmul(rk[:, t, :], ones[:, :], slot[:, t - 1, :], start=False, stop=True)
                last.then_inc(count_ready, 1)
                pe.matmul(gu[0:E, 2, 0:P], slot[:, NT - 1, :], ones[:, :], start=True, stop=True).then_inc(count_ready, 1)
                pe.wait_ge(nblk_ready, 1)
                pe.matmul(gu[:, 3, 0:E], nblk[:, :], upper[0:E, 0:E], start=True, stop=True).then_inc(base_ready, 1)
                pe.wait_ge(base_ready, 2)
                pe.matmul(gu[0:E, 3, 0:P], upper_i[:, :], nblk[:, :], start=True, stop=True).then_inc(table_ready, 1)
                pe.wait_ge(table_ready, 2)
                pe.matmul(gu[0:32, 3, 0:TAB], ones[0:E, 0:32], past[:, :], start=True, stop=True).then_inc(erow_ready, 1)
                pe.wait_ge(erow_ready, 2)
                pe.wait_ge(slot_ready, 1)
                pe.wait_ge(sp_w.ready, gu_cut)
                up(0)
                pe.wait_ge(sp_w.ready, dn_cut)
                with pe.Fori(0, NG - 1) as g:
                    transposes(g + 1)
                    down(g)
                    up(g + 1)
                down(NG - 1)
                pe.wait_ge(slots_loaded, 16)
                pe.wait_ge(h_ready, done(NG - 1))
                for a in range(2):
                    for c in range(2):
                        last = pe.transpose(gu[:, 2 * a + c, 0:HALF], slots_in[:, a, :, c], ident[0:HALF, 0:HALF])
                last.then_inc(slots_t, 1)

            @block.scalar
            def _(act):
                lead(act, ta_hi, sg_ready, hh_ready)

                def cut(g):
                    act.wait_ge(gu_ready, done(g - 1))
                    for j in range(J):
                        act.wait_ge(ta_ready, done(J * g + j))
                        act.activation(xg_hi[:, :, j * P:(j + 1) * P], tp[:, :, :], ACT.Copy).then_inc(ta_hi, 1)

                def silu(g):
                    act.wait_ge(gu_ready, done(g))
                    act.wait_ge(hh_ready, done(g - 1))
                    act.activation(sg[:, :, :], gu[:, 0:HC, :], ACT.Sigmoid).then_inc(sg_ready, 1)
                    act.wait_ge(h_product, done(g))
                    act.wait_ge(acc_ready, done(J * g - 1))
                    act.activation(h_hi[:, :, :], sg[:, :, :], ACT.Copy).then_inc(hh_ready, 1)

                cut(0)
                silu(0)
                with act.Fori(1, NG) as g:
                    cut(g)
                    silu(g)

            @block.vector
            def _(dve):
                lead(dve, ta_lo, h_product, h_ready, out_ready)
                s = Steps(dve, link)

                def cut(g):
                    for j in range(J):
                        dve.wait_ge(ta_hi, done(J * g + j))
                        dve.tensor_tensor(xg_lo[:, :, j * P:(j + 1) * P], tp[:, :, :],
                                          f32(xg_hi[:, :, j * P:(j + 1) * P]), ALU.subtract).then_inc(ta_lo, 1)

                def silu(g, s):
                    dve.wait_ge(sg_ready, done(g))
                    s.then(dve.tensor_tensor(sg[:, :, :], sg[:, :, :], gu[:, 0:HC, :], ALU.mult))
                    dve.tensor_tensor(sg[:, :, :], sg[:, :, :], gu[:, HC:2 * HC, :], ALU.mult).then_inc(h_product, 1)
                    dve.wait_ge(hh_ready, done(g))
                    dve.tensor_tensor(h_lo[:, :, :], sg[:, :, :], f32(h_hi[:, :, :]), ALU.subtract).then_inc(h_ready, 1)

                def residual(g):
                    for j in range(J):
                        t, i, u = J * g + j, g * (J // 2) + j // 2, j % 2
                        dve.wait_ge(acc_ready, done(t))
                        dve.wait_ge(r_loaded[u], loaded(i))
                        dve.wait_ge(stored[u], loaded(i - 1))
                        dve.scalar_tensor_tensor(out=out[:, u, :], in0=xr[:, u, :], scalar=ALPHA, in1=acc[:, :],
                                                 op0=ALU.mult, op1=ALU.add).then_inc(out_ready, 1)

                def wide(ap, n):
                    return ap.unsqueeze(3).to_broadcast([P, NT, EG, n])

                def pick():
                    dve.wait_ge(bias_loaded, 16)
                    s.then(dve.tensor_tensor(biased[:, :, :], scores[:, :, :],
                                             bias[:, :].unsqueeze(1).to_broadcast([P, NT, E]), ALU.add))
                    for t in range(NT):
                        for g in range(EG):
                            last = dve.max(top8[:, t * EG + g, :], biased[:, t, g * EG:(g + 1) * EG])
                    s.then(last)
                    best = top8[:, :, :].rearrange("p (t g) m -> p t g m", g=EG)
                    s.then(dve.tensor_tensor(gsum[:, :, :], best[:, :, :, 0], best[:, :, :, 1], ALU.add))
                    other = gsum[:, :, :].unsqueeze(2).to_broadcast([P, NT, EG, EG])
                    own = wide(gsum[:, :, :], EG)
                    dve.tensor_tensor(beats[:, :, :, :], other, own, ALU.is_gt)
                    s.then(dve.tensor_tensor(ties, other, own, ALU.is_equal))
                    s.then(dve.tensor_tensor(ties, ties, low8[:, :, :].unsqueeze(1).to_broadcast([P, NT, EG, EG]), ALU.mult))
                    s.then(dve.tensor_tensor(beats[:, :, :, :], beats[:, :, :, :], ties, ALU.add))
                    s.then(dve.tensor_reduce(grank[:, :, :], beats[:, :, :, :], AX.X, ALU.add))
                    s.then(dve.tensor_scalar(grank[:, :, :], grank[:, :, :], TOPG - 0.5, None, ALU.is_lt))
                    by_group = biased[:, :, :].rearrange("p t (g m) -> p t g m", g=EG)
                    s.then(dve.tensor_tensor(by_group, by_group, wide(grank[:, :, :], E // EG), ALU.mult))
                    s.then(dve.tensor_scalar(grank[:, :, :], grank[:, :, :], -1.0, BIG, ALU.add, ALU.mult))
                    s.then(dve.tensor_tensor(by_group, by_group, wide(grank[:, :, :], E // EG), ALU.add))
                    for t in range(NT):
                        last = dve.max(val8[:, t, :], biased[:, t, :])
                    s.then(last)
                    for t in range(NT):
                        dve.max_index(idx8[:, t, :], val8[:, t, :], biased[:, t, :])
                        last = dve.match_replace(chosen[:, t, :], val8[:, t, :], biased[:, t, :], -3 * BIG)
                    s.then(last)
                    s.then(dve.tensor_scalar(chosen[:, :, :], chosen[:, :, :], -2 * BIG, None, ALU.is_lt))
                    src = chosen
                    for n, dst in ((1, slot), (2, biased), (4, slot), (8, biased)):
                        dve.tensor_copy(dst[:, 0:n, :], src[:, 0:n, :])
                        s.then(dve.tensor_tensor(dst[:, n:, :], src[:, n:, :], src[:, 0:NT - n, :], ALU.add))
                        src = dst
                    dve.tensor_copy(slot[:, :, :], biased[:, :, :]).then_inc(chosen_ready, 1)

                def place():
                    dve.wait_ge(count_ready, 2)
                    s.then(dve.tensor_scalar(nblk_i[:, :], gu[0:E, 2, 0:P], float(P - 1), None, ALU.add))
                    s.then(dve.tensor_scalar(nblk_i[:, :], nblk_i[:, :], 7, None, ALU.arith_shift_right))
                    dve.tensor_scalar(nblk[:, :], nblk_i[:, :], 1.0, None, ALU.max).then_inc(nblk_ready, 1)
                    dve.wait_ge(base_ready, 1)
                    dve.tensor_scalar(base[:, :], gu[:, 3, 0:E], float(P), None, ALU.mult).then_inc(base_ready, 1)
                    dve.wait_ge(table_ready, 1)
                    s.then(dve.tensor_copy(incl[:, :], gu[0:E, 3, 0:1]))
                    dve.tensor_scalar(past[:, :], num[0:E, :], incl[:, :], None, ALU.is_ge).then_inc(table_ready, 1)
                    dve.wait_ge(erow_ready, 1)
                    s.then(dve.tensor_scalar(erow[:, 0, :], gu[0:1, 3, 0:TAB], E - 1.0, None, ALU.min))
                    s.then(dve.tensor_scalar(erow[:, 1, :], gu[0:1, 3, 0:TAB], E - 0.5, None, ALU.is_lt))
                    s.then(dve.tensor_reduce(gtot[0:1, 0:1], erow[:, 1, :], AX.X, ALU.add))
                    dve.tensor_scalar(routing.total[:, :], gtot[0:1, 0:1], -float(E), None, ALU.add)
                    dve.tensor_copy(routing.table[:, 0, :], erow[:, 0, :])
                    s.then(dve.tensor_tensor(erow[:, 1, 1:], erow[:, 0, 1:], erow[:, 0, 0:TAB - 1], ALU.subtract))
                    s.then(dve.memset(erow[:, 1, 0:1], 1.0))
                    s.then(dve.tensor_scalar(erow[:, 0, :], erow[:, 0, :], E - 1.5, None, ALU.is_lt))
                    s.then(dve.tensor_tensor(erow[:, 1, :], erow[:, 1, :], erow[:, 0, :], ALU.mult))
                    dve.tensor_copy(routing.table[:, 1, :], erow[:, 1, :]).then_inc(erow_ready, 1)
                    dve.tensor_tensor(slot[:, :, :], rk, base[:, :].unsqueeze(1).to_broadcast([P, NT, E]), ALU.add)\
                        .then_inc(slot_ready, 1)
                    dve.wait_ge(slot_ready, 1)

                def send(g):
                    ts = slice(J * g, J * g + J)
                    full = [P, J, TOPK, E]
                    s.then(dve.tensor_tensor(one_hot[:, :, :, :], idxf[:, ts, :].unsqueeze(3).to_broadcast(full),
                                             num[:, 0:E].unsqueeze(1).unsqueeze(1).to_broadcast(full), ALU.is_equal))
                    for src, dst in ((slot, slot8), (scores, gate8)):
                        s.then(dve.tensor_tensor(picked[:, :, :, :], one_hot[:, :, :, :],
                                                 src[:, ts, :].unsqueeze(2).to_broadcast(full), ALU.mult))
                        s.then(dve.tensor_reduce(dst[:, ts, :], picked[:, :, :, :], AX.X, ALU.add))
                    s.then(dve.tensor_reduce(gtot[:, ts], gate8[:, ts, :], AX.X, ALU.add))
                    s.then(dve.reciprocal(gtot[:, ts], gtot[:, ts]))
                    s.then(dve.tensor_scalar(gtot[:, ts], gtot[:, ts], ROUTED_SCALE, None, ALU.mult))
                    dve.tensor_copy(slot8_i[:, ts, :], slot8[:, ts, :])
                    dve.tensor_copy(pairs[:, ts, :, 0], tok_i[:, ts].unsqueeze(2).to_broadcast([P, J, TOPK]))
                    dve.tensor_tensor(pairs[:, ts, :, 1], gate8[:, ts, :],
                                      gtot[:, ts].unsqueeze(2).to_broadcast([P, J, TOPK]), ALU.mult)\
                        .then_inc(pairs_ready, 1)

                dve.memset(empty[:, :, 1], 0.0)
                dve.wait_ge(consts, 1)
                s.then(dve.tensor_copy(num[:, :], num_i[:, :]))
                dve.tensor_scalar(empty[:, :, 0], num[0:HALF, 0:P], float(T), None, ALU.add).then_inc(empty_ready, 1)
                dve.wait_ge(consts, 9)
                pick()
                s.then(dve.tensor_copy(idxf[:, :, :], idx8[:, :, :]))
                sp_w.cut(dve)
                cut(0)
                place()
                for g in range(NG):
                    send(g)
                before = s.n
                silu(0, s)
                with dve.Fori(0, NG - 1) as g:
                    cut(g + 1)
                    residual(g)
                    silu(g + 1, Steps(dve, link, g + before + 1))
                residual(NG - 1)
                dve.wait_ge(slots_t, 1)
                for a in range(2):
                    dve.tensor_copy(routing.rows[:, a, :], gu[:, 2 * a, 0:HALF])
                    dve.tensor_copy(routing.gates[:, a, :], gu[:, 2 * a + 1, 0:HALF])


def stage_experts(nc, ident, x_dram, acc_dram, exp_gate, exp_up, exp_down, routing):
    HC = HID // P
    GU = 2 * HID
    with Stage(nc, "exp") as st:
        raw_gu = st.sb("raw_gu", [P, 2, 2, KC, HID])
        raw_dn = st.sb("raw_dn", [P, 2, HC, D])
        gu_hi, gu_lo = st.sb("gu_hi", [P, 2, KC, GU], F32R), st.sb("gu_lo", [P, 2, KC, GU], F32R)
        dn_hi, dn_lo = st.sb("dn_hi", [P, 2, HC, D], F32R), st.sb("dn_lo", [P, 2, HC, D], F32R)
        xg = st.sb("xg", [P, 2, D])
        xt_hi, xt_lo = st.sb("xt_hi", [P, 2, KC, P], F32R), st.sb("xt_lo", [P, 2, KC, P], F32R)
        sig = st.sb("sig", [P, HID])
        h = st.sb("h", [P, HID])
        ht_hi, ht_lo = st.sb("ht_hi", [P, HC, P], F32R), st.sb("ht_lo", [P, HC, P], F32R)
        out = st.sb("out", [P, 2, D])
        get_rows, put_rows = st.sb("get_rows", [P, 2], I32), st.sb("put_rows", [P, 2], I32)
        gate = st.sb("gate_tile", [P, 1])
        gate_clear = st.sem("gate_clear")
        tp = st.ps("tp", [P, KC, P])
        gu = st.ps("gu", [P, GU])
        ht = st.ps("ht", [P, HC, P])
        y = st.ps("y", [P, D])
        gu_loaded, dn_loaded = st.sem("gu_loaded"), st.sem("dn_loaded")
        gu_hi_cut, gu_cut, dn_hi_cut, dn_cut = (st.sem(n) for n in ("gu_hi_cut", "gu_cut", "dn_hi_cut", "dn_cut"))
        get_copied, put_copied = st.sem("get_copied"), st.sem("put_copied")
        gathered = [st.sem("gathered0"), st.sem("gathered1")]
        tp_ready, x_hi_ready, x_ready, gu_ready = (st.sem(n) for n in ("tp_ready", "x_hi_ready", "x_ready", "gu_ready"))
        sig_ready, silu_ready, h_ready = (st.sem(n) for n in ("sig_ready", "silu_ready", "h_ready"))
        ht_ready, ht_hi_ready, ht_cut = (st.sem(n) for n in ("ht_ready", "ht_hi_ready", "ht_cut"))
        y_ready, out_ready, out_used, added = (st.sem(n) for n in ("y_ready", "out_ready", "out_used", "added"))
        rows = routing.rows[:, :, :].rearrange("p a q -> p (a q)")
        gates = routing.gates[:, :, :].rearrange("p a q -> p (a q)")

        def expert_of(eng, b):
            return eng.value_load(routing.table[0:1, 0, ds(b, 1)], min_val=0, max_val=E - 1)

        def first_of(eng, b):
            return eng.value_load(routing.table[0:1, 1, ds(b, 1)], min_val=0, max_val=1)

        def blocks(eng, body):
            more = eng.value_load(routing.total[0:1, 0:1], min_val=0, max_val=NBLK - E)
            body(0, 0, 0)
            body(1, 1, 0)
            with eng.Fori(1, NBLK // 2) as i:
                with eng.If(2 * i < more + E):
                    for u in range(2):
                        body(2 * i + u, u, i)
                eng.nop()
            return (more + 1) // 2 * 2 + E

        with nc.Block() as block:
            @block.sync
            def _(sp):
                lead(sp, gu_loaded, by=32)
                lead(sp, dn_loaded, by=16)
                with sp.Fori(0, E // 2) as i:
                    for u in range(2):
                        e = 2 * i + u
                        sp.wait_ge(gu_cut, done(e - 2, 2))
                        sp.wait_ge(gu_loaded, done(e - 1, 32))
                        for n, dram in enumerate((exp_gate, exp_up)):
                            sp.dma_start(raw_gu[:, u, n, :, :],
                                         dram[ds(e, 1), :, :].rearrange("a (p k) n -> p (a k) n", k=KC))\
                                .then_inc(gu_loaded, 16)
                        sp.wait_ge(dn_loaded, done(e - 1, 16))
                        sp.wait_ge(dn_cut, done(e - 2))
                        sp.dma_start(raw_dn[:, u, :, :],
                                     exp_down[ds(e, 1), :, :].rearrange("a (p c) n -> p (a c) n", c=HC))\
                            .then_inc(dn_loaded, 16)

            def slot(s):
                return ds(s, 1) if type(s) is not int else slice(s, s + 1)

            def by_chunk(tile, s, part):
                half = tile[:, slot(s), part * KC // 2:(part + 1) * KC // 2, :]
                return half.rearrange("p a k (m n) -> p (a m) k n", m=2)

            def raw_chunk(s, part):
                return raw_gu[:, slot(s), :, part * KC // 2:(part + 1) * KC // 2, :].rearrange("p a m k n -> p (a m) k n")

            def cut(e, part):
                return done(e, 2) - (1 - part)

            @block.tensor
            def _(pe):
                lead(pe, tp_ready, gu_ready, ht_ready, y_ready)

                def transposes(b, u, n):
                    pe.wait_ge(gathered[u], 16 * n)
                    pe.wait_ge(x_ready, done(b - 1))
                    for k in range(KC):
                        last = pe.transpose(tp[:, k, :], xg[:, u, k::KC], ident[:, :])
                    last.then_inc(tp_ready, 1)

                def up(b, u):
                    e = expert_of(pe, b)
                    pe.wait_ge(gu_cut, cut(e, 0))
                    pe.wait_ge(x_ready, done(b))
                    pe.wait_ge(h_ready, done(b - 1))
                    s = e % 2
                    w_hi = [gu_hi[:, slot(s), k, :] for k in range(KC)]
                    w_lo = [gu_lo[:, slot(s), k, :] for k in range(KC)]
                    for k in range(KC):
                        if k == KC // 2:
                            pe.wait_ge(gu_cut, cut(e, 1))
                        last = product(pe, gu[:, :], xt_hi[:, u, k, :], xt_lo[:, u, k, :], w_hi[k], w_lo[k],
                                       k == 0, k == KC - 1)
                    last.then_inc(gu_ready, 1)

                def turn(b):
                    pe.wait_ge(h_ready, done(b))
                    pe.wait_ge(ht_cut, done(b - 1))
                    for c in range(HC):
                        last = pe.transpose(ht[:, c, :], h[:, c::HC], ident[:, :])
                    last.then_inc(ht_ready, 1)

                def down(b):
                    e = expert_of(pe, b)
                    pe.wait_ge(dn_cut, done(e))
                    pe.wait_ge(ht_cut, done(b))
                    pe.wait_ge(out_ready, done(b - 1))
                    s = e % 2
                    for c in range(HC):
                        for n in range(2):
                            cols = slice(n * 512, (n + 1) * 512)
                            last = product(pe, y[:, cols], ht_hi[:, c, :], ht_lo[:, c, :], dn_hi[:, slot(s), c, cols],
                                           dn_lo[:, slot(s), c, cols], c == 0, c == HC - 1)
                    last.then_inc(y_ready, 1)

                def body(b, u, i):
                    up(b, u)
                    transposes(b + 1, 1 - u, i + 1 + u)
                    if type(b) is not int or b:
                        down(b - 1)
                    turn(b)

                transposes(0, 0, 1)
                count = blocks(pe, body)
                down(count - 1)

            @block.scalar
            def _(act):
                lead(act, gu_hi_cut, by=2)
                lead(act, dn_hi_cut, x_hi_ready, sig_ready, ht_hi_ready, out_ready)

                def cut_gu(e, s, b, part):
                    act.wait_ge(gu_loaded, done(e, 32))
                    act.wait_ge(gu_ready, done(b - 1))
                    act.activation(by_chunk(gu_hi, s, part), raw_chunk(s, part), ACT.Copy).then_inc(gu_hi_cut, 1)

                def cut_dn(e, s, b):
                    act.wait_ge(dn_loaded, done(e, 16))
                    act.wait_ge(y_ready, done(b - 1))
                    act.activation(dn_hi[:, slot(s), :, :], raw_dn[:, slot(s), :, :], ACT.Copy).then_inc(dn_hi_cut, 1)

                def cut_x(b, u):
                    act.wait_ge(tp_ready, done(b))
                    act.wait_ge(gu_ready, done(b - 2))
                    act.activation(xt_hi[:, u, :, :], tp[:, :, :], ACT.Copy).then_inc(x_hi_ready, 1)

                def cut_ht(b):
                    act.wait_ge(ht_ready, done(b))
                    act.wait_ge(y_ready, done(b - 1))
                    act.activation(ht_hi[:, :, :], ht[:, :, :], ACT.Copy).then_inc(ht_hi_ready, 1)

                def output(b, u):
                    act.wait_ge(y_ready, done(b))
                    act.wait_ge(out_used, done(b - 2))
                    act.activation(out[:, u, :], y[:, :], ACT.Copy, scale=gates[:, ds(b, 1)]).then_inc(out_ready, 1)

                def body(b, u, i):
                    started = type(b) is not int or b
                    if started:
                        cut_ht(b - 1)
                    if type(b) is not int or b > 1:
                        output(b - 2, u)
                    if started:
                        e, first = expert_of(act, b - 1), first_of(act, b - 1)
                        with act.If(first > 0):
                            cut_dn(e + 1, (e + 1) % 2, b - 1)
                    e, first = expert_of(act, b), first_of(act, b)
                    with act.If(first > 0):
                        cut_gu(e + 1, (e + 1) % 2, b, 0)
                    act.wait_ge(gu_ready, done(b))
                    act.wait_ge(h_ready, done(b - 1))
                    act.activation(sig[:, :], gu[:, 0:HID], ACT.Sigmoid).then_inc(sig_ready, 1)
                    cut_x(b + 1, 1 - u)
                    with act.If(first > 0):
                        cut_gu(e + 1, (e + 1) % 2, b, 1)
                    act.nop()

                cut_x(0, 0)
                cut_gu(0, 0, 0, 0)
                cut_gu(0, 0, 0, 1)
                cut_dn(0, 0, 0)
                count = blocks(act, body)
                cut_ht(count - 1)
                output(count - 2, 0)
                output(count - 1, 1)

            @block.vector
            def _(dve):
                lead(dve, gu_cut, by=2)
                lead(dve, dn_cut, x_ready, silu_ready, h_ready, ht_cut)

                def cut_gu(e, s, part):
                    dve.wait_ge(gu_hi_cut, cut(e, part))
                    dve.tensor_tensor(by_chunk(gu_lo, s, part), raw_chunk(s, part), f32(by_chunk(gu_hi, s, part)),
                                      ALU.subtract).then_inc(gu_cut, 1)

                def cut_dn(e, s):
                    dve.wait_ge(dn_hi_cut, done(e))
                    dve.tensor_tensor(dn_lo[:, slot(s), :, :], raw_dn[:, slot(s), :, :], f32(dn_hi[:, slot(s), :, :]),
                                      ALU.subtract).then_inc(dn_cut, 1)

                def cut_x(b, u):
                    dve.wait_ge(x_hi_ready, done(b))
                    dve.tensor_tensor(xt_lo[:, u, :, :], tp[:, :, :], f32(xt_hi[:, u, :, :]), ALU.subtract)\
                        .then_inc(x_ready, 1)

                def cut_ht(b):
                    dve.wait_ge(ht_hi_ready, done(b))
                    dve.tensor_tensor(ht_lo[:, :, :], ht[:, :, :], f32(ht_hi[:, :, :]), ALU.subtract).then_inc(ht_cut, 1)

                def body(b, u, i):
                    if type(b) is not int or b:
                        cut_ht(b - 1)
                        e, first = expert_of(dve, b - 1), first_of(dve, b - 1)
                        with dve.If(first > 0):
                            cut_dn(e + 1, (e + 1) % 2)
                    e, first = expert_of(dve, b), first_of(dve, b)
                    with dve.If(first > 0):
                        cut_gu(e + 1, (e + 1) % 2, 0)
                    dve.wait_ge(sig_ready, done(b))
                    dve.tensor_tensor(sig[:, :], sig[:, :], gu[:, 0:HID], ALU.mult).then_inc(silu_ready, 1)
                    dve.wait_ge(silu_ready, done(b))
                    dve.wait_ge(ht_ready, done(b - 1))
                    dve.tensor_tensor(h[:, :], sig[:, :], gu[:, HID:], ALU.mult).then_inc(h_ready, 1)
                    cut_x(b + 1, 1 - u)
                    with dve.If(first > 0):
                        cut_gu(e + 1, (e + 1) % 2, 1)
                    dve.nop()

                cut_x(0, 0)
                cut_gu(0, 0, 0)
                cut_gu(0, 0, 1)
                cut_dn(0, 0)
                count = blocks(dve, body)
                cut_ht(count - 1)

            @block.gpsimd
            def _(pool):
                lead(pool, out_used, get_copied, put_copied)

                def gather(b, u):
                    pool.wait_ge(tp_ready, done(b - 2))
                    pool.tensor_copy(get_rows[:, u:u + 1], rows[:, ds(b, 1)]).then_inc(get_copied, 1)
                    pool.wait_ge(get_copied, done(b))
                    pool.tensor_tensor(gate[:, :], gate[:, :], gate[:, :], ALU.mult)
                    pool.indirect_dma_start(xg[:, u, :], None, x_dram,
                                            bass.IndirectOffsetOnAxis(ap=get_rows[:, u:u + 1], axis=0))\
                        .then_inc(gathered[u], 16)

                def add(b, u):
                    pool.tensor_copy(put_rows[:, u:u + 1], rows[:, ds(b, 1)]).then_inc(put_copied, 1)
                    pool.wait_ge(put_copied, done(b))
                    pool.wait_ge(out_ready, done(b))
                    pool.tensor_tensor(gate[:, :], gate[:, :], gate[:, :], ALU.mult)
                    pool.indirect_dma_start(acc_dram, bass.IndirectOffsetOnAxis(ap=put_rows[:, u:u + 1], axis=0),
                                            out[:, u, :], None, compute_op=ALU.add).then_inc(added, 16)
                    pool.wait_ge(added, 16 * (b + 1))
                    pool.sem_inc(out_used, 1)

                def body(b, u, i):
                    gather(b + 2, u)
                    if type(b) is not int or b > 1:
                        add(b - 2, u)

                pool.memset(gate[:, :], 0.0).then_inc(gate_clear, 1)
                pool.wait_ge(gate_clear, 1)
                gather(0, 0)
                gather(1, 1)
                count = blocks(pool, body)
                add(count - 2, 0)
                add(count - 1, 1)
                for u in range(2):
                    pool.wait_ge(gathered[u], (count // 2 + 1) * 16)


def stage_final_norm(nc, acc_dram, ln_g, ln_b, out_dram):
    with Stage(nc, "fin") as st:
        norm = Norm(st, ln_g, ln_b)
        y_loaded = [st.sem("y_loaded0"), st.sem("y_loaded1")]
        link = st.sem("link")
        LN = 3
        with nc.Block() as block:
            @block.sync
            def _(sp):
                lead(sp, *y_loaded, by=8)
                norm.load(sp)
                with sp.Fori(0, NT // 2) as i:
                    for u in range(2):
                        t = 2 * i + u
                        sp.wait_ge(norm.shifted, done(t - 2))
                        sp.dma_start(norm.y[:, u, :], acc_dram[ds(t * P, P), :]).then_inc(y_loaded[u], 16)

            @block.vector
            def _(dve):
                norm.leads(dve=dve)
                dve.wait_ge(norm.loaded, 32)

                def stats(t, i, u, s):
                    dve.wait_ge(y_loaded[u], loaded(i))
                    norm.vector_stats(dve, s, u)

                def finish(t, u, s):
                    norm.vector_map(dve, s, t, u)
                    norm.vector_gain(dve, t, u)

                with dve.Fori(0, NT // 2) as i:
                    s = Steps(dve, link, LN * 2 * i)
                    for u in range(2):
                        stats(2 * i + u, i, u, s)
                    for u in range(2):
                        finish(2 * i + u, u, s)

            @block.scalar
            def _(act):
                norm.leads(act=act)
                with act.Fori(0, NT // 2) as i:
                    for u in range(2):
                        norm.scalar_root(act, 2 * i + u, u)
                    for u in range(2):
                        norm.scalar_norm(act, 2 * i + u, u)

            @block.gpsimd
            def _(pool):
                norm.leads(pool=pool)
                for u in range(2):
                    norm.pool_shift(pool, u, 0, u, out_dram)
                with pool.Fori(1, NT // 2) as i:
                    for u in range(2):
                        norm.pool_shift(pool, 2 * i + u, i, u, out_dram)
                norm.all_stored(pool)


def block_kernel(nc, x, mem, w_in, pool_w, pool_scale, w_out, ln1_g, ln1_b, w_cq, w_ck, w_cv, w_co, ln2_g, ln2_b,
                 w_router, router_bias, exp_gate, exp_up, exp_down, sh_gate, sh_up, sh_down, ln3_g, ln3_b, out):
    def dram(name, *shape):
        return nc.dram_tensor(name, shape, F32).ap()

    v, qt, kt = dram("v", T, AW), dram("qt", PAIRS, P, T), dram("kt", PAIRS, P, T)
    mix_hi, mix_lo = dram("mix_hi", PW // P, P, T), dram("mix_lo", PW // P, P, T)
    o = [dram(f"o{b}", T, AW) for b in range(len(PATTERNS))]
    stats = [dram(f"stats{b}", T, 2 * HEADS) for b in range(len(PATTERNS))]
    x1, x2, acc = dram("x1", T, D), dram("x2", ROWS, D), dram("acc", ROWS, D)
    slots = dram("slots", TAB * P, 2)
    with Stage(nc, "all") as st:
        ident = st.sb("ident", [P, P])
        make_identity(nc, ident)
        with Stage(nc, "front") as front:
            xt_hi, xt_lo = front.sb("xt_hi", [P, KC, T], F32R), front.sb("xt_lo", [P, KC, T], F32R)
            stage_transpose_and_v(nc, ident, xt_hi, xt_lo, x, w_in, v)
            stage_project_qk(nc, xt_hi, xt_lo, w_in, qt, kt)
            stage_pool(nc, xt_hi, xt_lo, w_in, pool_w, pool_scale, mix_hi, mix_lo)
        attention(nc, ident, v, qt, kt, o, stats)
        stage_mix(nc, ident, x1, x, o, stats, mix_hi, mix_lo, w_out, ln1_g, ln1_b)
        with Stage(nc, "memory") as memory:
            k_mem = memory.sb("k_mem", [P, MH, MEM])
            v_mem = memory.sb("v_mem", [P, MEM // P, MW])
            stage_memory(nc, ident, mem, w_ck, w_cv, k_mem, v_mem)
            stage_cross(nc, ident, x1, k_mem, v_mem, w_cq, w_co, ln2_g, ln2_b, x2)
        with Stage(nc, "moe") as moe:
            routing = Routing(moe)
            with Stage(nc, "scores") as st_scores:
                scores = st_scores.sb("scores", [P, NT, E])
                stage_route(nc, ident, x2, w_router, scores)
                stage_shared_and_dispatch(nc, ident, x2, acc, slots, sh_gate, sh_up, sh_down, router_bias, scores,
                                          routing)
            stage_experts(nc, ident, x2, acc, exp_gate, exp_up, exp_down, routing)
        stage_final_norm(nc, acc, ln3_g, ln3_b, out)


def kernel(**inputs):
    import concourse.bacc as bacc
    from concourse.bass_utils import run_bass_kernel_spmd

    nc = bacc.Bacc("TRN2", target_bir_lowering=False, num_devices=1)
    arrays, args = {}, {}
    for name, value in inputs.items():
        a = np.asarray(value)[0]
        if name == "pool_scale":
            a = a.reshape(len(POOL_WINDOWS), P).T
        a = np.ascontiguousarray(a)
        arrays[f"in_{name}"] = a
        args[name] = nc.dram_tensor(f"in_{name}", a.shape, mybir.dt.from_np(a.dtype), kind="ExternalInput").ap()
    args["out"] = nc.dram_tensor("out", (T, D), F32, kind="ExternalOutput").ap()
    block_kernel(nc, **args)
    result = run_bass_kernel_spmd(nc, [arrays], core_ids=[0])
    return np.asarray(result.results[0]["out"]).reshape(1, T, D)
```

```python
from contextlib import ExitStack

import concourse.bass as bass
import numpy as np
from concourse import mybir

F32 = mybir.dt.float32
F32R = mybir.dt.float32r
I32 = mybir.dt.int32
U32 = mybir.dt.uint32
ALU = mybir.AluOpType
ACT = mybir.ActivationFunctionType
AX = mybir.AxisListType

P = 128
D = 1024
T = 2048
NT = T // P
KC = D // P
HEADS, HD = 8, 64
AW = HEADS * HD
PAIRS = HEADS // 2
PATTERNS = ((128, 1), (512, 4), (2048, 16))
POOL_WINDOWS = (2, 4, 8, 16)
PADW = 16
PW = 512
MIX = AW + PW
MEM = 256
MH, MHD = 4, 128
MW = MH * MHD
E = 64
EG = 8
TOPG = 4
TOPK = 8
HID = 256
ROUTED_SCALE = 2.5
LN_EPS = 1e-5
BIG = 1e30
ALPHA = 2.0 ** 0.25
GRP = 512
NG = T // GRP
NBLK = T * TOPK // P + E
ds = bass.ds


class Stage:

    def __init__(self, nc, name):
        self.nc, self.name, self.ctx, self.sems = nc, name, ExitStack(), []

    def __enter__(self):
        return self

    def __exit__(self, *exc):
        if self.sems:
            self.nc.clear_and_free_semaphores(self.sems)
            self.nc.all_engine_barrier()
        self.ctx.close()

    def sb(self, name, shape, dt=F32):
        return self.ctx.enter_context(self.nc.sbuf_tensor(f"{self.name}_{name}", shape, dt))

    def ps(self, name, shape, dt=F32):
        return self.ctx.enter_context(self.nc.psum_tensor(f"{self.name}_{name}", shape, dt))

    def sem(self, name):
        self.sems.append(self.nc.alloc_semaphore(name=f"{self.name}_{name}"))
        return self.sems[-1]


class Steps:

    def __init__(self, eng, sem, base=0):
        self.eng, self.sem, self.base, self.n = eng, sem, base, 0

    def then(self, ins):
        ins.then_inc(self.sem, 1)
        self.n += 1
        self.eng.wait_ge(self.sem, self.base + self.n)


def product(pe, out, a_hi, a_lo, b_hi, b_lo, first, last):
    pe.matmul(out, a_hi, b_hi, start=first, stop=False)
    pe.matmul(out, a_hi, b_lo, start=False, stop=False)
    return pe.matmul(out, a_lo, b_hi, start=False, stop=last)


LEAD = 2


def lead(eng, *sems, by=1):
    for sem in sems:
        eng.sem_inc(sem, LEAD * by)


def done(t, by=1):
    return (t + 1 + LEAD) * by


def loaded(i):
    return 16 * i + 32


def f32(ap):
    return ap.bitcast(F32)


def make_identity(nc, ident):
    with Stage(nc, "const") as st:
        cleared = st.sem("cleared")
        with nc.Block() as block:
            @block.gpsimd
            def _(pool):
                pool.memset(ident[:, :], 0.0).then_inc(cleared, 1)
                pool.wait_ge(cleared, 1)
                pool.affine_select(out=ident[:, :], in_=ident[:, :], compare_op=ALU.not_equal, fill=1.0,
                                   base=0, pattern=[[-1, P]], channel_multiplier=1)


def stage_transpose_and_v(nc, ident, xt_hi, xt_lo, x, w_in, v_dram):
    with Stage(nc, "xv") as st:
        x_in = st.sb("x_in", [P, 2, D])
        w_raw = st.sb("w_raw", [P, KC, AW])
        w_hi = st.sb("w_hi", [P, KC, AW], F32R)
        w_lo = st.sb("w_lo", [P, KC, AW], F32R)
        t_hi = st.sb("t_hi", [P, 2, KC, P], F32R)
        t_lo = st.sb("t_lo", [P, 2, KC, P], F32R)
        v_out = st.sb("v_out", [P, 2, AW])
        tp = st.ps("tp", [P, 2, KC, P])
        pv = st.ps("pv", [P, 2, AW])
        w_loaded, w_hi_ready, w_lo_ready = st.sem("w_loaded"), st.sem("w_hi_ready"), st.sem("w_lo_ready")
        x_loaded = [st.sem("x_loaded0"), st.sem("x_loaded1")]
        v_stored = [st.sem("v_stored0"), st.sem("v_stored1")]
        tp_ready, hi_ready, lo_ready = st.sem("tp_ready"), st.sem("hi_ready"), st.sem("lo_ready")
        hi_kept, lo_kept = st.sem("hi_kept"), st.sem("lo_kept")
        pv_ready, v_ready = st.sem("pv_ready"), st.sem("v_ready")

        with nc.Block() as block:
            @block.sync
            def _(sp):
                for u in range(2):
                    lead(sp, x_loaded[u], by=8)
                with sp.Fori(0, NT // 2) as i:
                    for u in range(2):
                        t = 2 * i + u
                        sp.wait_ge(tp_ready, done(t - 2))
                        sp.dma_start(x_in[:, u, :], x[ds(t * P, P), :]).then_inc(x_loaded[u], 16)

            @block.gpsimd
            def _(pool):
                lead(pool, hi_kept)
                with pool.Fori(0, NT // 2) as i:
                    for u in range(2):
                        t = 2 * i + u
                        pool.wait_ge(hi_ready, done(t))
                        pool.tensor_copy(xt_hi[:, :, ds(t * P, P)], t_hi[:, u, :, :]).then_inc(hi_kept, 1)

            @block.scalar
            def _(act):
                act.dma_start(w_raw[:, :, :], w_in[:, 2 * AW:3 * AW].rearrange("(k p) n -> p k n", p=P))\
                    .then_inc(w_loaded, 16)
                lead(act, lo_kept, v_ready)
                lead(act, *v_stored, by=8)
                act.wait_ge(w_loaded, 16)
                act.activation(w_hi[:, :, :], w_raw[:, :, :], ACT.Copy).then_inc(w_hi_ready, 1)
                with act.Fori(0, NT // 2) as i:
                    for u in range(2):
                        t = 2 * i + u
                        act.wait_ge(lo_ready, done(t))
                        act.activation(xt_lo[:, :, ds(t * P, P)], t_lo[:, u, :, :], ACT.Copy).then_inc(lo_kept, 1)
                        act.wait_ge(pv_ready, done(t))
                        act.wait_ge(v_stored[u], loaded(i - 1))
                        act.activation(v_out[:, u, :], pv[:, u, :], ACT.Copy).then_inc(v_ready, 1)
                        act.wait_ge(v_ready, done(t))
                        act.dma_start(v_dram[ds(t * P, P), :], v_out[:, u, :]).then_inc(v_stored[u], 16)
                for u in range(2):
                    act.wait_ge(v_stored[u], loaded(NT // 2 - 1))

            @block.vector
            def _(dve):
                lead(dve, hi_ready, lo_ready)
                dve.wait_ge(w_hi_ready, 1)
                dve.tensor_tensor(w_lo[:, :, :], w_raw[:, :, :], f32(w_hi[:, :, :]), ALU.subtract)\
                    .then_inc(w_lo_ready, 1)
                with dve.Fori(0, NT // 2) as i:
                    for u in range(2):
                        t = 2 * i + u
                        dve.wait_ge(tp_ready, done(t))
                        dve.wait_ge(hi_kept, done(t - 2))
                        dve.wait_ge(lo_kept, done(t - 2))
                        dve.wait_ge(pv_ready, done(t - 2))
                        dve.tensor_copy(t_hi[:, u, :, :], tp[:, u, :, :]).then_inc(hi_ready, 1)
                        dve.wait_ge(hi_ready, done(t))
                        dve.tensor_tensor(t_lo[:, u, :, :], tp[:, u, :, :], f32(t_hi[:, u, :, :]), ALU.subtract)\
                            .then_inc(lo_ready, 1)

            @block.tensor
            def _(pe):
                lead(pe, tp_ready, pv_ready)

                def transposes(i, u):
                    pe.wait_ge(x_loaded[u], loaded(i))
                    pe.wait_ge(lo_ready, done(2 * i + u - 2))
                    for k in range(KC):
                        last = pe.transpose(tp[:, u, k, :], x_in[:, u, k * P:(k + 1) * P], ident[:, :])
                    last.then_inc(tp_ready, 1)

                def products(t, u):
                    pe.wait_ge(lo_ready, done(t))
                    pe.wait_ge(v_ready, done(t - 2))
                    for k in range(KC):
                        last = product(pe, pv[:, u, :], t_hi[:, u, k, :], t_lo[:, u, k, :],
                                       w_hi[:, k, :], w_lo[:, k, :], k == 0, k == KC - 1)
                    last.then_inc(pv_ready, 1)

                transposes(0, 0)
                pe.wait_ge(w_lo_ready, 1)
                with pe.Fori(0, NT // 2 - 1) as i:
                    transposes(i, 1)
                    products(2 * i, 0)
                    transposes(i + 1, 0)
                    products(2 * i + 1, 1)
                transposes(NT // 2 - 1, 1)
                products(NT - 2, 0)
                products(NT - 1, 1)


def stage_project_qk(nc, xt_hi, xt_lo, w_in, qt_dram, kt_dram):
    steps = AW // P
    with Stage(nc, "qk") as st:
        w_raw = st.sb("w_raw", [P, 2, KC, P])
        w_hi = st.sb("w_hi", [P, 2, KC, P], F32R)
        w_lo = st.sb("w_lo", [P, 2, KC, P], F32R)
        out = st.sb("out", [P, 2, NG, GRP])
        acc = st.ps("acc", [P, 2, NG, GRP])
        w_loaded = [st.sem("w_loaded0"), st.sem("w_loaded1")]
        stored = [st.sem("stored0"), st.sem("stored1")]
        hi_ready, lo_ready = st.sem("hi_ready"), st.sem("lo_ready")
        acc_ready, out_ready = st.sem("acc_ready"), st.sem("out_ready")
        with nc.Block() as block:
            @block.sync
            def _(sp):
                lead(sp, *w_loaded, by=8)
                with sp.Fori(0, steps) as i:
                    for u in range(2):
                        sp.wait_ge(lo_ready, done(2 * i + u - 2))
                        sp.dma_start(w_raw[:, u, :, :],
                                     w_in[:, ds(u * AW + i * P, P)].rearrange("(k p) n -> p k n", p=P))\
                            .then_inc(w_loaded[u], 16)

            @block.vector
            def _(dve):
                lead(dve, hi_ready, lo_ready)
                with dve.Fori(0, steps) as i:
                    for u in range(2):
                        t = 2 * i + u
                        dve.wait_ge(w_loaded[u], loaded(i))
                        dve.wait_ge(acc_ready, done(t - 2))
                        dve.tensor_copy(w_hi[:, u, :, :], w_raw[:, u, :, :]).then_inc(hi_ready, 1)
                        dve.wait_ge(hi_ready, done(t))
                        dve.tensor_tensor(w_lo[:, u, :, :], w_raw[:, u, :, :], f32(w_hi[:, u, :, :]), ALU.subtract)\
                            .then_inc(lo_ready, 1)

            @block.tensor
            def _(pe):
                lead(pe, acc_ready)
                with pe.Fori(0, steps) as i:
                    for u in range(2):
                        t = 2 * i + u
                        pe.wait_ge(lo_ready, done(t))
                        pe.wait_ge(out_ready, done(t - 2))
                        for k in range(KC):
                            for g in range(NG):
                                cols = slice(g * GRP, (g + 1) * GRP)
                                last = product(pe, acc[:, u, g, :], w_hi[:, u, k, :], w_lo[:, u, k, :],
                                               xt_hi[:, k, cols], xt_lo[:, k, cols], k == 0, k == KC - 1)
                        last.then_inc(acc_ready, 1)

            @block.scalar
            def _(act):
                lead(act, out_ready)
                lead(act, *stored, by=8)
                with act.Fori(0, steps) as i:
                    for u, (scale, dram) in enumerate(((-(HD ** -0.5), qt_dram), (1.0, kt_dram))):
                        t = 2 * i + u
                        act.wait_ge(acc_ready, done(t))
                        act.wait_ge(stored[u], loaded(i - 1))
                        act.activation(out[:, u, :, :], acc[:, u, :, :], ACT.Copy, scale=scale).then_inc(out_ready, 1)
                        act.wait_ge(out_ready, done(t))
                        act.dma_start(dram[ds(i, 1), :, :].rearrange("a p n -> p (a n)"),
                                      out[:, u, :, :].rearrange("p g n -> p (g n)")).then_inc(stored[u], 16)
                for u in range(2):
                    act.wait_ge(stored[u], loaded(steps - 1))


def stage_pool(nc, xt_hi, xt_lo, w_in, pool_w, pool_scale, mix_hi_dram, mix_lo_dram):
    groups = len(POOL_WINDOWS)
    with Stage(nc, "pool") as st:
        w_raw = st.sb("w_raw", [P, 2, KC, P])
        w_hi = st.sb("w_hi", [P, 2, KC, P], F32R)
        w_lo = st.sb("w_lo", [P, 2, KC, P], F32R)
        pw = st.sb("pw", [P, groups, P])
        sc = st.sb("sc", [P, groups])
        tok = st.sb("tok", [P, PADW + T])
        sum_a = st.sb("sum_a", [P, PADW + T])
        sum_b = st.sb("sum_b", [P, PADW + T])
        first_n = st.sb("first_n", [P, PADW], I32)
        first_inv = st.sb("first_inv", [P, PADW])
        out_hi = st.sb("out_hi", [P, T], F32R)
        out_lo = st.sb("out_lo", [P, T], F32R)
        acc = st.ps("acc", [P, 2, NG, GRP])
        w_loaded, small_loaded = st.sem("w_loaded"), st.sem("small_loaded")
        split, acc_ready, tok_ready = st.sem("split"), st.sem("acc_ready"), st.sem("tok_ready")
        pooled, mixed, hi_ready, lo_ready = st.sem("pooled"), st.sem("mixed"), st.sem("hi_ready"), st.sem("lo_ready")
        padded, step, stored = st.sem("padded"), st.sem("step"), st.sem("stored")
        with nc.Block() as block:
            @block.sync
            def _(sp):
                sp.dma_start(pw[:, :, :], pool_w.rearrange("g c d -> c g d")).then_inc(small_loaded, 16)
                sp.dma_start(sc[:, :], pool_scale).then_inc(small_loaded, 16)
                for g in range(groups):
                    if g >= 2:
                        sp.wait_ge(split, 2 * (g - 1))
                        sp.wait_ge(w_loaded, 16 * g)
                    col = 3 * AW + g * P
                    sp.dma_start(w_raw[:, g % 2, :, :], w_in[:, col:col + P].rearrange("(k p) n -> p k n", p=P))\
                        .then_inc(w_loaded, 16)
                    if g == 0:
                        sp.wait_ge(w_loaded, 16)

            @block.gpsimd
            def _(pool):
                for b in (tok, sum_a, sum_b):
                    pool.memset(b[:, 0:PADW], 0.0).then_inc(padded, 1)
                pool.iota(first_n[:, :], pattern=[[1, PADW]], base=1, channel_multiplier=0).then_inc(padded, 1)

            @block.vector
            def _(dve):
                s = Steps(dve, step)
                dve.wait_ge(padded, 4)
                s.then(dve.tensor_copy(first_inv[:, :], first_n[:, :]))
                s.then(dve.reciprocal(first_inv[:, :], first_inv[:, :]))

                def split_weights(g):
                    dve.wait_ge(w_loaded, 16 * (g + 1))
                    if g >= 2:
                        dve.wait_ge(acc_ready, g - 1)
                    dve.tensor_copy(w_hi[:, g % 2, :, :], w_raw[:, g % 2, :, :]).then_inc(split, 1)
                    dve.wait_ge(split, 2 * g + 1)
                    dve.tensor_tensor(w_lo[:, g % 2, :, :], w_raw[:, g % 2, :, :], f32(w_hi[:, g % 2, :, :]),
                                      ALU.subtract).then_inc(split, 1)

                def rest(g):
                    dve.wait_ge(hi_ready, g + 1)
                    if g >= 1:
                        dve.wait_ge(stored, 32 * g)
                    dve.scalar_tensor_tensor(out=out_lo[:, :], in0=acc[:, g % 2, :, :].rearrange("p a n -> p (a n)"),
                                             scalar=sc[:, g:g + 1], in1=f32(out_hi[:, :]),
                                             op0=ALU.mult, op1=ALU.subtract).then_inc(lo_ready, 1)

                split_weights(0)
                split_weights(1)
                for g, w in enumerate(POOL_WINDOWS):
                    dve.wait_ge(tok_ready, g + 1)
                    if g >= 1:
                        dve.wait_ge(mixed, g)
                    src, ends = tok, [sum_a, sum_b]
                    for j in range(g + 1):
                        back, dst = 2 ** j, ends[j % 2]
                        s.then(dve.tensor_tensor(dst[:, PADW:], src[:, PADW:], src[:, PADW - back:PADW + T - back],
                                                 ALU.add))
                        src = dst
                    dst = ends[(g + 1) % 2]
                    s.then(dve.scalar_tensor_tensor(out=dst[:, PADW:], in0=src[:, PADW:], scalar=1.0 / w,
                                                    in1=tok[:, PADW:], op0=ALU.mult, op1=ALU.subtract))
                    s.then(dve.tensor_tensor(src[:, PADW:PADW + w], src[:, PADW:PADW + w], first_inv[:, 0:w], ALU.mult))
                    dve.tensor_tensor(dst[:, PADW:PADW + w], src[:, PADW:PADW + w], tok[:, PADW:PADW + w],
                                      ALU.subtract).then_inc(pooled, 1)
                    if g + 2 < groups:
                        split_weights(g + 2)
                    rest(g)

            @block.tensor
            def _(pe):
                def project(g):
                    pe.wait_ge(split, 2 * g + 2)
                    if g >= 2:
                        pe.wait_ge(lo_ready, g - 1)
                    for k in range(KC):
                        for n in range(NG):
                            cols = slice(n * GRP, (n + 1) * GRP)
                            last = product(pe, acc[:, g % 2, n, :], w_hi[:, g % 2, k, :], w_lo[:, g % 2, k, :],
                                           xt_hi[:, k, cols], xt_lo[:, k, cols], k == 0, k == KC - 1)
                    last.then_inc(acc_ready, 1)

                def linear(g):
                    pe.wait_ge(pooled, g + 1)
                    src = [sum_a, sum_b][(g + 1) % 2]
                    for n in range(NG):
                        last = pe.matmul(acc[:, g % 2, n, :], pw[:, g, :],
                                         src[:, PADW + n * GRP:PADW + (n + 1) * GRP], start=True, stop=True)
                    last.then_inc(mixed, 1)

                pe.wait_ge(small_loaded, 32)
                project(0)
                for g in range(groups):
                    if g + 1 < groups:
                        project(g + 1)
                    linear(g)

            @block.scalar
            def _(act):
                act.wait_ge(padded, 4)
                act.wait_ge(small_loaded, 32)
                for g in range(groups):
                    act.wait_ge(acc_ready, g + 1)
                    if g >= 1:
                        act.wait_ge(pooled, g)
                    act.activation(tok[:, PADW:], acc[:, g % 2, :, :].rearrange("p a n -> p (a n)"), ACT.Copy)\
                        .then_inc(tok_ready, 1)
                    act.wait_ge(mixed, g + 1)
                    if g >= 1:
                        act.wait_ge(stored, 32 * g)
                    act.activation(out_hi[:, :], acc[:, g % 2, :, :].rearrange("p a n -> p (a n)"), ACT.Copy,
                                   scale=sc[:, g:g + 1]).then_inc(hi_ready, 1)
                    act.wait_ge(lo_ready, g + 1)
                    act.dma_start(mix_hi_dram[g, :, :], f32(out_hi[:, :])).then_inc(stored, 16)
                    act.dma_start(mix_lo_dram[g, :, :], f32(out_lo[:, :])).then_inc(stored, 16)
                act.wait_ge(stored, 32 * groups)


def attention(nc, ident, v_dram, qt_dram, kt_dram, o_dram, stats_dram):
    tiles = [(b, dil, m, 1 if m < dil else 2) for b, (_, dil) in enumerate(PATTERNS) for m in range(NT)]
    assert all(window // dil == P for window, dil in PATTERNS)
    branches = len(PATTERNS)
    with Stage(nc, "attn") as st:
        q_t = st.sb("q_t", [P, 2, PAIRS, T])
        k_t = st.sb("k_t", [P, PAIRS, T])
        v_dil = st.sb("v_dil", [P, 2, NT, AW])
        bias = st.sb("bias", [P, 2, HEADS, 2 * P])
        dist_i = st.sb("dist_i", [P, 2 * P], I32)
        probs = st.sb("probs", [P, 2, HEADS, 2 * P])
        stats = st.sb("stats", [P, 4, 2, HEADS])
        p_t = st.sb("p_t", [P, 2, 2, 2, P])
        o_sb = st.sb("o_sb", [P, 2, AW])
        s_ps = st.ps("s_ps", [P, PAIRS, 2, 256])
        pt_ps = st.ps("pt_ps", [P, 2, 2, 256])
        o_ps = st.ps("o_ps", [P, 2, AW])
        cleared, half_cleared = st.sem("cleared"), st.sem("half_cleared")
        group_loaded = [st.sem(f"group_loaded{n}") for n in range(NG)]
        v_loaded = {b: st.sem(f"v_loaded{b}") for b in range(1, branches)}
        dist_ready, slopes_ready, cut_ready, bias_ready = (
            st.sem(n) for n in ("dist_ready", "slopes_ready", "cut_ready", "bias_ready"))
        s_ready, sm_ready = st.sem("s_ready"), st.sem("sm_ready")
        p_ready, pt_ready, pt_copied, pair_done = (st.sem(n) for n in ("p_ready", "pt_ready", "pt_copied", "pair_done"))
        o_copied = st.sem("o_copied")
        stored = [st.sem("stored0"), st.sem("stored1")]

        def run(scores, finish, tail=None):
            for t in range(len(tiles) + 1):
                for c in range(PAIRS):
                    if t < len(tiles):
                        scores(t, c)
                    if t:
                        finish(t - 1, c)
                if t and tail is not None:
                    tail(t - 1)

        def tokens(dil, m, count=P, back=0):
            first = (m // dil) * P * dil + m % dil - back * P * dil
            return ds(first, count, dil)

        with nc.Block() as block:
            @block.gpsimd
            def _(pool):
                pool.iota(dist_i[:, :], pattern=[[-1, 2 * P]], base=P, channel_multiplier=1).then_inc(dist_ready, 1)
                pool.wait_ge(dist_ready, 1)
                pool.memset(q_t[HD:, 0, :, :], 0.0).then_inc(cleared, 1)
                pool.wait_ge(cleared, 1)
                for b in range(branches):
                    pool.wait_ge(slopes_ready, b + 1)
                    pool.affine_select(out=bias[:, b % 2, :, :], in_=bias[:, b % 2, :, :], compare_op=ALU.is_ge, fill=BIG,
                                       base=P, pattern=[[0, HEADS], [-1, 2 * P]], channel_multiplier=1)\
                        .then_inc(cut_ready, 1)
                    pool.wait_ge(cut_ready, b + 1)
                    pool.affine_select(out=bias[:, b % 2, :, :], in_=bias[:, b % 2, :, :], compare_op=ALU.is_ge, fill=BIG,
                                       base=0, pattern=[[0, HEADS], [1, 2 * P]], channel_multiplier=-1)\
                        .then_inc(bias_ready, 1)

            @block.tensor
            def _(pe):
                def scores(t, c):
                    b, dil, m, blocks = tiles[t]
                    if c == 0 and b == 0 and m % (GRP // P) == 0:
                        pe.wait_ge(group_loaded[m * P // GRP], 64)
                    if t >= 1:
                        pe.wait_ge(sm_ready, PAIRS * (t - 1) + c + 1)
                    for half in range(2):
                        last = pe.matmul(s_ps[:, c, half, 0:blocks * P], q_t[:, half, c, tokens(dil, m)],
                                         k_t[:, c, tokens(dil, m, blocks * P, blocks - 1)], start=True, stop=True)
                    last.then_inc(s_ready, 1)

                def values(t, c):
                    b, dil, m, blocks = tiles[t]
                    pe.wait_ge(pt_copied, PAIRS * t + c + 1)
                    if c == 0 and t >= 2:
                        pe.wait_ge(o_copied, t - 1)
                    if c == 0 and m == 0 and b:
                        pe.wait_ge(v_loaded[b], 16 * (NT // dil))
                    for half in range(2):
                        h = 2 * c + half
                        for k in range(blocks):
                            last = pe.matmul(o_ps[:, t % 2, h * HD:(h + 1) * HD], p_t[:, c % 2, half, k, :],
                                             v_dil[:, b % 2, m - dil * (blocks - 1 - k), h * HD:(h + 1) * HD],
                                             start=k == 0, stop=k == blocks - 1)
                    last.then_inc(pair_done, 1)

                def finish(t, c):
                    n = PAIRS * t + c
                    pe.wait_ge(p_ready, n + 1)
                    if n >= 2:
                        pe.wait_ge(pt_copied, n - 1)
                    for half in range(2):
                        for k in range(tiles[t][3]):
                            last = pe.transpose(pt_ps[:, c % 2, half, k * P:(k + 1) * P],
                                                probs[:, t % 2, 2 * c + half, k * P:(k + 1) * P], ident[:, :])
                    last.then_inc(pt_ready, 1)
                    if c:
                        values(t, c - 1)

                pe.wait_ge(cleared, 1)
                pe.wait_ge(half_cleared, 1)
                run(scores, finish, lambda t: values(t, PAIRS - 1))

            @block.vector
            def _(dve):
                def slopes(b):
                    for h in range(HEADS):
                        last = dve.tensor_scalar(bias[:, b % 2, h, :], dist_i[:, :],
                                                 PATTERNS[b][1] * 2.0 ** (-8.0 * (h + 1) / HEADS), None, ALU.mult)
                    last.then_inc(slopes_ready, 1)

                def scores(t, c):
                    b, dil, m, blocks = tiles[t]
                    dve.wait_ge(s_ready, PAIRS * t + c + 1)
                    if c == 0:
                        dve.wait_ge(bias_ready, b + 1)
                    if c == 0 and m == 0 and 2 <= b + 1 < branches:
                        slopes(b + 1)
                    if c == 0 and t >= 2:
                        dve.wait_ge(pt_ready, PAIRS * (t - 1))
                    if c == 0 and t >= 4:
                        dve.wait_ge(stored[t % 2], 32 * (t // 2 - 1))
                    for half in range(2):
                        h = 2 * c + half
                        last = dve.tensor_tensor_reduce(out=probs[:, t % 2, h, 0:blocks * P],
                                                        in0=s_ps[:, c, half, 0:blocks * P],
                                                        in1=bias[:, b % 2, h, (2 - blocks) * P:], scale=1.0, scalar=3e38,
                                                        op0=ALU.add, op1=ALU.min, accum_out=stats[:, t % 4, 0, h:h + 1])
                    last.then_inc(sm_ready, 1)

                def finish(t, c):
                    n = PAIRS * t + c
                    dve.wait_ge(pt_ready, n + 1)
                    if n >= 2:
                        dve.wait_ge(pair_done, n - 1)
                    blocks = tiles[t][3]
                    dve.tensor_copy(p_t[:, c % 2, :, 0:blocks, :],
                                    pt_ps[:, c % 2, :, 0:blocks * P].rearrange("p a (k j) -> p a k j", j=P))\
                        .then_inc(pt_copied, 1)

                dve.memset(q_t[0:HD, 1, :, :], 0.0).then_inc(half_cleared, 1)
                dve.wait_ge(dist_ready, 1)
                slopes(0)
                slopes(1)
                run(scores, finish)

            @block.scalar
            def _(act):
                def exponentials(t, c):
                    blocks = tiles[t][3]
                    act.wait_ge(sm_ready, PAIRS * t + c + 1)
                    for half in range(2):
                        h = 2 * c + half
                        row = probs[:, t % 2, h, 0:blocks * P]
                        last = act.activation(row, row, ACT.Exp, scale=-1.0, bias=stats[:, t % 4, 0, h:h + 1],
                                              accum_out=stats[:, t % 4, 1, h:h + 1])
                    last.then_inc(p_ready, 1)

                def copy_out(t):
                    act.wait_ge(pair_done, PAIRS * (t + 1))
                    if t >= 2:
                        act.wait_ge(stored[t % 2], 32 * (t // 2))
                    act.activation(o_sb[:, t % 2, :], o_ps[:, t % 2, :], ACT.Copy).then_inc(o_copied, 1)

                run(exponentials, lambda t, c: None, copy_out)

            @block.sync
            def _(sp):
                def load_v(b):
                    dil = PATTERNS[b][1]
                    source = v_dram.rearrange("(n i r) f -> i n r f", r=dil, i=P)
                    for n in range(NT // dil):
                        sp.dma_start(v_dil[:, b % 2, n * dil:(n + 1) * dil, :], source[:, n, :, :])\
                            .then_inc(v_loaded[b], 16)

                def store(t):
                    b, dil, m, _ = tiles[t]
                    sp.wait_ge(o_copied, t + 1)
                    sp.dma_start(o_dram[b][tokens(dil, m), :], o_sb[:, t % 2, :]).then_inc(stored[t % 2], 16)
                    sp.dma_start(stats_dram[b][tokens(dil, m), :], stats[:, t % 4, :, :].rearrange("p a h -> p (a h)"))\
                        .then_inc(stored[t % 2], 16)
                    if m == NT - 1 and b + 2 < branches:
                        load_v(b + 2)

                assert PATTERNS[0][1] == 1
                for n in range(NG):
                    cols, per = slice(n * GRP, (n + 1) * GRP), GRP // P
                    for half in range(2):
                        rows = slice(half * HD, (half + 1) * HD)
                        sp.dma_start(q_t[rows, half, :, cols], qt_dram[:, rows, cols].rearrange("c p n -> p c n"))\
                            .then_inc(group_loaded[n], 16)
                    sp.dma_start(k_t[:, :, cols], kt_dram[:, :, cols].rearrange("c p n -> p c n"))\
                        .then_inc(group_loaded[n], 16)
                    sp.dma_start(v_dil[:, 0, n * per:(n + 1) * per, :], v_dram[cols, :].rearrange("(a i) f -> i a f", i=P))\
                        .then_inc(group_loaded[n], 16)
                load_v(1)
                run(lambda t, c: None, lambda t, c: None, store)
                for u in range(2):
                    sp.wait_ge(stored[u], 32 * (len(tiles) // 2))


class Norm:

    def __init__(self, st, gain, shift, depth=2):
        self.depth = depth
        self.y = st.sb("y", [P, depth, D])
        self.out = st.sb("out", [P, depth, D])
        self.stored = [st.sem(f"stored{u}") for u in range(depth)]
        self.part = st.sb("bn", [P, depth, 2, 6])
        self.mv = st.sb("mv", [P, depth, 2])
        self.sd = st.sb("sd", [P, depth, 3])
        self.gate = st.sb("gate", [P, 1])
        self.gain, self.shift = st.sb("gain", [P, D]), st.sb("shift", [P, D])
        self.gain_in, self.shift_in = gain, shift
        self.loaded = st.sem("norm_loaded")
        self.var_ready, self.root_ready, self.map_ready = st.sem("var_ready"), st.sem("root_ready"), st.sem("map_ready")
        self.normed, self.gained, self.shifted = st.sem("normed"), st.sem("gained"), st.sem("shifted")

    def load(self, sp):
        sp.dma_start(self.gain[:, :], self.gain_in.partition_broadcast(P)).then_inc(self.loaded, 16)
        sp.dma_start(self.shift[:, :], self.shift_in.partition_broadcast(P)).then_inc(self.loaded, 16)

    def vector_stats(self, dve, s, u):
        for half in range(2):
            ins = dve.bn_stats(self.part[:, u, half, :], self.y[:, u, half * 512:(half + 1) * 512])
            if half:
                s.then(ins)
        dve.memset(self.gate[:, :], 0.0)
        s.then(dve.bn_aggr(self.mv[:, u, :], self.part[:, u, :, :].rearrange("p a b -> p (a b)")))
        dve.tensor_scalar(self.sd[:, u, 0:1], self.mv[:, u, 1:2], LN_EPS, None, ALU.add).then_inc(self.var_ready, 1)

    def scalar_root(self, act, t, u):
        act.wait_ge(self.var_ready, done(t))
        act.activation(self.sd[:, u, 0:1], self.sd[:, u, 0:1], ACT.Sqrt).then_inc(self.root_ready, 1)

    def vector_map(self, dve, s, t, u):
        dve.wait_ge(self.root_ready, done(t))
        s.then(dve.reciprocal(self.sd[:, u, 1:2], self.sd[:, u, 0:1]))
        dve.scalar_tensor_tensor(out=self.sd[:, u, 2:3], in0=self.mv[:, u, 0:1], scalar=-1.0,
                                 in1=self.sd[:, u, 1:2], op0=ALU.mult, op1=ALU.mult).then_inc(self.map_ready, 1)

    def scalar_norm(self, act, t, u):
        act.wait_ge(self.map_ready, done(t))
        act.activation(self.y[:, u, :], self.y[:, u, :], ACT.Identity, bias=self.sd[:, u, 2:3],
                       scale=self.sd[:, u, 1:2]).then_inc(self.normed, 1)

    def vector_gain(self, dve, t, u):
        dve.wait_ge(self.normed, done(t))
        dve.tensor_tensor(self.y[:, u, :], self.y[:, u, :], self.gain[:, :], ALU.mult).then_inc(self.gained, 1)

    def pool_shift(self, pool, t, i, u, *drams):
        pool.wait_ge(self.gained, done(t))
        if type(i) is not int or i:
            pool.wait_ge(self.stored[u], len(drams) * 16 * i)
        pool.tensor_tensor(self.out[:, u, :], self.y[:, u, :], self.shift[:, :], ALU.add).then_inc(self.shifted, 1)
        pool.wait_ge(self.shifted, done(t))
        for dram in drams:
            pool.dma_start(dram[ds(t * P, P), :], self.out[:, u, :]).then_inc(self.stored[u], 16)

    def all_stored(self, pool, drams=1):
        for u in range(self.depth):
            pool.wait_ge(self.stored[u], drams * 16 * (NT // self.depth))

    def leads(self, dve=None, act=None, pool=None):
        if dve:
            lead(dve, self.var_ready, self.map_ready, self.gained)
        if act:
            lead(act, self.root_ready, self.normed)
        if pool:
            lead(pool, self.shifted)


class Splitter:

    def __init__(self, st, width, depth=2):
        self.depth = depth
        self.raw = st.sb("w_raw", [P, depth, width])
        self.loaded = [st.sem(f"w_loaded{u}") for u in range(depth)]
        self.hi_ready, self.ready = st.sem("w_hi_ready"), st.sem("w_ready")
        self.jobs = []

    def add(self, dram, hi, lo):
        k = dram.shape[0] // P
        for j in range(k):
            self.jobs.append((dram[j * P:(j + 1) * P, :], hi[:, j, :], lo[:, j, :], dram.shape[1]))
        return len(self.jobs)

    def load(self, sp):
        for n, (src, _, _, w) in enumerate(self.jobs):
            u = n % self.depth
            if n >= self.depth:
                sp.wait_ge(self.ready, n - self.depth + 1)
            sp.dma_start(self.raw[:, u, 0:w], src).then_inc(self.loaded[u], 16)

    def cut_hi(self, act):
        for n, (_, hi, _, w) in enumerate(self.jobs):
            u = n % self.depth
            act.wait_ge(self.loaded[u], 16 * (n // self.depth + 1))
            act.activation(hi, self.raw[:, u, 0:w], ACT.Copy).then_inc(self.hi_ready, 1)

    def cut_lo(self, eng):
        for n, (_, hi, lo, w) in enumerate(self.jobs):
            eng.wait_ge(self.hi_ready, n + 1)
            eng.tensor_tensor(lo, self.raw[:, n % self.depth, 0:w], f32(hi), ALU.subtract).then_inc(self.ready, 1)


def stage_mix(nc, ident, y_dram, x, o_dram, stats_dram, mix_hi_dram, mix_lo_dram, w_out, ln_g, ln_b):
    nb = len(PATTERNS)
    with Stage(nc, "mix") as st:
        sp_w = Splitter(st, D, 4)
        w_hi = st.sb("w_hi", [P, MIX // P, D], F32R)
        w_lo = st.sb("w_lo", [P, MIX // P, D], F32R)
        sp_w.add(w_out, w_hi, w_lo)
        norm = Norm(st, ln_g, ln_b)
        o_in = st.sb("o_in", [P, 2, nb, AW])
        s_in = st.sb("s_in", [P, 2, nb, 2, HEADS])
        m_hi = st.sb("m_hi", [P, 2, PW // P, P], F32R)
        m_lo = st.sb("m_lo", [P, 2, PW // P, P], F32R)
        x_in = st.sb("x_in", [P, 2, D])
        low = st.sb("low", [P, 2, HEADS])
        wt = st.sb("wt", [P, 2, nb, HEADS])
        wl = st.sb("wl", [P, 2, nb, HEADS])
        den = st.sb("den", [P, 2, HEADS])
        a_hi = st.sb("a_hi", [P, 2, AW // P, P], F32R)
        a_lo = st.sb("a_lo", [P, 2, AW // P, P], F32R)
        tp = st.ps("tp", [P, 2, AW // P, P])
        acc = st.ps("acc", [P, 2, D])
        in_loaded = [st.sem("in_loaded0"), st.sem("in_loaded1")]
        m_loaded = [st.sem("m_loaded0"), st.sem("m_loaded1")]
        x_loaded = [st.sem("x_loaded0"), st.sem("x_loaded1")]
        link, diff_ready, weight_ready = st.sem("link"), st.sem("diff_ready"), st.sem("weight_ready")
        attn_ready, tp_ready, hi_ready = st.sem("attn_ready"), st.sem("tp_ready"), st.sem("hi_ready")
        a_ready, acc_ready, y_ready = st.sem("a_ready"), st.sem("acc_ready"), st.sem("y_ready")
        TILE = 11

        with nc.Block() as block:
            @block.sync
            def _(sp):
                lead(sp, *x_loaded, by=8)
                lead(sp, *in_loaded, by=8 * 2 * nb)
                lead(sp, *m_loaded, by=8 * 2)

                def load_attention(t, u):
                    sp.wait_ge(tp_ready, done(t - 2))
                    rows = ds(t * P, P)
                    for b in range(nb):
                        sp.dma_start(o_in[:, u, b, :], o_dram[b][rows, :]).then_inc(in_loaded[u], 16)
                    for b in range(nb):
                        sp.dma_start(s_in[:, u, b, :, :].rearrange("p a h -> p (a h)"), stats_dram[b][rows, :])\
                            .then_inc(in_loaded[u], 16)

                def load_rest(t, i, u):
                    rows = ds(t * P, P)
                    sp.wait_ge(y_ready, done(t - 2))
                    sp.dma_start(x_in[:, u, :], x[rows, :]).then_inc(x_loaded[u], 16)
                    for part, dram in ((m_hi, mix_hi_dram), (m_lo, mix_lo_dram)):
                        sp.dma_start(f32(part[:, u, :, :]), dram[:, :, rows].rearrange("g c n -> c g n"))\
                            .then_inc(m_loaded[u], 16)

                for t in range(2):
                    load_attention(t, t)
                for t in range(2):
                    load_rest(t, 0, t)
                sp_w.load(sp)
                norm.load(sp)
                load_attention(2, 0)
                with sp.Fori(1, NT // 2 - 1) as i:
                    for u in range(2):
                        load_attention(2 * i + u + 1, 1 - u)
                        load_rest(2 * i + u, i, u)
                load_attention(NT - 1, 1)
                for u in range(2):
                    load_rest(NT - 2 + u, NT // 2 - 1, u)

            @block.vector
            def _(dve):
                lead(dve, diff_ready, attn_ready, a_ready, y_ready)
                norm.leads(dve=dve)

                def merge_weights(t, i, u, s):
                    dve.wait_ge(in_loaded[u], 2 * nb * loaded(i))
                    s.then(dve.tensor_tensor(low[:, u, :], s_in[:, u, 0, 0, :], s_in[:, u, 1, 0, :], ALU.min))
                    s.then(dve.tensor_tensor(low[:, u, :], low[:, u, :], s_in[:, u, 2, 0, :], ALU.min))
                    dve.tensor_tensor(wt[:, u, :, :], low[:, u, :].unsqueeze(1).to_broadcast([P, nb, HEADS]),
                                      s_in[:, u, :, 0, :], ALU.subtract).then_inc(diff_ready, 1)

                def merge(t, u, s):
                    dve.wait_ge(weight_ready, done(t))
                    s.then(dve.tensor_tensor(wl[:, u, :, :], wt[:, u, :, :], s_in[:, u, :, 1, :], ALU.mult))
                    s.then(dve.tensor_reduce(den[:, u, :], wl[:, u, :, :].rearrange("p b h -> p h b"), AX.X, ALU.add))
                    s.then(dve.reciprocal(den[:, u, :], den[:, u, :]))
                    s.then(dve.tensor_tensor(wt[:, u, :, :], wt[:, u, :, :],
                                             den[:, u, :].unsqueeze(1).to_broadcast([P, nb, HEADS]), ALU.mult))
                    outs = o_in[:, u, :, :].rearrange("p b (h d) -> p (b h) d", d=HD)
                    s.then(dve.tensor_tensor(outs, outs, wt[:, u, :, :].rearrange("p b h -> p (b h)").unsqueeze(2)
                                             .to_broadcast([P, nb * HEADS, HD]), ALU.mult))
                    s.then(dve.tensor_tensor(o_in[:, u, 0, :], o_in[:, u, 0, :], o_in[:, u, 1, :], ALU.add))
                    dve.tensor_tensor(o_in[:, u, 0, :], o_in[:, u, 0, :], o_in[:, u, 2, :], ALU.add)\
                        .then_inc(attn_ready, 1)

                def rest(t, u):
                    dve.wait_ge(hi_ready, done(t))
                    dve.tensor_tensor(a_lo[:, u, :, :], tp[:, u, :, :], f32(a_hi[:, u, :, :]), ALU.subtract)\
                        .then_inc(a_ready, 1)

                def residual(t, i, u, s):
                    dve.wait_ge(acc_ready, done(t))
                    dve.wait_ge(x_loaded[u], loaded(i))
                    dve.wait_ge(norm.shifted, done(t - 2))
                    dve.scalar_tensor_tensor(out=norm.y[:, u, :], in0=x_in[:, u, :], scalar=ALPHA,
                                             in1=acc[:, u, :], op0=ALU.mult, op1=ALU.add).then_inc(y_ready, 1)
                    dve.wait_ge(y_ready, done(t))
                    norm.vector_stats(dve, s, u)

                def tile(t, i, u, before, first=False, last=False):
                    s = Steps(dve, link, before)
                    if not last:
                        merge_weights(t + 2, i + 1, u, s)
                    if not first:
                        norm.vector_map(dve, s, t - 1, 1 - u)
                    if not last:
                        merge(t + 2, u, s)
                    if not first:
                        norm.vector_gain(dve, t - 1, 1 - u)
                    residual(t, i, u, s)
                    if not last:
                        rest(t + 2, u)
                    return before + s.n

                s = Steps(dve, link)
                for t in range(2):
                    merge_weights(t, 0, t, s)
                    merge(t, t, s)
                    rest(t, t)
                sp_w.cut_lo(dve)
                dve.wait_ge(norm.loaded, 32)
                n = tile(0, 0, 0, s.n, first=True)
                n = tile(1, 0, 1, n)
                with dve.Fori(1, NT // 2 - 1) as i:
                    for u in range(2):
                        tile(2 * i + u, i, u, n + TILE * (2 * i + u - 2))
                n += TILE * (NT - 4)
                for u in range(2):
                    n = tile(NT - 2 + u, NT // 2 - 1, u, n, last=True)
                s = Steps(dve, link, n)
                norm.vector_map(dve, s, NT - 1, 1)
                norm.vector_gain(dve, NT - 1, 1)

            @block.scalar
            def _(act):
                lead(act, weight_ready, hi_ready)
                norm.leads(act=act)

                def weights(t, u):
                    act.wait_ge(diff_ready, done(t))
                    act.activation(wt[:, u, :, :], wt[:, u, :, :], ACT.Exp).then_inc(weight_ready, 1)

                def cut(t, u):
                    act.wait_ge(tp_ready, done(t))
                    act.wait_ge(acc_ready, done(t - 2))
                    act.activation(a_hi[:, u, :, :], tp[:, u, :, :], ACT.Copy).then_inc(hi_ready, 1)

                def tile(t, u, first=False, last=False):
                    if not last:
                        weights(t + 2, u)
                    if not first:
                        norm.scalar_norm(act, t - 1, 1 - u)
                    if not last:
                        cut(t + 2, u)
                    norm.scalar_root(act, t, u)

                weights(0, 0)
                cut(0, 0)
                weights(1, 1)
                cut(1, 1)
                sp_w.cut_hi(act)
                tile(0, 0, first=True)
                tile(1, 1)
                with act.Fori(1, NT // 2 - 1) as i:
                    for u in range(2):
                        tile(2 * i + u, u)
                for u in range(2):
                    tile(NT - 2 + u, u, last=True)
                norm.scalar_norm(act, NT - 1, 1)

            @block.tensor
            def _(pe):
                lead(pe, tp_ready, acc_ready)

                def transposes(t, u):
                    pe.wait_ge(attn_ready, done(t))
                    pe.wait_ge(a_ready, done(t - 2))
                    for c in range(AW // P):
                        last = pe.transpose(tp[:, u, c, :], o_in[:, u, 0, c * P:(c + 1) * P], ident[:, :])
                    last.then_inc(tp_ready, 1)

                def products(t, i, u, first=False):
                    pe.wait_ge(a_ready, done(t))
                    pe.wait_ge(m_loaded[u], 2 * loaded(i))
                    pe.wait_ge(y_ready, done(t - 2))
                    parts = [(a_hi[:, u, c, :], a_lo[:, u, c, :]) for c in range(AW // P)]
                    parts += [(m_hi[:, u, c, :], m_lo[:, u, c, :]) for c in range(PW // P)]
                    for k, (hi, lo) in enumerate(parts):
                        if first:
                            pe.wait_ge(sp_w.ready, k + 1)
                        for n in range(2):
                            cols = slice(n * 512, (n + 1) * 512)
                            last = product(pe, acc[:, u, cols], hi, lo, w_hi[:, k, cols], w_lo[:, k, cols],
                                           k == 0, k == len(parts) - 1)
                    last.then_inc(acc_ready, 1)

                transposes(0, 0)
                for u in range(2):
                    transposes(u + 1, 1 - u)
                    products(u, 0, u, first=u == 0)
                with pe.Fori(1, NT // 2 - 1) as i:
                    for u in range(2):
                        transposes(2 * i + u + 1, 1 - u)
                        products(2 * i + u, i, u)
                transposes(NT - 1, 1)
                products(NT - 2, NT // 2 - 1, 0)
                products(NT - 1, NT // 2 - 1, 1)

            @block.gpsimd
            def _(pool):
                norm.leads(pool=pool)
                for u in range(2):
                    norm.pool_shift(pool, u, 0, u, y_dram)
                with pool.Fori(1, NT // 2) as i:
                    for u in range(2):
                        norm.pool_shift(pool, 2 * i + u, i, u, y_dram)
                norm.all_stored(pool)


def stage_memory(nc, ident, mem, w_ck, w_cv, k_mem, v_mem):
    blocks = MEM // P
    with Stage(nc, "mem") as st:
        m_in = st.sb("m_in", [P, blocks, D])
        m_t = st.sb("m_t", [P, KC, MEM])
        wk = st.sb("wk", [P, KC, MW])
        wv = st.sb("wv", [P, KC, MW])
        tp = st.ps("tp", [P, KC, MEM])
        kp = st.ps("kp", [P, MH, MEM])
        vp = st.ps("vp", [P, blocks, MW])
        m_loaded, w_loaded = st.sem("m_loaded"), st.sem("w_loaded")
        tp_ready, t_ready, k_ready, v_ready = (st.sem(n) for n in ("tp_ready", "t_ready", "k_ready", "v_ready"))
        with nc.Block() as block:
            @block.sync
            def _(sp):
                sp.dma_start(m_in[:, :, :], mem.rearrange("(b p) n -> p b n", p=P)).then_inc(m_loaded, 16)
                sp.dma_start(wk[:, :, :], w_ck.rearrange("(k p) n -> p k n", p=P)).then_inc(w_loaded, 16)
                sp.wait_ge(w_loaded, 16)
                sp.dma_start(wv[:, :, :], w_cv.rearrange("(k p) n -> p k n", p=P)).then_inc(w_loaded, 16)

            @block.tensor
            def _(pe):
                pe.wait_ge(m_loaded, 16)
                for b in range(blocks):
                    for k in range(KC):
                        last = pe.transpose(tp[:, k, b * P:(b + 1) * P], m_in[:, b, k * P:(k + 1) * P], ident[:, :])
                last.then_inc(tp_ready, 1)
                pe.wait_ge(t_ready, 1)
                pe.wait_ge(w_loaded, 16)
                for h in range(MH):
                    for k in range(KC):
                        last = pe.matmul(kp[:, h, :], wk[:, k, h * P:(h + 1) * P], m_t[:, k, :],
                                         start=k == 0, stop=k == KC - 1)
                last.then_inc(k_ready, 1)
                pe.wait_ge(w_loaded, 32)
                for b in range(blocks):
                    for k in range(KC):
                        last = pe.matmul(vp[:, b, :], m_t[:, k, b * P:(b + 1) * P], wv[:, k, :],
                                         start=k == 0, stop=k == KC - 1)
                last.then_inc(v_ready, 1)

            @block.vector
            def _(dve):
                dve.wait_ge(tp_ready, 1)
                dve.tensor_copy(m_t[:, :, :], tp[:, :, :]).then_inc(t_ready, 1)
                dve.wait_ge(k_ready, 1)
                dve.tensor_copy(k_mem[:, :, :], kp[:, :, :])

            @block.scalar
            def _(act):
                act.wait_ge(v_ready, 1)
                act.activation(v_mem[:, :, :], vp[:, :, :], ACT.Copy)


def stage_cross(nc, ident, x_dram, k_mem, v_mem, w_cq, w_co, ln_g, ln_b, *y_drams):
    scale = MHD ** -0.5
    mb = MEM // P
    J = GRP // P
    with Stage(nc, "cross") as st:
        sp_w = Splitter(st, D, 3)
        cq_hi, cq_lo = st.sb("cq_hi", [P, KC, MW], F32R), st.sb("cq_lo", [P, KC, MW], F32R)
        co_hi, co_lo = st.sb("co_hi", [P, MH, D], F32R), st.sb("co_lo", [P, MH, D], F32R)
        sp_w.add(w_cq, cq_hi, cq_lo)
        co_cut = sp_w.add(w_co, co_hi, co_lo)
        norm = Norm(st, ln_g, ln_b)
        xa = st.sb("xa", [P, 2, D])
        xr = st.sb("xr", [P, 2, D])
        xg_hi, xg_lo = st.sb("xg_hi", [P, KC, GRP], F32R), st.sb("xg_lo", [P, KC, GRP], F32R)
        q_t = st.sb("q_t", [P, MH, GRP])
        probs = st.sb("probs", [P, MH, MEM])
        p_t = st.sb("p_t", [P, MH, mb, GRP])
        o_hi, o_lo = st.sb("o_hi", [P, MH, GRP], F32R), st.sb("o_lo", [P, MH, GRP], F32R)
        top, nlow, tot, inv = (st.sb(n, [P, 2, MH]) for n in ("top", "nlow", "tot", "inv"))
        tp = st.ps("tp", [P, KC, P])
        s_ps = st.ps("s_ps", [P, MH, MEM])
        qd = st.ps("qd", [P, 2, GRP])
        acc = st.ps("acc", [P, D])
        a_loaded = [st.sem("a_loaded0"), st.sem("a_loaded1")]
        r_loaded = [st.sem("r_loaded0"), st.sem("r_loaded1")]
        ta_ready, ta_hi, ta_lo = st.sem("ta_ready"), st.sem("ta_hi"), st.sem("ta_lo")
        q_acc, q_copied = st.sem("q_acc"), st.sem("q_copied")
        s_ready, top_ready, low_ready, e_ready, p_ready = (
            st.sem(n) for n in ("s_ready", "top_ready", "low_ready", "e_ready", "p_ready"))
        pt_ready, pt_copied = st.sem("pt_ready"), st.sem("pt_copied")
        d_ready, d_hi, d_lo = st.sem("d_ready"), st.sem("d_hi"), st.sem("d_lo")
        acc_ready, y_ready, link = st.sem("acc_ready"), st.sem("y_ready"), st.sem("link")

        with nc.Block() as block:
            @block.sync
            def _(sp):
                lead(sp, *a_loaded, *r_loaded, by=8)
                norm.load(sp)

                def load_a(t, i, u):
                    sp.wait_ge(ta_ready, done(t - 2))
                    sp.dma_start(xa[:, u, :], x_dram[ds(t * P, P), :]).then_inc(a_loaded[u], 16)

                def load_r(t, i, u):
                    sp.wait_ge(y_ready, done(t - 2))
                    sp.dma_start(xr[:, u, :], x_dram[ds(t * P, P), :]).then_inc(r_loaded[u], 16)

                for t in range(J):
                    load_a(t, t // 2, t % 2)
                sp_w.load(sp)
                for t in range(J, 2 * J):
                    load_a(t, t // 2, t % 2)
                for t in range(2):
                    load_r(t, 0, t)
                with sp.Fori(0, (NT - 2 * J) // 2) as i:
                    for u in range(2):
                        load_a(2 * i + u + 2 * J, i + J, u)
                        load_r(2 * i + u + 2, i + 1, u)
                for t in range(NT - 2 * J + 2, NT):
                    load_r(t, t // 2, t % 2)

            def groups(eng, tile, group):
                def one(g, first=False, last=False, end=False):
                    for j in range(J):
                        tile(g, j, first, last, end)
                    if not end:
                        group(g, last)

                one(0, first=True)
                for g in range(1, NG - 1):
                    one(g)
                one(NG - 1, last=True)
                one(NG, end=True)

            @block.tensor
            def _(pe):
                lead(pe, ta_ready, q_acc, s_ready, pt_ready, d_ready, acc_ready)

                def transpose_x(t, i, u):
                    pe.wait_ge(a_loaded[u], loaded(i))
                    for k in range(KC):
                        last = pe.transpose(tp[:, k, :], xa[:, u, k * P:(k + 1) * P], ident[:, :])
                    last.then_inc(ta_ready, 1)

                def queries(g):
                    pe.wait_ge(ta_lo, done(J * g + J - 1))
                    for h in range(MH):
                        if h < 2:
                            if type(g) is not int or g:
                                pe.wait_ge(d_lo, done(MH * (g - 1) + h + 2))
                        else:
                            pe.wait_ge(q_copied, done(MH * g + h - 2))
                        for k in range(KC):
                            if type(g) is int and g == 0 and h == 0:
                                pe.wait_ge(sp_w.ready, k + 1)
                            last = product(pe, qd[:, h % 2, :], cq_hi[:, k, h * P:(h + 1) * P],
                                           cq_lo[:, k, h * P:(h + 1) * P], xg_hi[:, k, :], xg_lo[:, k, :],
                                           k == 0, k == KC - 1)
                        last.then_inc(q_acc, 1)

                def tile(g, j, first, last, end):
                    t = J * g + j
                    if not end:
                        pe.wait_ge(q_copied, done(MH * g + MH - 1))
                        pe.wait_ge(e_ready, done(t - 1))
                        for h in range(MH):
                            ins = pe.matmul(s_ps[:, h, :], q_t[:, h, j * P:(j + 1) * P], k_mem[:, h, :],
                                            start=True, stop=True)
                        ins.then_inc(s_ready, 1)
                    if j and not last and not end:
                        pe.wait_ge(pt_copied, done(t - 1))
                        transpose_x(t + J - 1, (J // 2) * (g + 1) + (j - 1) // 2, (j - 1) % 2)
                    if not first:
                        pe.wait_ge(d_lo, done(MH * (g - 1) + MH - 1))
                        pe.wait_ge(y_ready, done(t - J - 1))
                        for h in range(MH):
                            for n in range(2):
                                cols = slice(n * 512, (n + 1) * 512)
                                ins = product(pe, acc[:, cols], o_hi[:, h, j * P:(j + 1) * P],
                                              o_lo[:, h, j * P:(j + 1) * P], co_hi[:, h, cols], co_lo[:, h, cols],
                                              h == 0, h == MH - 1)
                        ins.then_inc(acc_ready, 1)
                    if not end:
                        pe.wait_ge(p_ready, done(t))
                        if last:
                            pe.wait_ge(pt_copied, done(t - 1))
                        else:
                            pe.wait_ge(ta_lo, done(t + J - 1))
                        for h in range(MH):
                            for b in range(mb):
                                ins = pe.transpose(tp[:, 2 * h + b, :], probs[:, h, b * P:(b + 1) * P], ident[:, :])
                        ins.then_inc(pt_ready, 1)

                def group(g, last):
                    pe.wait_ge(pt_copied, done(J * g + J - 1))
                    if not last:
                        transpose_x(J * g + 2 * J - 1, (J // 2) * (g + 1) + J // 2 - 1, 1)
                    for h in range(MH):
                        if h < 2:
                            pe.wait_ge(q_copied, done(MH * g + h + 2))
                        else:
                            pe.wait_ge(d_lo, done(MH * g + h - 2))
                        for b in range(mb):
                            ins = pe.matmul(qd[:, h % 2, :], v_mem[:, b, h * P:(h + 1) * P], p_t[:, h, b, :],
                                            start=b == 0, stop=b == mb - 1)
                        ins.then_inc(d_ready, 1)
                    if not last:
                        queries(g + 1)

                for t in range(J):
                    if t:
                        pe.wait_ge(ta_lo, done(t - 1))
                    transpose_x(t, t // 2, t % 2)
                queries(0)
                pe.wait_ge(sp_w.ready, co_cut)
                groups(pe, tile, group)

            @block.vector
            def _(dve):
                lead(dve, ta_lo, top_ready, low_ready, p_ready, d_lo, y_ready)
                norm.leads(dve=dve)
                dve.wait_ge(norm.loaded, 32)
                s = Steps(dve, link)

                def cut_x(t, col):
                    dve.wait_ge(ta_hi, done(t))
                    dve.tensor_tensor(xg_lo[:, :, col:col + P], tp[:, :, :], f32(xg_hi[:, :, col:col + P]),
                                      ALU.subtract).then_inc(ta_lo, 1)

                def tile(g, j, first, last, end):
                    t = J * g + j
                    u = j % 2
                    e = t - J
                    if not end:
                        dve.wait_ge(s_ready, done(t))
                        dve.wait_ge(e_ready, done(t - 2))
                        dve.tensor_reduce(top[:, u, :], s_ps[:, :, :], AX.X, ALU.max).then_inc(top_ready, 1)
                        dve.wait_ge(top_ready, done(t))
                        dve.tensor_scalar(nlow[:, u, :], top[:, u, :], -scale, None, ALU.mult).then_inc(low_ready, 1)
                    if e >= 1:
                        norm.vector_map(dve, s, e - 1, 1 - u)
                    if not end:
                        dve.wait_ge(e_ready, done(t))
                        s.then(dve.reciprocal(inv[:, u, :], tot[:, u, :]))
                        dve.tensor_tensor(probs[:, :, :], probs[:, :, :],
                                          inv[:, u, :].unsqueeze(2).to_broadcast([P, MH, MEM]), ALU.mult)\
                            .then_inc(p_ready, 1)
                    if j and not last and not end:
                        cut_x(t + J - 1, (j - 1) * P)
                    if e >= 1:
                        norm.vector_gain(dve, e - 1, 1 - u)
                    if e >= 0:
                        dve.wait_ge(acc_ready, done(e))
                        dve.wait_ge(r_loaded[u], loaded((J // 2) * (g - 1) + j // 2))
                        dve.wait_ge(norm.shifted, done(e - 2))
                        dve.scalar_tensor_tensor(out=norm.y[:, u, :], in0=xr[:, u, :], scalar=ALPHA,
                                                 in1=acc[:, :], op0=ALU.mult, op1=ALU.add).then_inc(y_ready, 1)
                    if e >= 0:
                        dve.wait_ge(y_ready, done(e))
                        norm.vector_stats(dve, s, u)

                def group(g, last):
                    if not last:
                        cut_x(J * g + 2 * J - 1, (J - 1) * P)
                    for h in range(MH):
                        dve.wait_ge(d_hi, done(MH * g + h))
                        dve.tensor_tensor(o_lo[:, h, :], qd[:, h % 2, :], f32(o_hi[:, h, :]), ALU.subtract)\
                            .then_inc(d_lo, 1)

                for t in range(J):
                    cut_x(t, t * P)
                sp_w.cut_lo(dve)
                groups(dve, tile, group)
                norm.vector_map(dve, s, NT - 1, 1)
                norm.vector_gain(dve, NT - 1, 1)

            @block.scalar
            def _(act):
                lead(act, ta_hi, q_copied, e_ready, pt_copied, d_hi)
                norm.leads(act=act)

                def cut_x(t, col):
                    act.wait_ge(ta_ready, done(t))
                    act.activation(xg_hi[:, :, col:col + P], tp[:, :, :], ACT.Copy).then_inc(ta_hi, 1)

                def copy_queries(g):
                    for h in range(MH):
                        act.wait_ge(q_acc, done(MH * g + h))
                        act.activation(q_t[:, h, :], qd[:, h % 2, :], ACT.Copy).then_inc(q_copied, 1)

                def tile(g, j, first, last, end):
                    t = J * g + j
                    u = j % 2
                    if not end:
                        act.wait_ge(low_ready, done(t))
                        act.wait_ge(pt_ready, done(t - 1))
                        act.wait_ge(p_ready, done(t - 2))
                        for h in range(MH):
                            ins = act.activation(probs[:, h, :], s_ps[:, h, :], ACT.Exp, scale=scale,
                                                 bias=nlow[:, u, h:h + 1], accum_out=tot[:, u, h:h + 1])
                        ins.then_inc(e_ready, 1)
                    if j and not last and not end:
                        cut_x(t + J - 1, (j - 1) * P)
                    if t > J:
                        norm.scalar_norm(act, t - J - 1, 1 - u)
                    if not end:
                        act.wait_ge(pt_ready, done(t))
                        act.activation(p_t[:, :, :, j * P:(j + 1) * P],
                                       tp[:, :, :].rearrange("p (h b) n -> p h b n", b=mb), ACT.Copy)\
                            .then_inc(pt_copied, 1)
                    if t >= J:
                        norm.scalar_root(act, t - J, u)

                def group(g, last):
                    if not last:
                        cut_x(J * g + 2 * J - 1, (J - 1) * P)
                    for h in range(MH):
                        act.wait_ge(d_ready, done(MH * g + h))
                        act.activation(o_hi[:, h, :], qd[:, h % 2, :], ACT.Copy).then_inc(d_hi, 1)
                    if not last:
                        copy_queries(g + 1)

                for t in range(J):
                    cut_x(t, t * P)
                sp_w.cut_hi(act)
                copy_queries(0)
                groups(act, tile, group)
                norm.scalar_norm(act, NT - 1, 1)

            @block.gpsimd
            def _(pool):
                norm.leads(pool=pool)
                for u in range(2):
                    norm.pool_shift(pool, u, 0, u, *y_drams)
                with pool.Fori(1, NT // 2) as i:
                    for u in range(2):
                        norm.pool_shift(pool, 2 * i + u, i, u, *y_drams)
                norm.all_stored(pool, len(y_drams))


TAB = NBLK + 4
HALF = TAB // 2
ROWS = T + P


def stage_route(nc, ident, x_dram, w_router, scores):
    J = GRP // P
    with Stage(nc, "route") as st:
        w_raw = st.sb("w_raw", [P, KC, E])
        w_hi, w_lo = st.sb("w_hi", [P, KC, P], F32R), st.sb("w_lo", [P, KC, P], F32R)
        xa = st.sb("xa", [P, 2, D])
        xg_hi, xg_lo = st.sb("xg_hi", [P, 2, KC, GRP], F32R), st.sb("xg_lo", [P, 2, KC, GRP], F32R)
        lg_t = st.sb("lg_t", [E, 2, GRP])
        tp = st.ps("tp", [P, 2, KC, P])
        lg = st.ps("lg", [P, 2, GRP])
        tb = st.ps("tb", [P, 2, 512])
        w_loaded, w_cut, cleared = st.sem("w_loaded"), st.sem("w_cut"), st.sem("cleared")
        a_loaded = [st.sem("a_loaded0"), st.sem("a_loaded1")]
        ta_ready, ta_hi, ta_lo = st.sem("ta_ready"), st.sem("ta_hi"), st.sem("ta_lo")
        lg_ready, lg_copied, tb_ready, s_ready = (st.sem(n) for n in ("lg_ready", "lg_copied", "tb_ready", "s_ready"))
        with nc.Block() as block:
            @block.gpsimd
            def _(pool):
                pool.memset(f32(w_hi[:, :, :]), 0.0).then_inc(cleared, 1)
                pool.memset(f32(w_lo[:, :, :]), 0.0).then_inc(cleared, 1)

            @block.sync
            def _(sp):
                sp.dma_start(w_raw[:, :, :], w_router.rearrange("(k p) n -> p k n", p=P)).then_inc(w_loaded, 16)
                for t in range(NT):
                    if t >= 2:
                        sp.wait_ge(ta_ready, t - 1)
                    sp.dma_start(xa[:, t % 2, :], x_dram[t * P:(t + 1) * P, :]).then_inc(a_loaded[t % 2], 16)

            @block.tensor
            def _(pe):
                def transposes(g):
                    for t in range(J * g, J * g + J):
                        pe.wait_ge(a_loaded[t % 2], 16 * (t // 2 + 1))
                        if t >= 2:
                            pe.wait_ge(ta_lo, t - 1)
                        for k in range(KC):
                            last = pe.transpose(tp[:, t % 2, k, :], xa[:, t % 2, k * P:(k + 1) * P], ident[:, :])
                        last.then_inc(ta_ready, 1)

                def logits(g):
                    pe.wait_ge(ta_lo, J * (g + 1))
                    if g >= 2:
                        pe.wait_ge(lg_copied, g - 1)
                    for k in range(KC):
                        last = product(pe, lg[:, g % 2, :], w_hi[:, k, :], w_lo[:, k, :], xg_hi[:, g % 2, k, :],
                                       xg_lo[:, g % 2, k, :], k == 0, k == KC - 1)
                    last.then_inc(lg_ready, 1)

                def back(g):
                    pe.wait_ge(lg_copied, g + 1)
                    if g >= 2:
                        pe.wait_ge(s_ready, g - 1)
                    for j in range(J):
                        last = pe.transpose(tb[:, g % 2, j * E:(j + 1) * E], lg_t[:, g % 2, j * P:(j + 1) * P],
                                            ident[0:E, 0:E])
                    last.then_inc(tb_ready, 1)

                transposes(0)
                pe.wait_ge(w_cut, 2)
                for g in range(NG):
                    if g + 1 < NG:
                        transposes(g + 1)
                    logits(g)
                    back(g)

            @block.vector
            def _(dve):
                dve.wait_ge(w_loaded, 16)
                dve.wait_ge(cleared, 2)
                dve.tensor_copy(w_hi[:, :, 0:E], w_raw[:, :, :]).then_inc(w_cut, 1)
                dve.wait_ge(w_cut, 1)
                dve.tensor_tensor(w_lo[:, :, 0:E], w_raw[:, :, :], f32(w_hi[:, :, 0:E]), ALU.subtract).then_inc(w_cut, 1)
                for t in range(NT):
                    g, cols = t // J, slice(t % J * P, (t % J + 1) * P)
                    dve.wait_ge(ta_hi, t + 1)
                    dve.tensor_tensor(xg_lo[:, g % 2, :, cols], tp[:, t % 2, :, :], f32(xg_hi[:, g % 2, :, cols]),
                                      ALU.subtract).then_inc(ta_lo, 1)

            @block.scalar
            def _(act):
                def finish(g):
                    act.wait_ge(lg_ready, g + 1)
                    act.activation(lg_t[:, g % 2, :], lg[0:E, g % 2, :], ACT.Copy).then_inc(lg_copied, 1)
                    act.wait_ge(tb_ready, g + 1)
                    act.activation(scores[:, J * g:J * (g + 1), :].rearrange("p t e -> p (t e)"),
                                   tb[:, g % 2, 0:J * E], ACT.Sigmoid).then_inc(s_ready, 1)

                for t in range(NT):
                    g, cols = t // J, slice(t % J * P, (t % J + 1) * P)
                    act.wait_ge(ta_ready, t + 1)
                    if g >= 2 and t % J == 0:
                        act.wait_ge(lg_ready, g - 1)
                    act.activation(xg_hi[:, g % 2, :, cols], tp[:, t % 2, :, :], ACT.Copy).then_inc(ta_hi, 1)
                    if t % J == J - 1 and g:
                        finish(g - 1)
                finish(NG - 1)


class Routing:

    def __init__(self, st):
        self.rows = st.sb("rows", [P, 2, HALF], I32)
        self.gates = st.sb("gates", [P, 2, HALF])
        self.table = st.sb("table", [1, 2, TAB], I32)
        self.total = st.sb("total", [1, 1], I32)


def stage_shared_and_dispatch(nc, ident, x_dram, acc_dram, slots_dram, sh_gate, sh_up, sh_down, bias_in, scores,
                              routing):
    J = GRP // P
    HC = HID // P
    with Stage(nc, "shared") as st:
        sp_w = Splitter(st, D, 6)
        gu_hi, gu_lo = st.sb("gu_hi", [P, KC, 2 * HID], F32R), st.sb("gu_lo", [P, KC, 2 * HID], F32R)
        dn_hi, dn_lo = st.sb("dn_hi", [P, HC, D], F32R), st.sb("dn_lo", [P, HC, D], F32R)
        sp_w.add(sh_gate, gu_hi[:, :, 0:HID], gu_lo[:, :, 0:HID])
        gu_cut = sp_w.add(sh_up, gu_hi[:, :, HID:], gu_lo[:, :, HID:])
        dn_cut = sp_w.add(sh_down, dn_hi, dn_lo)
        xa = st.sb("xa", [P, 2, D])
        xr = st.sb("xr", [P, 2, D])
        out = st.sb("out", [P, 2, D])
        xg_hi, xg_lo = st.sb("xg_hi", [P, KC, GRP], F32R), st.sb("xg_lo", [P, KC, GRP], F32R)
        sg = st.sb("sg", [P, HC, GRP])
        h_hi, h_lo = st.sb("h_hi", [P, HC, GRP], F32R), st.sb("h_lo", [P, HC, GRP], F32R)
        bias = st.sb("bias", [P, E])
        upper = st.sb("upper", [P, P])
        upper_i = st.sb("upper_i", [E, E])
        ones = st.sb("ones", [P, P])
        low8 = st.sb("low8", [P, EG, EG])
        num_i = st.sb("num_i", [P, TAB], I32)
        num = st.sb("num", [P, TAB])
        tok_i = st.sb("tok_i", [P, NT], I32)
        biased = st.sb("biased", [P, NT, E])
        top8 = st.sb("top8", [P, NT * EG, 8])
        gsum = st.sb("gsum", [P, NT, EG])
        beats = st.sb("beats", [P, NT, EG, EG])
        ties = top8[:, :, :].rearrange("p (t g) m -> p t g m", g=EG)
        grank = st.sb("grank", [P, NT, EG])
        val8 = st.sb("val8", [P, NT, TOPK])
        idx8 = st.sb("idx8", [P, NT, TOPK], U32)
        idxf = st.sb("idxf", [P, NT, TOPK])
        chosen = st.sb("chosen", [P, NT, E])
        slot = st.sb("slot", [P, NT, E])
        one_hot = st.sb("one_hot", [P, J, TOPK, E])
        picked = st.sb("picked", [P, J, TOPK, E])
        slot8 = st.sb("slot8", [P, NT, TOPK])
        slot8_i = st.sb("slot8_i", [P, NT, TOPK], I32)
        gate8 = st.sb("gate8", [P, NT, TOPK])
        gtot = st.sb("gtot", [P, NT])
        pairs = st.sb("pairs", [P, NT, TOPK, 2])
        empty = st.sb("empty", [HALF, P, 2])
        nblk_i = st.sb("nblk_i", [E, P], I32)
        nblk = st.sb("nblk", [E, P])
        base = st.sb("base", [P, E])
        incl = st.sb("incl", [E, 1])
        past = st.sb("past", [E, TAB])
        erow = st.sb("erow", [1, 2, TAB])
        slots_in = st.sb("slots_in", [HALF, 2, P, 2])
        tp = st.ps("tp", [P, KC, P])
        gu = st.ps("gu", [P, 2 * HC, GRP])
        acc = st.ps("acc", [P, D])
        (a_loaded0, a_loaded1, r_loaded0, r_loaded1, ta_ready, ta_hi, ta_lo, gu_ready, sg_ready, hh_ready, h_ready,
         acc_ready, out_ready, stored0, stored1, link) = (st.sem(n) for n in (
             "a_loaded0", "a_loaded1", "r_loaded0", "r_loaded1", "ta_ready", "ta_hi", "ta_lo", "gu_ready",
             "sg_ready", "hh_ready", "h_ready", "acc_ready", "out_ready", "stored0", "stored1", "link"))
        a_loaded, r_loaded, stored = [a_loaded0, a_loaded1], [r_loaded0, r_loaded1], [stored0, stored1]
        (consts, bias_loaded, chosen_ready, count_ready, nblk_ready, base_ready, slot_ready, table_ready, erow_ready,
         empty_ready, inited, pairs_ready, scattered, slots_loaded, slots_t, z_ready) = (st.sem(n) for n in (
             "consts", "bias_loaded", "chosen_ready", "count_ready", "nblk_ready", "base_ready", "slot_ready",
             "table_ready", "erow_ready", "empty_ready", "inited", "pairs_ready", "scattered", "slots_loaded",
             "slots_t", "z_ready"))
        h_product, z_stored = st.sem("h_product"), st.sem("z_stored")
        zero = st.sb("zero", [P, D])
        rk = tp[:, :, :].rearrange("p k n -> p (k n)").rearrange("p (t e) -> p t e", e=E)
        counts, sums = acc[:, 0:P], acc[:, 512:512 + TAB]
        slots_v = slots_dram.rearrange("(a q p) c -> q a p c", a=2, p=P)

        with nc.Block() as block:
            @block.gpsimd
            def _(pool):
                pool.iota(num_i[:, :], pattern=[[1, TAB]], base=0, channel_multiplier=0).then_inc(consts, 1)
                pool.iota(tok_i[:, :], pattern=[[P, NT]], base=0, channel_multiplier=1).then_inc(consts, 1)
                pool.memset(zero[:, :], 0.0).then_inc(z_ready, 1)
                pool.memset(ones[:, :], 1.0).then_inc(consts, 1)
                pool.memset(upper[:, :], 1.0).then_inc(consts, 1)
                pool.memset(upper_i[:, :], 1.0).then_inc(consts, 1)
                pool.memset(low8[:, :, :], 1.0).then_inc(consts, 1)
                pool.wait_ge(consts, 6)
                pool.affine_select(out=upper[:, :], in_=upper[:, :], compare_op=ALU.is_gt, fill=0.0, base=0,
                                   pattern=[[1, P]], channel_multiplier=-1).then_inc(consts, 1)
                pool.affine_select(out=upper_i[:, :], in_=upper_i[:, :], compare_op=ALU.is_ge, fill=0.0, base=0,
                                   pattern=[[1, E]], channel_multiplier=-1).then_inc(consts, 1)
                pool.affine_select(out=low8[:, :, :], in_=low8[:, :, :], compare_op=ALU.is_gt, fill=0.0, base=0,
                                   pattern=[[1, EG], [-1, EG]], channel_multiplier=0).then_inc(consts, 1)
                sp_w.cut_lo(pool)
                pool.wait_ge(inited, 32)
                n = 0
                for g in range(NG):
                    pool.wait_ge(pairs_ready, g + 1)
                    for t in range(J * g, J * g + J):
                        for k in range(TOPK):
                            pool.indirect_dma_start(slots_dram, bass.IndirectOffsetOnAxis(ap=slot8_i[:, t, k:k + 1], axis=0),
                                                    pairs[:, t, k, :], None).then_inc(scattered, 16)
                            n += 16
                pool.wait_ge(scattered, n)

            @block.sync
            def _(sp):
                lead(sp, *a_loaded, *r_loaded, *stored, by=8)
                sp.dma_start(bias[:, :], bias_in.partition_broadcast(P)).then_inc(bias_loaded, 16)

                def load_a(t, i, u):
                    sp.wait_ge(ta_ready, done(t - 2))
                    sp.dma_start(xa[:, u, :], x_dram[ds(t * P, P), :]).then_inc(a_loaded[u], 16)

                def load_r(t, i, u):
                    sp.wait_ge(out_ready, done(t - 2))
                    sp.dma_start(xr[:, u, :], x_dram[ds(t * P, P), :]).then_inc(r_loaded[u], 16)

                def store(t, u):
                    sp.wait_ge(out_ready, done(t))
                    sp.dma_start(acc_dram[ds(t * P, P), :], out[:, u, :]).then_inc(stored[u], 16)

                load_a(0, 0, 0)
                load_a(1, 0, 1)
                load_a(2, 1, 0)
                load_a(3, 1, 1)
                sp.wait_ge(empty_ready, 1)
                for a in range(2):
                    sp.dma_start(slots_v[:, a, :, :], empty[:, :, :]).then_inc(inited, 16)
                sp.wait_ge(z_ready, 1)
                for dram in (x_dram, acc_dram):
                    sp.dma_start(dram[T:ROWS, :], zero[:, :]).then_inc(z_stored, 16)
                sp_w.load(sp)
                for t in (J, J + 1):
                    load_a(t, t // 2, t % 2)
                for t in range(2):
                    load_r(t, 0, t)
                with sp.Fori(0, (NT - J - 2) // 2) as i:
                    for u in range(2):
                        load_a(2 * i + u + J + 2, i + J // 2 + 1, u)
                        load_r(2 * i + u + 2, i + 1, u)
                        store(2 * i + u, u)
                for t in range(NT - J - 2, NT):
                    if t + 2 < NT:
                        load_r(t + 2, t // 2 + 1, t % 2)
                    store(t, t % 2)
                sp.wait_ge(z_stored, 32)
                for u in range(2):
                    sp.wait_ge(stored[u], loaded(NT // 2 - 1))
                sp.wait_ge(scattered, 16 * NT * TOPK)
                sp.dma_start(slots_in[:, :, :, :], slots_v).then_inc(slots_loaded, 16)

            @block.tensor
            def _(pe):
                lead(pe, ta_ready, gu_ready, acc_ready)

                def transposes(g, j):
                    pe.wait_ge(a_loaded[j % 2], loaded(g * (J // 2) + j // 2))
                    pe.wait_ge(ta_lo, done(J * g + j - 1))
                    for k in range(KC):
                        last = pe.transpose(tp[:, k, :], xa[:, j % 2, k * P:(k + 1) * P], ident[:, :])
                    last.then_inc(ta_ready, 1)

                def up(g):
                    pe.wait_ge(ta_lo, done(J * g + J - 1))
                    pe.wait_ge(h_ready, done(g - 1))
                    for c in range(2 * HC):
                        for k in range(KC):
                            last = product(pe, gu[:, c, :], gu_hi[:, k, c * P:(c + 1) * P], gu_lo[:, k, c * P:(c + 1) * P],
                                           xg_hi[:, k, :], xg_lo[:, k, :], k == 0, k == KC - 1)
                    last.then_inc(gu_ready, 1)

                def down(g, j):
                    if j == 0:
                        pe.wait_ge(h_ready, done(g))
                    pe.wait_ge(out_ready, done(J * g + j - 1))
                    for c in range(HC):
                        for n in range(2):
                            cols, rows = slice(n * 512, (n + 1) * 512), slice(j * P, (j + 1) * P)
                            last = product(pe, acc[:, cols], h_hi[:, c, rows], h_lo[:, c, rows],
                                           dn_hi[:, c, cols], dn_lo[:, c, cols], c == 0, c == HC - 1)
                    last.then_inc(acc_ready, 1)

                for j in range(J):
                    transposes(0, j)
                pe.wait_ge(sp_w.ready, gu_cut)
                up(0)
                pe.wait_ge(consts, 9)
                pe.wait_ge(chosen_ready, 1)
                for t in range(NT):
                    last = pe.matmul(rk[:, t, :], upper[:, :], chosen[:, t, :], start=True, stop=t == 0)
                    if t:
                        last = pe.matmul(rk[:, t, :], ones[:, :], slot[:, t - 1, :], start=False, stop=True)
                last.then_inc(count_ready, 1)
                pe.matmul(counts[0:E, :], slot[:, NT - 1, :], ones[:, :], start=True, stop=True).then_inc(count_ready, 1)
                pe.wait_ge(nblk_ready, 1)
                pe.matmul(sums[:, 0:E], nblk[:, :], upper[0:E, 0:E], start=True, stop=True).then_inc(base_ready, 1)
                pe.wait_ge(base_ready, 2)
                pe.matmul(sums[0:E, 0:P], upper_i[:, :], nblk[:, :], start=True, stop=True).then_inc(table_ready, 1)
                pe.wait_ge(table_ready, 2)
                pe.matmul(sums[0:32, :], ones[0:E, 0:32], past[:, :], start=True, stop=True).then_inc(erow_ready, 1)
                pe.wait_ge(erow_ready, 2)
                pe.wait_ge(slot_ready, 1)
                pe.wait_ge(sp_w.ready, dn_cut)
                with pe.Fori(0, NG - 1) as g:
                    for j in range(J):
                        transposes(g + 1, j)
                        down(g, j)
                    up(g + 1)
                for j in range(J):
                    down(NG - 1, j)
                pe.wait_ge(slots_loaded, 16)
                pe.wait_ge(h_ready, done(NG - 1))
                for a in range(2):
                    for c in range(2):
                        last = pe.transpose(gu[:, 2 * a + c, 0:HALF], slots_in[:, a, :, c], ident[0:HALF, 0:HALF])
                last.then_inc(slots_t, 1)

            @block.scalar
            def _(act):
                lead(act, ta_hi, sg_ready, hh_ready)

                def cut(g):
                    act.wait_ge(gu_ready, done(g - 1))
                    for j in range(J):
                        act.wait_ge(ta_ready, done(J * g + j))
                        act.activation(xg_hi[:, :, j * P:(j + 1) * P], tp[:, :, :], ACT.Copy).then_inc(ta_hi, 1)

                def silu(g):
                    act.wait_ge(gu_ready, done(g))
                    act.wait_ge(hh_ready, done(g - 1))
                    act.activation(sg[:, :, :], gu[:, 0:HC, :], ACT.Sigmoid).then_inc(sg_ready, 1)
                    act.wait_ge(h_product, done(g))
                    act.wait_ge(acc_ready, done(J * g - 1))
                    act.activation(h_hi[:, :, :], sg[:, :, :], ACT.Copy).then_inc(hh_ready, 1)

                cut(0)
                sp_w.cut_hi(act)
                silu(0)
                with act.Fori(1, NG) as g:
                    cut(g)
                    silu(g)

            @block.vector
            def _(dve):
                lead(dve, ta_lo, h_product, h_ready, out_ready)
                s = Steps(dve, link)

                def cut(g, j):
                    dve.wait_ge(ta_hi, done(J * g + j))
                    dve.tensor_tensor(xg_lo[:, :, j * P:(j + 1) * P], tp[:, :, :],
                                      f32(xg_hi[:, :, j * P:(j + 1) * P]), ALU.subtract).then_inc(ta_lo, 1)

                def silu(g, s):
                    dve.wait_ge(sg_ready, done(g))
                    s.then(dve.tensor_tensor(sg[:, :, :], sg[:, :, :], gu[:, 0:HC, :], ALU.mult))
                    dve.tensor_tensor(sg[:, :, :], sg[:, :, :], gu[:, HC:2 * HC, :], ALU.mult).then_inc(h_product, 1)
                    dve.wait_ge(hh_ready, done(g))
                    dve.tensor_tensor(h_lo[:, :, :], sg[:, :, :], f32(h_hi[:, :, :]), ALU.subtract).then_inc(h_ready, 1)

                def residual(g, j):
                    t, i, u = J * g + j, g * (J // 2) + j // 2, j % 2
                    dve.wait_ge(acc_ready, done(t))
                    dve.wait_ge(r_loaded[u], loaded(i))
                    dve.wait_ge(stored[u], loaded(i - 1))
                    dve.scalar_tensor_tensor(out=out[:, u, :], in0=xr[:, u, :], scalar=ALPHA, in1=acc[:, :],
                                             op0=ALU.mult, op1=ALU.add).then_inc(out_ready, 1)

                def wide(ap, n):
                    return ap.unsqueeze(3).to_broadcast([P, NT, EG, n])

                def pick():
                    dve.wait_ge(bias_loaded, 16)
                    s.then(dve.tensor_tensor(biased[:, :, :], scores[:, :, :],
                                             bias[:, :].unsqueeze(1).to_broadcast([P, NT, E]), ALU.add))
                    for t in range(NT):
                        for g in range(EG):
                            last = dve.max(top8[:, t * EG + g, :], biased[:, t, g * EG:(g + 1) * EG])
                    s.then(last)
                    best = top8[:, :, :].rearrange("p (t g) m -> p t g m", g=EG)
                    s.then(dve.tensor_tensor(gsum[:, :, :], best[:, :, :, 0], best[:, :, :, 1], ALU.add))
                    other = gsum[:, :, :].unsqueeze(2).to_broadcast([P, NT, EG, EG])
                    own = wide(gsum[:, :, :], EG)
                    dve.tensor_tensor(beats[:, :, :, :], other, own, ALU.is_gt)
                    s.then(dve.tensor_tensor(ties, other, own, ALU.is_equal))
                    s.then(dve.tensor_tensor(ties, ties, low8[:, :, :].unsqueeze(1).to_broadcast([P, NT, EG, EG]), ALU.mult))
                    s.then(dve.tensor_tensor(beats[:, :, :, :], beats[:, :, :, :], ties, ALU.add))
                    s.then(dve.tensor_reduce(grank[:, :, :], beats[:, :, :, :], AX.X, ALU.add))
                    s.then(dve.tensor_scalar(grank[:, :, :], grank[:, :, :], TOPG - 0.5, None, ALU.is_lt))
                    by_group = biased[:, :, :].rearrange("p t (g m) -> p t g m", g=EG)
                    s.then(dve.tensor_tensor(by_group, by_group, wide(grank[:, :, :], E // EG), ALU.mult))
                    s.then(dve.tensor_scalar(grank[:, :, :], grank[:, :, :], -1.0, BIG, ALU.add, ALU.mult))
                    s.then(dve.tensor_tensor(by_group, by_group, wide(grank[:, :, :], E // EG), ALU.add))
                    for t in range(NT):
                        last = dve.max(val8[:, t, :], biased[:, t, :])
                    s.then(last)
                    for t in range(NT):
                        dve.max_index(idx8[:, t, :], val8[:, t, :], biased[:, t, :])
                        last = dve.match_replace(chosen[:, t, :], val8[:, t, :], biased[:, t, :], -3 * BIG)
                    s.then(last)
                    s.then(dve.tensor_scalar(chosen[:, :, :], chosen[:, :, :], -2 * BIG, None, ALU.is_lt))
                    src = chosen
                    for n, dst in ((1, slot), (2, biased), (4, slot), (8, biased)):
                        dve.tensor_copy(dst[:, 0:n, :], src[:, 0:n, :])
                        s.then(dve.tensor_tensor(dst[:, n:, :], src[:, n:, :], src[:, 0:NT - n, :], ALU.add))
                        src = dst
                    dve.tensor_copy(slot[:, :, :], biased[:, :, :]).then_inc(chosen_ready, 1)

                def place():
                    dve.wait_ge(count_ready, 2)
                    s.then(dve.tensor_scalar(nblk_i[:, :], counts[0:E, :], float(P - 1), None, ALU.add))
                    s.then(dve.tensor_scalar(nblk_i[:, :], nblk_i[:, :], 7, None, ALU.arith_shift_right))
                    dve.tensor_scalar(nblk[:, :], nblk_i[:, :], 1.0, None, ALU.max).then_inc(nblk_ready, 1)
                    dve.wait_ge(base_ready, 1)
                    dve.tensor_scalar(base[:, :], sums[:, 0:E], float(P), None, ALU.mult).then_inc(base_ready, 1)
                    dve.wait_ge(table_ready, 1)
                    s.then(dve.tensor_copy(incl[:, :], sums[0:E, 0:1]))
                    dve.tensor_scalar(past[:, :], num[0:E, :], incl[:, :], None, ALU.is_ge).then_inc(table_ready, 1)
                    dve.wait_ge(erow_ready, 1)
                    s.then(dve.tensor_scalar(erow[:, 0, :], sums[0:1, :], E - 1.0, None, ALU.min))
                    s.then(dve.tensor_scalar(erow[:, 1, :], sums[0:1, :], E - 0.5, None, ALU.is_lt))
                    s.then(dve.tensor_reduce(gtot[0:1, 0:1], erow[:, 1, :], AX.X, ALU.add))
                    dve.tensor_scalar(routing.total[:, :], gtot[0:1, 0:1], -float(E), None, ALU.add)
                    dve.tensor_copy(routing.table[:, 0, :], erow[:, 0, :])
                    s.then(dve.tensor_tensor(erow[:, 1, 1:], erow[:, 0, 1:], erow[:, 0, 0:TAB - 1], ALU.subtract))
                    s.then(dve.memset(erow[:, 1, 0:1], 1.0))
                    s.then(dve.tensor_scalar(erow[:, 0, :], erow[:, 0, :], E - 1.5, None, ALU.is_lt))
                    s.then(dve.tensor_tensor(erow[:, 1, :], erow[:, 1, :], erow[:, 0, :], ALU.mult))
                    dve.tensor_copy(routing.table[:, 1, :], erow[:, 1, :]).then_inc(erow_ready, 1)
                    dve.tensor_tensor(slot[:, :, :], rk, base[:, :].unsqueeze(1).to_broadcast([P, NT, E]), ALU.add)\
                        .then_inc(slot_ready, 1)
                    dve.wait_ge(slot_ready, 1)

                def send(g):
                    ts = slice(J * g, J * g + J)
                    full = [P, J, TOPK, E]
                    s.then(dve.tensor_tensor(one_hot[:, :, :, :], idxf[:, ts, :].unsqueeze(3).to_broadcast(full),
                                             num[:, 0:E].unsqueeze(1).unsqueeze(1).to_broadcast(full), ALU.is_equal))
                    for src, dst in ((slot, slot8), (scores, gate8)):
                        s.then(dve.tensor_tensor(picked[:, :, :, :], one_hot[:, :, :, :],
                                                 src[:, ts, :].unsqueeze(2).to_broadcast(full), ALU.mult))
                        s.then(dve.tensor_reduce(dst[:, ts, :], picked[:, :, :, :], AX.X, ALU.add))
                    s.then(dve.tensor_reduce(gtot[:, ts], gate8[:, ts, :], AX.X, ALU.add))
                    s.then(dve.reciprocal(gtot[:, ts], gtot[:, ts]))
                    s.then(dve.tensor_scalar(gtot[:, ts], gtot[:, ts], ROUTED_SCALE, None, ALU.mult))
                    dve.tensor_copy(slot8_i[:, ts, :], slot8[:, ts, :])
                    dve.tensor_copy(pairs[:, ts, :, 0], tok_i[:, ts].unsqueeze(2).to_broadcast([P, J, TOPK]))
                    dve.tensor_tensor(pairs[:, ts, :, 1], gate8[:, ts, :],
                                      gtot[:, ts].unsqueeze(2).to_broadcast([P, J, TOPK]), ALU.mult)\
                        .then_inc(pairs_ready, 1)

                dve.memset(empty[:, :, 1], 0.0)
                dve.wait_ge(consts, 1)
                s.then(dve.tensor_copy(num[:, :], num_i[:, :]))
                dve.tensor_scalar(empty[:, :, 0], num[0:HALF, 0:P], float(T), None, ALU.add).then_inc(empty_ready, 1)
                dve.wait_ge(consts, 9)
                for j in range(J):
                    cut(0, j)
                pick()
                s.then(dve.tensor_copy(idxf[:, :, :], idx8[:, :, :]))
                place()
                sends = {0: (0,), 1: (1, 2), 2: (3,)}
                for g in range(NG):
                    for n in sends.get(g, ()):
                        send(n)
                    silu(g, s)
                    for j in range(J):
                        if g + 1 < NG:
                            cut(g + 1, j)
                        residual(g, j)
                dve.wait_ge(slots_t, 1)
                for a in range(2):
                    dve.tensor_copy(routing.rows[:, a, :], gu[:, 2 * a, 0:HALF])
                    dve.tensor_copy(routing.gates[:, a, :], gu[:, 2 * a + 1, 0:HALF])


def stage_experts(nc, ident, x_dram, acc_dram, exp_gate, exp_up, exp_down, routing):
    HC = HID // P
    GU = 2 * HID
    UNROLL = 4
    assert E % UNROLL == 0 and NBLK % UNROLL == 0
    with Stage(nc, "exp") as st:
        raw_gu = st.sb("raw_gu", [P, 2, 2, KC, HID])
        raw_dn = st.sb("raw_dn", [P, 2, HC, D])
        gu_hi, gu_lo = st.sb("gu_hi", [P, 2, KC, GU], F32R), st.sb("gu_lo", [P, 2, KC, GU], F32R)
        dn_hi, dn_lo = st.sb("dn_hi", [P, 2, HC, D], F32R), st.sb("dn_lo", [P, 2, HC, D], F32R)
        xg = st.sb("xg", [P, 2, D])
        xt_hi, xt_lo = st.sb("xt_hi", [P, 2, KC, P], F32R), st.sb("xt_lo", [P, 2, KC, P], F32R)
        sig = st.sb("sig", [P, HID])
        h = st.sb("h", [P, HID])
        ht_hi, ht_lo = st.sb("ht_hi", [P, HC, P], F32R), st.sb("ht_lo", [P, HC, P], F32R)
        out = st.sb("out", [P, 2, D])
        get_rows, put_rows = st.sb("get_rows", [P, 2], I32), st.sb("put_rows", [P, 2], I32)
        gate = st.sb("gate_tile", [P, 1])
        gate_clear = st.sem("gate_clear")
        tp = st.ps("tp", [P, KC, P])
        gu = st.ps("gu", [P, GU])
        ht = st.ps("ht", [P, HC, P])
        y = st.ps("y", [P, D])
        gu_loaded, dn_loaded = st.sem("gu_loaded"), st.sem("dn_loaded")
        gu_hi_cut, gu_cut, dn_hi_cut, dn_cut = (st.sem(n) for n in ("gu_hi_cut", "gu_cut", "dn_hi_cut", "dn_cut"))
        get_copied, put_copied = st.sem("get_copied"), st.sem("put_copied")
        gathered = [st.sem("gathered0"), st.sem("gathered1")]
        tp_ready, x_hi_ready, x_ready, gu_ready = (st.sem(n) for n in ("tp_ready", "x_hi_ready", "x_ready", "gu_ready"))
        sig_ready, silu_ready, h_ready = (st.sem(n) for n in ("sig_ready", "silu_ready", "h_ready"))
        ht_ready, ht_hi_ready, ht_cut = (st.sem(n) for n in ("ht_ready", "ht_hi_ready", "ht_cut"))
        y_ready, out_ready, out_used, added = (st.sem(n) for n in ("y_ready", "out_ready", "out_used", "added"))
        rows = routing.rows[:, :, :].rearrange("p a q -> p (a q)")
        gates = routing.gates[:, :, :].rearrange("p a q -> p (a q)")

        def expert_of(eng, b):
            return eng.value_load(routing.table[0:1, 0, ds(b, 1)], min_val=0, max_val=E - 1)

        def first_of(eng, b):
            return eng.value_load(routing.table[0:1, 1, ds(b, 1)], min_val=0, max_val=1)

        def blocks(eng, body):
            more = eng.value_load(routing.total[0:1, 0:1], min_val=0, max_val=NBLK - E)
            for b in range(UNROLL):
                body(b, b % 2, b // 2)
            with eng.Fori(1, NBLK // UNROLL) as i:
                with eng.If(UNROLL * i < more + E):
                    for q in range(UNROLL):
                        body(UNROLL * i + q, q % 2, UNROLL // 2 * i + q // 2)
                eng.nop()
            return (more + UNROLL - 1) // UNROLL * UNROLL + E

        with nc.Block() as block:
            @block.sync
            def _(sp):
                lead(sp, gu_loaded, by=32)
                lead(sp, dn_loaded, by=16)
                with sp.Fori(0, E // 2) as i:
                    for u in range(2):
                        e = 2 * i + u
                        sp.wait_ge(gu_cut, done(e - 2, 2))
                        sp.wait_ge(gu_loaded, done(e - 1, 32))
                        for n, dram in enumerate((exp_gate, exp_up)):
                            sp.dma_start(raw_gu[:, u, n, :, :],
                                         dram[ds(e, 1), :, :].rearrange("a (p k) n -> p (a k) n", k=KC))\
                                .then_inc(gu_loaded, 16)
                        sp.wait_ge(dn_loaded, done(e - 1, 16))
                        sp.wait_ge(dn_cut, done(e - 2))
                        sp.dma_start(raw_dn[:, u, :, :],
                                     exp_down[ds(e, 1), :, :].rearrange("a (p c) n -> p (a c) n", c=HC))\
                            .then_inc(dn_loaded, 16)

            def slot(s):
                return ds(s, 1) if type(s) is not int else slice(s, s + 1)

            def by_chunk(tile, s, part):
                half = tile[:, slot(s), part * KC // 2:(part + 1) * KC // 2, :]
                return half.rearrange("p a k (m n) -> p (a m) k n", m=2)

            def raw_chunk(s, part):
                return raw_gu[:, slot(s), :, part * KC // 2:(part + 1) * KC // 2, :].rearrange("p a m k n -> p (a m) k n")

            def cut(e, part):
                return done(e, 2) - (1 - part)

            @block.tensor
            def _(pe):
                lead(pe, tp_ready, gu_ready, ht_ready, y_ready)

                def transposes(b, u, n):
                    pe.wait_ge(gathered[u], 16 * n)
                    pe.wait_ge(x_ready, done(b - 1))
                    for k in range(KC):
                        last = pe.transpose(tp[:, k, :], xg[:, u, k::KC], ident[:, :])
                    last.then_inc(tp_ready, 1)

                def up(b, u):
                    e = expert_of(pe, b)
                    pe.wait_ge(gu_cut, cut(e, 0))
                    pe.wait_ge(x_ready, done(b))
                    pe.wait_ge(h_ready, done(b - 1))
                    s = e % 2
                    w_hi = [gu_hi[:, slot(s), k, :] for k in range(KC)]
                    w_lo = [gu_lo[:, slot(s), k, :] for k in range(KC)]
                    for k in range(KC):
                        if k == KC // 2:
                            pe.wait_ge(gu_cut, cut(e, 1))
                        last = product(pe, gu[:, :], xt_hi[:, u, k, :], xt_lo[:, u, k, :], w_hi[k], w_lo[k],
                                       k == 0, k == KC - 1)
                    last.then_inc(gu_ready, 1)

                def turn(b):
                    pe.wait_ge(h_ready, done(b))
                    pe.wait_ge(ht_cut, done(b - 1))
                    for c in range(HC):
                        last = pe.transpose(ht[:, c, :], h[:, c::HC], ident[:, :])
                    last.then_inc(ht_ready, 1)

                def down(b):
                    e = expert_of(pe, b)
                    pe.wait_ge(dn_cut, done(e))
                    pe.wait_ge(ht_cut, done(b))
                    pe.wait_ge(out_ready, done(b - 1))
                    s = e % 2
                    for c in range(HC):
                        for n in range(2):
                            cols = slice(n * 512, (n + 1) * 512)
                            last = product(pe, y[:, cols], ht_hi[:, c, :], ht_lo[:, c, :], dn_hi[:, slot(s), c, cols],
                                           dn_lo[:, slot(s), c, cols], c == 0, c == HC - 1)
                    last.then_inc(y_ready, 1)

                def body(b, u, i):
                    up(b, u)
                    transposes(b + 1, 1 - u, i + 1 + u)
                    if type(b) is not int or b:
                        down(b - 1)
                    turn(b)

                transposes(0, 0, 1)
                count = blocks(pe, body)
                down(count - 1)

            @block.scalar
            def _(act):
                lead(act, gu_hi_cut, by=2)
                lead(act, dn_hi_cut, x_hi_ready, sig_ready, ht_hi_ready, out_ready)

                def cut_gu(e, s, b, part):
                    act.wait_ge(gu_loaded, done(e, 32))
                    act.wait_ge(gu_ready, done(b - 1))
                    act.activation(by_chunk(gu_hi, s, part), raw_chunk(s, part), ACT.Copy).then_inc(gu_hi_cut, 1)

                def cut_dn(e, s, b):
                    act.wait_ge(dn_loaded, done(e, 16))
                    act.wait_ge(y_ready, done(b - 1))
                    act.activation(dn_hi[:, slot(s), :, :], raw_dn[:, slot(s), :, :], ACT.Copy).then_inc(dn_hi_cut, 1)

                def cut_x(b, u):
                    act.wait_ge(tp_ready, done(b))
                    act.wait_ge(gu_ready, done(b - 2))
                    act.activation(xt_hi[:, u, :, :], tp[:, :, :], ACT.Copy).then_inc(x_hi_ready, 1)

                def cut_ht(b):
                    act.wait_ge(ht_ready, done(b))
                    act.wait_ge(y_ready, done(b - 1))
                    act.activation(ht_hi[:, :, :], ht[:, :, :], ACT.Copy).then_inc(ht_hi_ready, 1)

                def output(b, u):
                    act.wait_ge(y_ready, done(b))
                    act.wait_ge(out_used, done(b - 2))
                    act.activation(out[:, u, :], y[:, :], ACT.Copy, scale=gates[:, ds(b, 1)]).then_inc(out_ready, 1)

                def body(b, u, i):
                    started = type(b) is not int or b
                    if started:
                        cut_ht(b - 1)
                    if type(b) is not int or b > 1:
                        output(b - 2, u)
                    if started:
                        e, first = expert_of(act, b - 1), first_of(act, b - 1)
                        with act.If(first > 0):
                            cut_dn(e + 1, (e + 1) % 2, b - 1)
                    e, first = expert_of(act, b), first_of(act, b)
                    with act.If(first > 0):
                        cut_gu(e + 1, (e + 1) % 2, b, 0)
                    act.wait_ge(gu_ready, done(b))
                    act.wait_ge(h_ready, done(b - 1))
                    act.activation(sig[:, :], gu[:, 0:HID], ACT.Sigmoid).then_inc(sig_ready, 1)
                    cut_x(b + 1, 1 - u)
                    with act.If(first > 0):
                        cut_gu(e + 1, (e + 1) % 2, b, 1)
                    act.nop()

                cut_x(0, 0)
                cut_gu(0, 0, 0, 0)
                cut_gu(0, 0, 0, 1)
                cut_dn(0, 0, 0)
                count = blocks(act, body)
                cut_ht(count - 1)
                output(count - 2, 0)
                output(count - 1, 1)

            @block.vector
            def _(dve):
                lead(dve, gu_cut, by=2)
                lead(dve, dn_cut, x_ready, silu_ready, h_ready, ht_cut)

                def cut_gu(e, s, part):
                    dve.wait_ge(gu_hi_cut, cut(e, part))
                    dve.tensor_tensor(by_chunk(gu_lo, s, part), raw_chunk(s, part), f32(by_chunk(gu_hi, s, part)),
                                      ALU.subtract).then_inc(gu_cut, 1)

                def cut_dn(e, s):
                    dve.wait_ge(dn_hi_cut, done(e))
                    dve.tensor_tensor(dn_lo[:, slot(s), :, :], raw_dn[:, slot(s), :, :], f32(dn_hi[:, slot(s), :, :]),
                                      ALU.subtract).then_inc(dn_cut, 1)

                def cut_x(b, u):
                    dve.wait_ge(x_hi_ready, done(b))
                    dve.tensor_tensor(xt_lo[:, u, :, :], tp[:, :, :], f32(xt_hi[:, u, :, :]), ALU.subtract)\
                        .then_inc(x_ready, 1)

                def cut_ht(b):
                    dve.wait_ge(ht_hi_ready, done(b))
                    dve.tensor_tensor(ht_lo[:, :, :], ht[:, :, :], f32(ht_hi[:, :, :]), ALU.subtract).then_inc(ht_cut, 1)

                def body(b, u, i):
                    if type(b) is not int or b:
                        cut_ht(b - 1)
                        e, first = expert_of(dve, b - 1), first_of(dve, b - 1)
                        with dve.If(first > 0):
                            cut_dn(e + 1, (e + 1) % 2)
                    e, first = expert_of(dve, b), first_of(dve, b)
                    with dve.If(first > 0):
                        cut_gu(e + 1, (e + 1) % 2, 0)
                    dve.wait_ge(sig_ready, done(b))
                    dve.tensor_tensor(sig[:, :], sig[:, :], gu[:, 0:HID], ALU.mult).then_inc(silu_ready, 1)
                    dve.wait_ge(silu_ready, done(b))
                    dve.wait_ge(ht_ready, done(b - 1))
                    dve.tensor_tensor(h[:, :], sig[:, :], gu[:, HID:], ALU.mult).then_inc(h_ready, 1)
                    cut_x(b + 1, 1 - u)
                    with dve.If(first > 0):
                        cut_gu(e + 1, (e + 1) % 2, 1)
                    dve.nop()

                cut_x(0, 0)
                cut_gu(0, 0, 0)
                cut_gu(0, 0, 1)
                cut_dn(0, 0)
                count = blocks(dve, body)
                cut_ht(count - 1)

            @block.gpsimd
            def _(pool):
                lead(pool, out_used, get_copied, put_copied)

                def gather(b, u):
                    pool.wait_ge(tp_ready, done(b - 2))
                    pool.tensor_copy(get_rows[:, u:u + 1], rows[:, ds(b, 1)]).then_inc(get_copied, 1)
                    pool.wait_ge(get_copied, done(b))
                    pool.tensor_tensor(gate[:, :], gate[:, :], gate[:, :], ALU.mult)
                    pool.indirect_dma_start(xg[:, u, :], None, x_dram,
                                            bass.IndirectOffsetOnAxis(ap=get_rows[:, u:u + 1], axis=0))\
                        .then_inc(gathered[u], 16)

                def add(b, u):
                    pool.tensor_copy(put_rows[:, u:u + 1], rows[:, ds(b, 1)]).then_inc(put_copied, 1)
                    pool.wait_ge(put_copied, done(b))
                    pool.wait_ge(out_ready, done(b))
                    pool.tensor_tensor(gate[:, :], gate[:, :], gate[:, :], ALU.mult)
                    pool.indirect_dma_start(acc_dram, bass.IndirectOffsetOnAxis(ap=put_rows[:, u:u + 1], axis=0),
                                            out[:, u, :], None, compute_op=ALU.add).then_inc(added, 16)
                    pool.wait_ge(added, 16 * (b + 1))
                    pool.sem_inc(out_used, 1)

                def body(b, u, i):
                    gather(b + 2, u)
                    if type(b) is not int or b > 1:
                        add(b - 2, u)

                pool.memset(gate[:, :], 0.0).then_inc(gate_clear, 1)
                pool.wait_ge(gate_clear, 1)
                gather(0, 0)
                gather(1, 1)
                count = blocks(pool, body)
                add(count - 2, 0)
                add(count - 1, 1)
                for u in range(2):
                    pool.wait_ge(gathered[u], (count // 2 + 1) * 16)


def stage_final_norm(nc, acc_dram, ln_g, ln_b, out_dram):
    depth = 8
    with Stage(nc, "fin") as st:
        norm = Norm(st, ln_g, ln_b, depth)
        y_loaded = [st.sem(f"y_loaded{u}") for u in range(depth)]
        link = st.sem("link")
        with nc.Block() as block:
            @block.sync
            def _(sp):
                for t in range(NT + depth):
                    u = t % depth
                    if t >= depth:
                        sp.wait_ge(norm.shifted, done(t - depth))
                        sp.dma_start(out_dram[(t - depth) * P:(t - depth + 1) * P, :], norm.out[:, u, :])\
                            .then_inc(norm.stored[u], 16)
                    if t < NT:
                        sp.dma_start(norm.y[:, u, :], acc_dram[t * P:(t + 1) * P, :]).then_inc(y_loaded[u], 16)
                    if t == 0:
                        norm.load(sp)
                norm.all_stored(sp)

            @block.vector
            def _(dve):
                norm.leads(dve=dve)
                s = Steps(dve, link)
                for t in range(NT + 2):
                    if t < NT:
                        dve.wait_ge(y_loaded[t % depth], 16 * (t // depth + 1))
                        norm.vector_stats(dve, s, t % depth)
                    if 1 <= t <= NT:
                        norm.vector_map(dve, s, t - 1, (t - 1) % depth)
                    if t == 2:
                        dve.wait_ge(norm.loaded, 32)
                    if t >= 2:
                        norm.vector_gain(dve, t - 2, (t - 2) % depth)

            @block.scalar
            def _(act):
                norm.leads(act=act)
                for t in range(NT + 1):
                    if t < NT:
                        norm.scalar_root(act, t, t % depth)
                    if t:
                        norm.scalar_norm(act, t - 1, (t - 1) % depth)

            @block.gpsimd
            def _(pool):
                norm.leads(pool=pool)
                for t in range(NT):
                    pool.wait_ge(norm.gained, done(t))
                    if t >= depth:
                        pool.wait_ge(norm.stored[t % depth], 16 * (t // depth))
                    pool.tensor_tensor(norm.out[:, t % depth, :], norm.y[:, t % depth, :], norm.shift[:, :], ALU.add)\
                        .then_inc(norm.shifted, 1)


def block_kernel(nc, x, mem, w_in, pool_w, pool_scale, w_out, ln1_g, ln1_b, w_cq, w_ck, w_cv, w_co, ln2_g, ln2_b,
                 w_router, router_bias, exp_gate, exp_up, exp_down, sh_gate, sh_up, sh_down, ln3_g, ln3_b, out):
    def dram(name, *shape):
        return nc.dram_tensor(name, shape, F32).ap()

    v, qt, kt = dram("v", T, AW), dram("qt", PAIRS, P, T), dram("kt", PAIRS, P, T)
    mix_hi, mix_lo = dram("mix_hi", PW // P, P, T), dram("mix_lo", PW // P, P, T)
    o = [dram(f"o{b}", T, AW) for b in range(len(PATTERNS))]
    stats = [dram(f"stats{b}", T, 2 * HEADS) for b in range(len(PATTERNS))]
    x1, x2, acc = dram("x1", T, D), dram("x2", ROWS, D), dram("acc", ROWS, D)
    slots = dram("slots", TAB * P, 2)
    with Stage(nc, "all") as st:
        ident = st.sb("ident", [P, P])
        make_identity(nc, ident)
        with Stage(nc, "front") as front:
            xt_hi, xt_lo = front.sb("xt_hi", [P, KC, T], F32R), front.sb("xt_lo", [P, KC, T], F32R)
            stage_transpose_and_v(nc, ident, xt_hi, xt_lo, x, w_in, v)
            stage_project_qk(nc, xt_hi, xt_lo, w_in, qt, kt)
            stage_pool(nc, xt_hi, xt_lo, w_in, pool_w, pool_scale, mix_hi, mix_lo)
        attention(nc, ident, v, qt, kt, o, stats)
        stage_mix(nc, ident, x1, x, o, stats, mix_hi, mix_lo, w_out, ln1_g, ln1_b)
        with Stage(nc, "memory") as memory:
            k_mem = memory.sb("k_mem", [P, MH, MEM])
            v_mem = memory.sb("v_mem", [P, MEM // P, MW])
            stage_memory(nc, ident, mem, w_ck, w_cv, k_mem, v_mem)
            stage_cross(nc, ident, x1, k_mem, v_mem, w_cq, w_co, ln2_g, ln2_b, x2)
        with Stage(nc, "moe") as moe:
            routing = Routing(moe)
            with Stage(nc, "scores") as st_scores:
                scores = st_scores.sb("scores", [P, NT, E])
                stage_route(nc, ident, x2, w_router, scores)
                stage_shared_and_dispatch(nc, ident, x2, acc, slots, sh_gate, sh_up, sh_down, router_bias, scores,
                                          routing)
            stage_experts(nc, ident, x2, acc, exp_gate, exp_up, exp_down, routing)
        stage_final_norm(nc, acc, ln3_g, ln3_b, out)


def kernel(**inputs):
    import concourse.bacc as bacc
    from concourse.bass_utils import run_bass_kernel_spmd

    nc = bacc.Bacc("TRN2", target_bir_lowering=False, num_devices=1)
    arrays, args = {}, {}
    for name, value in inputs.items():
        a = np.asarray(value)[0]
        if name == "pool_scale":
            a = a.reshape(len(POOL_WINDOWS), P).T
        a = np.ascontiguousarray(a)
        arrays[f"in_{name}"] = a
        args[name] = nc.dram_tensor(f"in_{name}", a.shape, mybir.dt.from_np(a.dtype), kind="ExternalInput").ap()
    args["out"] = nc.dram_tensor("out", (T, D), F32, kind="ExternalOutput").ap()
    block_kernel(nc, **args)
    result = run_bass_kernel_spmd(nc, [arrays], core_ids=[0])
    return np.asarray(result.results[0]["out"]).reshape(1, T, D)
```
